# Optimizing a Trainium2 kernel written in Bass

```python
import math
import jax, jax.numpy as jnp
from jax import lax
import numpy as np
import jax
import jax.numpy as jnp

D_MODEL = 1024
BATCH = 1
SEQ = 256
DEPTH = 2

HEAD_DIM = 64
D_MIX = D_MODEL
RWKV_HEADS = (3 * D_MIX) // (8 * HEAD_DIM)
D_RWKV = RWKV_HEADS * HEAD_DIM
ATTN_HEADS = (3 * D_MIX) // (8 * HEAD_DIM)
D_ATTN = ATTN_HEADS * HEAD_DIM
D_CONV = D_MIX - D_RWKV - D_ATTN
DECAY_LORA = 32
ICLR_LORA = 32
GATE_LORA = 64
CONV_WIDTH = 31
DILATED_PATTERNS = ((128, 1), (512, 4), (2048, 16))
ATTN_BLOCK = 128
D_FF = 2816
NORM_EPS = 1e-6
RWKV_GN_EPS = 64e-5
CONV_LN_EPS = 1e-5
D_SHIFT = 3 * D_RWKV + DECAY_LORA + ICLR_LORA + GATE_LORA
D_IN = D_SHIFT + 3 * D_ATTN + 2 * D_CONV


def _alibi_slopes(n):
    def pow2(m):
        start = 2.0 ** (-8.0 / m)
        return [start ** (i + 1) for i in range(m)]
    if math.log2(n).is_integer():
        return pow2(n)
    c = 2 ** int(math.floor(math.log2(n)))
    return pow2(c) + pow2(2 * c)[0::2][: n - c]

def _rms_norm(x, g):
    xf = x.astype(jnp.float32)
    y = xf * lax.rsqrt(jnp.mean(xf * xf, axis=-1, keepdims=True) + NORM_EPS)
    return y.astype(x.dtype) * g

def _head_rms(t, g):
    return t * lax.rsqrt(jnp.mean(t * t, axis=-1, keepdims=True) + NORM_EPS) * g.astype(jnp.float32)

def _swiglu(x, w_gate, w_up, w_down):
    return (jax.nn.silu(x @ w_gate) * (x @ w_up)) @ w_down

def _token_shift(p, mu):
    prev = jnp.pad(p, ((0, 0), (1, 0), (0, 0)))[:, :-1]
    return p + (prev - p) * mu.astype(p.dtype)

def _rwkv7_scan(r, w, k, v, kk, a):
    B, S, H, N = r.shape
    xs = tuple(jnp.moveaxis(t, 1, 0) for t in (r, w, k, v, -kk, kk * a))

    def step(state, inp):
        r_t, w_t, k_t, v_t, a_t, b_t = inp
        sa = jnp.einsum('bhij,bhj->bhi', state, a_t)
        state = (state * w_t[:, :, None, :]
                 + sa[..., None] * b_t[:, :, None, :]
                 + v_t[..., None] * k_t[:, :, None, :])
        y_t = jnp.einsum('bhij,bhj->bhi', state, r_t)
        return state, y_t

    state0 = jnp.zeros((B, H, N, N), jnp.float32)
    _, y = lax.scan(step, state0, xs)
    return jnp.moveaxis(y, 0, 1)

def _rwkv7_mixer(p, w0, w2, a0, a2, g2, k_k, k_a, r_k, ln_w, ln_b):
    B, S, _ = p.shape
    o = 0
    r = p[..., o:o + D_RWKV]; o += D_RWKV
    k = p[..., o:o + D_RWKV]; o += D_RWKV
    v = p[..., o:o + D_RWKV]; o += D_RWKV
    xw = p[..., o:o + DECAY_LORA]; o += DECAY_LORA
    xa = p[..., o:o + ICLR_LORA]; o += ICLR_LORA
    xg = p[..., o:o + GATE_LORA]
    f32 = jnp.float32
    w_log = -jax.nn.softplus(-(w0.astype(f32) + jnp.tanh(xw) @ w2.astype(f32))) - 0.5
    decay = jnp.exp(-jnp.exp(w_log))
    a = jax.nn.sigmoid(a0.astype(f32) + xa @ a2.astype(f32))
    g = jax.nn.sigmoid(xg) @ g2.astype(f32)
    heads = lambda t: t.reshape(B, S, RWKV_HEADS, HEAD_DIM)
    kk = heads(k * k_k.astype(f32))
    kk = kk * lax.rsqrt(jnp.sum(kk * kk, axis=-1, keepdims=True) + 1e-12)
    k = k * (1.0 + (a - 1.0) * k_a.astype(f32))
    rh, kh, vh = heads(r), heads(k), heads(v)
    y = _rwkv7_scan(rh, heads(decay), kh, vh, kk, heads(a))
    mu = jnp.mean(y, axis=-1, keepdims=True)
    var = jnp.mean(jnp.square(y - mu), axis=-1, keepdims=True)
    y = ((y - mu) * lax.rsqrt(var + RWKV_GN_EPS)).reshape(B, S, D_RWKV)
    y = y * ln_w.astype(f32) + ln_b.astype(f32)
    bonus = jnp.sum(rh * kh * r_k.astype(f32), axis=-1, keepdims=True) * vh
    return (y + bonus.reshape(B, S, D_RWKV)) * g

def _dilated_attention(q, k, v, slopes, window, dilation):
    B, S, H, N = q.shape
    n_keys = window // dilation
    L = S // dilation
    nb = -(-L // ATTN_BLOCK)
    Lp = nb * ATTN_BLOCK

    def blocks(t):
        t = t.reshape(B, L, dilation, H, N)
        t = jnp.pad(t, ((0, 0), (0, Lp - L), (0, 0), (0, 0), (0, 0)))
        return t.reshape(B, nb, ATTN_BLOCK, dilation, H, N)

    def band(t):
        prev = jnp.pad(t, ((0, 0), (1, 0), (0, 0), (0, 0), (0, 0), (0, 0)))[:, :-1]
        return jnp.concatenate([prev, t], axis=2)

    qb = blocks(q)
    kb = band(blocks(k))
    vb = band(blocks(v))
    s = jnp.einsum('bnqchd,bnkchd->bnqchk', qb, kb)
    qi = jnp.arange(ATTN_BLOCK)
    ki = jnp.arange(2 * ATTN_BLOCK)
    dist = qi[:, None] + ATTN_BLOCK - ki[None, :]
    key_idx = jnp.arange(nb)[:, None] * ATTN_BLOCK + ki[None, :] - ATTN_BLOCK
    valid = ((dist >= 0) & (dist <= n_keys))[None] & (key_idx >= 0)[:, None, :]
    bias = -slopes[:, None] * (dist * dilation).astype(jnp.float32)[:, None, None, :]
    s = jnp.where(valid[None, :, :, None, None, :], s + bias, -jnp.inf)
    lse = jax.nn.logsumexp(s, axis=-1)
    p = jnp.exp(s - lse[..., None])
    o = jnp.einsum('bnqchk,bnkchd->bnqchd', p, vb)
    o = o.reshape(B, Lp, dilation, H, N)[:, :L].reshape(B, S, H, N)
    lse = lse.reshape(B, Lp, dilation, H)[:, :L].reshape(B, S, H)
    return o, lse

def _attention_mixer(qkv, q_norm, k_norm):
    B, S, _ = qkv.shape
    q = qkv[..., :D_ATTN].reshape(B, S, ATTN_HEADS, HEAD_DIM)
    k = qkv[..., D_ATTN:2 * D_ATTN].reshape(B, S, ATTN_HEADS, HEAD_DIM)
    v = qkv[..., 2 * D_ATTN:].reshape(B, S, ATTN_HEADS, HEAD_DIM)
    q = _head_rms(q, q_norm) * (HEAD_DIM ** -0.5)
    k = _head_rms(k, k_norm)
    slopes = jnp.asarray(_alibi_slopes(ATTN_HEADS), jnp.float32)
    res = [_dilated_attention(q, k, v, slopes, w, d) for (w, d) in DILATED_PATTERNS]
    outs = jnp.stack([r_[0] for r_ in res], axis=0)
    lses = jnp.stack([r_[1] for r_ in res], axis=0)
    alpha = jax.nn.softmax(lses, axis=0)
    out = jnp.sum(alpha[..., None] * outs, axis=0)
    return out.reshape(B, S, D_ATTN)

def _conv_mixer(u, dw_w, dw_b, ln_w, ln_b):
    f32 = jnp.float32
    z = u[..., :D_CONV] * jax.nn.sigmoid(u[..., D_CONV:])
    z = lax.conv_general_dilated(z, dw_w.astype(f32)[:, None, :], window_strides=(1,),
                                 padding=[(CONV_WIDTH - 1, 0)],
                                 dimension_numbers=('NWC', 'WIO', 'NWC'),
                                 feature_group_count=D_CONV) + dw_b.astype(f32)
    mu = jnp.mean(z, axis=-1, keepdims=True)
    var = jnp.mean(jnp.square(z - mu), axis=-1, keepdims=True)
    z = (z - mu) * lax.rsqrt(var + CONV_LN_EPS) * ln_w.astype(f32) + ln_b.astype(f32)
    return jax.nn.silu(z)

def first_inputs(seed: int = 0) -> dict:
    key = jax.random.key(seed)
    ks = iter(jax.random.split(key, 40))
    f32 = jnp.float32
    L = DEPTH

    def normal(shape, scale):
        return jax.random.normal(next(ks), shape, f32) * scale

    def gain(shape):
        return 1.0 + 0.05 * jax.random.normal(next(ks), shape, f32)

    def unif(shape, lo, hi):
        return jax.random.uniform(next(ks), shape, f32, lo, hi)

    return {
        'x': normal((BATCH, SEQ, D_MODEL), 1.0),
        'norm_ffn1': gain((L, D_MODEL)),
        'ffn1_w_gate': normal((L, D_MODEL, D_FF), D_MODEL ** -0.5),
        'ffn1_w_up': normal((L, D_MODEL, D_FF), D_MODEL ** -0.5),
        'ffn1_w_down': normal((L, D_FF, D_MODEL), D_FF ** -0.5),
        'norm_mix': gain((L, D_MODEL)),
        'w_in': normal((L, D_MODEL, D_IN), D_MODEL ** -0.5),
        'shift_mu': unif((L, D_SHIFT), 0.0, 1.0),
        'rwkv_w0': unif((L, D_RWKV), -6.0, 1.0),
        'rwkv_w2': normal((L, DECAY_LORA, D_RWKV), 0.1),
        'rwkv_a0': normal((L, D_RWKV), 0.5),
        'rwkv_a2': normal((L, ICLR_LORA, D_RWKV), 0.1),
        'rwkv_g2': normal((L, GATE_LORA, D_RWKV), GATE_LORA ** -0.5),
        'rwkv_k_k': 0.85 + normal((L, D_RWKV), 0.05),
        'rwkv_k_a': gain((L, D_RWKV)),
        'rwkv_r_k': 0.5 + normal((L, RWKV_HEADS, HEAD_DIM), 0.1),
        'rwkv_ln_w': gain((L, D_RWKV)),
        'rwkv_ln_b': normal((L, D_RWKV), 0.02),
        'attn_q_norm': gain((L, HEAD_DIM)),
        'attn_k_norm': gain((L, HEAD_DIM)),
        'conv_dw_w': normal((L, CONV_WIDTH, D_CONV), CONV_WIDTH ** -0.5),
        'conv_dw_b': normal((L, D_CONV), 0.02),
        'conv_ln_w': gain((L, D_CONV)),
        'conv_ln_b': normal((L, D_CONV), 0.02),
        'w_out': normal((L, D_MIX, D_MODEL), D_MIX ** -0.5),
        'norm_ffn2': gain((L, D_MODEL)),
        'ffn2_w_gate': normal((L, D_MODEL, D_FF), D_MODEL ** -0.5),
        'ffn2_w_up': normal((L, D_MODEL, D_FF), D_MODEL ** -0.5),
        'ffn2_w_down': normal((L, D_FF, D_MODEL), D_FF ** -0.5),
    }

def first_block(x, norm_ffn1, ffn1_w_gate, ffn1_w_up, ffn1_w_down, norm_mix, w_in, shift_mu,
              rwkv_w0, rwkv_w2, rwkv_a0, rwkv_a2, rwkv_g2, rwkv_k_k, rwkv_k_a, rwkv_r_k,
              rwkv_ln_w, rwkv_ln_b, attn_q_norm, attn_k_norm, conv_dw_w, conv_dw_b,
              conv_ln_w, conv_ln_b, w_out, norm_ffn2, ffn2_w_gate, ffn2_w_up, ffn2_w_down):
    for l in range(DEPTH):
        x = x + 0.5 * _swiglu(_rms_norm(x, norm_ffn1[l]), ffn1_w_gate[l], ffn1_w_up[l], ffn1_w_down[l])
        h = _rms_norm(x, norm_mix[l])
        proj = (h @ w_in[l]).astype(jnp.float32)
        p_rwkv = _token_shift(proj[..., :D_SHIFT], shift_mu[l])
        y_rwkv = _rwkv7_mixer(p_rwkv, rwkv_w0[l], rwkv_w2[l], rwkv_a0[l], rwkv_a2[l], rwkv_g2[l],
                              rwkv_k_k[l], rwkv_k_a[l], rwkv_r_k[l], rwkv_ln_w[l], rwkv_ln_b[l])
        y_attn = _attention_mixer(proj[..., D_SHIFT:D_SHIFT + 3 * D_ATTN], attn_q_norm[l], attn_k_norm[l])
        y_conv = _conv_mixer(proj[..., D_SHIFT + 3 * D_ATTN:], conv_dw_w[l], conv_dw_b[l],
                             conv_ln_w[l], conv_ln_b[l])
        mix = jnp.concatenate([y_rwkv, y_attn, y_conv], axis=-1).astype(x.dtype)
        x = x + mix @ w_out[l]
        x = x + 0.5 * _swiglu(_rms_norm(x, norm_ffn2[l]), ffn2_w_gate[l], ffn2_w_up[l], ffn2_w_down[l])
    return x


DEPTH_2 = 1

GRID_W = 64
CTX_LEN = 256
ROPE_BASE = 10000.0
EPS = 1e-6
BLK = 128
A_HEADS = 8
A_KV_HEADS = 2
WINDOW = 128
SSM_HEADS = 16
SSM_HEADDIM = 64
SSM_INNER = SSM_HEADS * SSM_HEADDIM
SSM_GROUPS = 2
SSM_STATE = 128
SSM_CONV = 3
SSM_CHUNK = 128
SSM_BC = SSM_GROUPS * SSM_STATE
SSM_XBC = SSM_INNER + 2 * SSM_BC
C_HEADS = 8
C_KV_HEADS = 2
FFN_CONV = 3
A_Q_W = A_HEADS * HEAD_DIM
A_KV_W = A_KV_HEADS * HEAD_DIM
C_Q_W = C_HEADS * HEAD_DIM
C_KV_W = C_KV_HEADS * HEAD_DIM
IN_WIDTH = (A_Q_W + 2 * A_KV_W) + (SSM_INNER + SSM_XBC + 2 * SSM_HEADS) + (C_Q_W + 2 * C_KV_W) + 3 * D_MODEL


def _in_spans():
    sizes = (('a_q', A_Q_W), ('a_k', A_KV_W), ('a_v', A_KV_W),
             ('b_z', SSM_INNER), ('b_xbc', SSM_XBC), ('b_dt', 2 * SSM_HEADS),
             ('c_q', C_Q_W), ('c_k', C_KV_W), ('c_v', C_KV_W),
             ('gates', 3 * D_MODEL))
    spans, start = {}, 0
    for name, n in sizes:
        spans[name] = (start, start + n)
        start += n
    return spans

def rms_norm(x, g):
    xf = x.astype(jnp.float32)
    y = xf * lax.rsqrt(jnp.mean(xf * xf, axis=-1, keepdims=True) + EPS)
    return (y * g.astype(jnp.float32)).astype(x.dtype)

def modulate(h, shift, scale):
    return h * (1 + scale) + shift

def grid_rope(rows):
    t_row = jnp.repeat(jnp.arange(rows), GRID_W).astype(jnp.float32)
    t_col = jnp.tile(jnp.arange(GRID_W), rows).astype(jnp.float32)
    n = HEAD_DIM // 4
    inv = ROPE_BASE ** (-jnp.arange(n, dtype=jnp.float32) / n)
    ang = jnp.concatenate([t_row[:, None] * inv, t_col[:, None] * inv], axis=-1)
    return jnp.cos(ang), jnp.sin(ang)

def apply_rope(x, cos, sin):
    b, L, h, dh = x.shape
    xr = x.astype(jnp.float32).reshape(b, L, h, dh // 2, 2)
    c = cos[None, :, None, :]
    s = sin[None, :, None, :]
    x1, x2 = xr[..., 0], xr[..., 1]
    out = jnp.stack([x1 * c - x2 * s, x1 * s + x2 * c], axis=-1)
    return out.reshape(b, L, h, dh).astype(x.dtype)

def dwconv(u, w, bias):
    k = w.shape[0]
    pad = k // 2
    y = lax.conv_general_dilated(u, w[:, None, :].astype(u.dtype), window_strides=(1,),
                                 padding=[(pad, pad)], dimension_numbers=('NWC', 'WIO', 'NWC'),
                                 feature_group_count=u.shape[-1])
    return y + bias.astype(u.dtype)

def dense_attention(q, k, v, sink):
    b, lq, hq, dh = q.shape
    hkv = k.shape[2]
    g = hq // hkv
    qg = q.reshape(b, lq, hkv, g, dh)
    s = jnp.einsum('bqhgd,bkhd->bhgqk', qg, k).astype(jnp.float32) * (dh ** -0.5)
    if sink is not None:
        s_sink = jnp.broadcast_to(sink.astype(jnp.float32).reshape(1, hkv, g, 1, 1), s.shape[:-1] + (1,))
        s = jnp.concatenate([s, s_sink], axis=-1)
    p = jax.nn.softmax(s, axis=-1)
    if sink is not None:
        p = p[..., :-1]
    o = jnp.einsum('bhgqk,bkhd->bqhgd', p.astype(v.dtype), v)
    return o.reshape(b, lq, hq * dh)

def window_attention(q, k, v, kc, vc, sink):
    b, L, hq, dh = q.shape
    hkv = k.shape[2]
    g = hq // hkv
    nb = L // BLK
    lc = kc.shape[1]
    qb = q.reshape(b, nb, BLK, hkv, g, dh)
    pad = ((0, 0), (BLK, BLK), (0, 0), (0, 0))
    kp = jnp.pad(k, pad).reshape(b, nb + 2, BLK, hkv, dh)
    vp = jnp.pad(v, pad).reshape(b, nb + 2, BLK, hkv, dh)
    kw = jnp.concatenate([kp[:, :-2], kp[:, 1:-1], kp[:, 2:]], axis=2)
    vw = jnp.concatenate([vp[:, :-2], vp[:, 1:-1], vp[:, 2:]], axis=2)
    scale = dh ** -0.5
    s_loc = jnp.einsum('bnqhgd,bnjhd->bnhgqj', qb, kw).astype(jnp.float32) * scale
    s_ctx = jnp.einsum('bnqhgd,bchd->bnhgqc', qb, kc).astype(jnp.float32) * scale
    q_pos = (jnp.arange(nb) * BLK)[:, None] + jnp.arange(BLK)[None, :]
    k_pos = (jnp.arange(nb) * BLK - BLK)[:, None] + jnp.arange(3 * BLK)[None, :]
    rel = q_pos[:, :, None] - k_pos[:, None, :]
    valid = (jnp.abs(rel) <= WINDOW) & (k_pos[:, None, :] >= 0) & (k_pos[:, None, :] < L)
    s_loc = jnp.where(valid[None, :, None, None], s_loc, -jnp.inf)
    s_sink = jnp.broadcast_to(sink.astype(jnp.float32).reshape(1, 1, hkv, g, 1, 1), s_loc.shape[:-1] + (1,))
    p = jax.nn.softmax(jnp.concatenate([s_loc, s_ctx, s_sink], axis=-1), axis=-1)
    nloc = 3 * BLK
    p_loc = p[..., :nloc].astype(v.dtype)
    p_ctx = p[..., nloc:nloc + lc].astype(v.dtype)
    o = jnp.einsum('bnhgqj,bnjhd->bnqhgd', p_loc, vw) + jnp.einsum('bnhgqc,bchd->bnqhgd', p_ctx, vc)
    return o.reshape(b, L, hq * dh)

def grid_attention(q, k, v, kc, vc):
    b, L, hq, dh = q.shape
    nb = L // BLK
    k_all = jnp.concatenate([k, kc], axis=1)
    v_all = jnp.concatenate([v, vc], axis=1)
    qb = jnp.moveaxis(q.reshape(b, nb, BLK, hq, dh), 1, 0)
    ob = lax.map(lambda qi: dense_attention(qi, k_all, v_all, None), qb)
    return jnp.moveaxis(ob, 0, 1).reshape(b, L, hq * dh)

def ssm_inputs(xbc_raw, dt_raw, conv_w, conv_b, dt_bias):
    b, L, _ = xbc_raw.shape
    xbc = jax.nn.silu(dwconv(xbc_raw, conv_w, conv_b))
    xs = xbc[..., :SSM_INNER].reshape(b, L, SSM_HEADS, SSM_HEADDIM)
    bm = xbc[..., SSM_INNER:SSM_INNER + SSM_BC].reshape(b, L, SSM_GROUPS, SSM_STATE)
    cm = xbc[..., SSM_INNER + SSM_BC:].reshape(b, L, SSM_GROUPS, SSM_STATE)
    dt = jax.nn.softplus(dt_raw.astype(jnp.float32).reshape(b, L, 2, SSM_HEADS) + dt_bias.astype(jnp.float32))
    return xs, bm, cm, dt

def ssd_scan(xh, dt, a_coef, bm, cm, h0, want_y):
    b, L, H, P = xh.shape
    G, N = bm.shape[2], bm.shape[3]
    hg = H // G
    q = SSM_CHUNK
    nc = L // q
    f32 = jnp.float32
    xdt = (xh.astype(f32) * dt[..., None]).reshape(b, nc, q, G, hg, P)
    bc = bm.astype(f32).reshape(b, nc, q, G, N)
    cc = cm.astype(f32).reshape(b, nc, q, G, N)
    acs = jnp.cumsum((dt * a_coef.astype(f32)).reshape(b, nc, q, G, hg), axis=2)
    decay_end = jnp.exp(acs[:, :, -1:] - acs)
    states = jnp.einsum('bcjgn,bcjghp->bcghpn', bc, xdt * decay_end[..., None])
    chunk_decay = jnp.exp(acs[:, :, -1])

    def step(h, inp):
        st, dec = inp
        return h * dec[..., None, None] + st, h

    h_last, h_in = lax.scan(step, h0.reshape(b, G, hg, P, N),
                            (jnp.moveaxis(states, 1, 0), jnp.moveaxis(chunk_decay, 1, 0)))
    h_last = h_last.reshape(b, H, P, N)
    if not want_y:
        return None, h_last
    h_in = jnp.moveaxis(h_in, 0, 1)
    seg = acs[:, :, :, None] - acs[:, :, None, :]
    tri = jnp.tril(jnp.ones((q, q), dtype=bool))
    lmat = jnp.exp(jnp.where(tri[:, :, None, None], seg, -jnp.inf))
    cb = jnp.einsum('bcign,bcjgn->bcijg', cc, bc)
    y_diag = jnp.einsum('bcijgh,bcjghp->bcighp', cb[..., None] * lmat, xdt)
    y_off = jnp.einsum('bcign,bcghpn->bcighp', cc, h_in) * jnp.exp(acs)[..., None]
    y = (y_diag + y_off).reshape(b, L, H, P).astype(xh.dtype)
    return y, h_last

def ssm_output(yf, yb, xs, z, d_skip, norm_g):
    b, L = xs.shape[0], xs.shape[1]
    y = yf + yb + xs * d_skip[:, None].astype(xs.dtype)
    y = y.reshape(b, L, SSM_INNER)
    return rms_norm(y * jax.nn.silu(z), norm_g)

def merge_branches(ya, yb, yc, g_raw, w_oa, w_ob, w_oc, w_out):
    g = jax.nn.sigmoid(g_raw.astype(jnp.float32)).astype(ya.dtype)
    ga, gb, gc = jnp.split(g, 3, axis=-1)
    m = ga * (ya @ w_oa) + gb * (yb @ w_ob) + gc * (yc @ w_oc)
    return m @ w_out

def conv_ffn(h, w_up, w_gate, conv_w, conv_b, w_down):
    up = h @ w_up
    gt = dwconv(h @ w_gate, conv_w, conv_b)
    return (jax.nn.silu(gt) * up) @ w_down

def hybrid_layer(x, xc, c_mod, cc_mod, cos, sin, w_in, norm1, norm2, a_sink, ssm_conv_w, ssm_conv_b,
                 ssm_a_log, ssm_dt_bias, ssm_d, ssm_norm, c_q_norm, c_k_norm, w_oa, w_ob, w_oc, w_out,
                 ffn_w_up, ffn_w_gate, ffn_conv_w, ffn_conv_b, ffn_w_down, need_ctx_out):
    b, L, _ = x.shape
    lc = xc.shape[1]
    sp = _in_spans()
    shift1, scale1, gate1, shift2, scale2, gate2 = jnp.split(c_mod[:, None, :], 6, axis=-1)
    h = modulate(rms_norm(x, norm1), shift1, scale1)
    hc = modulate(rms_norm(xc, norm1), cc_mod[:D_MODEL], cc_mod[D_MODEL:2 * D_MODEL])
    u = h @ w_in

    def lat(name):
        return u[..., sp[name][0]:sp[name][1]]

    def ctxp(name):
        return hc @ w_in[:, sp[name][0]:sp[name][1]]

    qa = apply_rope(lat('a_q').reshape(b, L, A_HEADS, HEAD_DIM), cos, sin)
    ka = apply_rope(lat('a_k').reshape(b, L, A_KV_HEADS, HEAD_DIM), cos, sin)
    va = lat('a_v').reshape(b, L, A_KV_HEADS, HEAD_DIM)
    kac = ctxp('a_k').reshape(b, lc, A_KV_HEADS, HEAD_DIM)
    vac = ctxp('a_v').reshape(b, lc, A_KV_HEADS, HEAD_DIM)
    ya = window_attention(qa, ka, va, kac, vac, a_sink)

    qg = apply_rope(rms_norm(lat('c_q').reshape(b, L, C_HEADS, HEAD_DIM), c_q_norm), cos, sin)
    kg = apply_rope(rms_norm(lat('c_k').reshape(b, L, C_KV_HEADS, HEAD_DIM), c_k_norm), cos, sin)
    vg = lat('c_v').reshape(b, L, C_KV_HEADS, HEAD_DIM)
    kgc = rms_norm(ctxp('c_k').reshape(b, lc, C_KV_HEADS, HEAD_DIM), c_k_norm)
    vgc = ctxp('c_v').reshape(b, lc, C_KV_HEADS, HEAD_DIM)
    yg = grid_attention(qg, kg, vg, kgc, vgc)

    a_coef = -jnp.exp(ssm_a_log.astype(jnp.float32))
    xs_c, bm_c, cm_c, dt_c = ssm_inputs(ctxp('b_xbc'), ctxp('b_dt'), ssm_conv_w, ssm_conv_b, ssm_dt_bias)
    h0 = jnp.zeros((b, SSM_HEADS, SSM_HEADDIM, SSM_STATE), jnp.float32)
    yf_c, hf_c = ssd_scan(xs_c, dt_c[:, :, 0], a_coef[0], bm_c, cm_c, h0, need_ctx_out)
    yb_c, hb_c = ssd_scan(jnp.flip(xs_c, 1), jnp.flip(dt_c[:, :, 1], 1), a_coef[1],
                          jnp.flip(bm_c, 1), jnp.flip(cm_c, 1), h0, need_ctx_out)
    xs, bm, cm, dt = ssm_inputs(lat('b_xbc'), lat('b_dt'), ssm_conv_w, ssm_conv_b, ssm_dt_bias)
    yf, _ = ssd_scan(xs, dt[:, :, 0], a_coef[0], bm, cm, hf_c, True)
    yb, _ = ssd_scan(jnp.flip(xs, 1), jnp.flip(dt[:, :, 1], 1), a_coef[1],
                     jnp.flip(bm, 1), jnp.flip(cm, 1), hb_c, True)
    ys = ssm_output(yf, jnp.flip(yb, 1), xs, lat('b_z'), ssm_d, ssm_norm)

    x = x + gate1 * merge_branches(ya, ys, yg, lat('gates'), w_oa, w_ob, w_oc, w_out)
    h2 = modulate(rms_norm(x, norm2), shift2, scale2)
    x = x + gate2 * conv_ffn(h2, ffn_w_up, ffn_w_gate, ffn_conv_w, ffn_conv_b, ffn_w_down)
    if not need_ctx_out:
        return x, None

    cgate1 = cc_mod[2 * D_MODEL:3 * D_MODEL]
    cshift2 = cc_mod[3 * D_MODEL:4 * D_MODEL]
    cscale2 = cc_mod[4 * D_MODEL:5 * D_MODEL]
    cgate2 = cc_mod[5 * D_MODEL:]
    yac = dense_attention(ctxp('a_q').reshape(b, lc, A_HEADS, HEAD_DIM), kac, vac, a_sink)
    ygc = dense_attention(rms_norm(ctxp('c_q').reshape(b, lc, C_HEADS, HEAD_DIM), c_q_norm), kgc, vgc, None)
    ysc = ssm_output(yf_c, jnp.flip(yb_c, 1), xs_c, ctxp('b_z'), ssm_d, ssm_norm)
    xc = xc + cgate1 * merge_branches(yac, ysc, ygc, ctxp('gates'), w_oa, w_ob, w_oc, w_out)
    h2c = modulate(rms_norm(xc, norm2), cshift2, cscale2)
    xc = xc + cgate2 * conv_ffn(h2c, ffn_w_up, ffn_w_gate, ffn_conv_w, ffn_conv_b, ffn_w_down)
    return x, xc

def second_inputs(seed: int = 0) -> dict:
    key = jax.random.key(seed)
    ks = jax.random.split(key, 32)
    f32 = jnp.float32

    def nrm(k, shape, scale):
        return jax.random.normal(k, shape, f32) * scale

    d = D_MODEL
    dt0 = jnp.exp(jax.random.uniform(ks[11], (DEPTH_2, 2, SSM_HEADS), f32, math.log(1e-3), math.log(1e-1)))
    return {
        'x': nrm(ks[0], (BATCH, SEQ, d), 1.0),
        'c': nrm(ks[1], (BATCH, d), 1.0),
        'ctx': nrm(ks[2], (BATCH, CTX_LEN, d), 1.0),
        'c_ctx': nrm(ks[3], (d,), 1.0),
        'w_mod': nrm(ks[4], (DEPTH_2, d, 6 * d), 0.5 * d ** -0.5),
        'b_mod': nrm(ks[5], (DEPTH_2, 6 * d), 0.02),
        'norm1': 1.0 + nrm(ks[6], (DEPTH_2, d), 0.05),
        'norm2': 1.0 + nrm(ks[7], (DEPTH_2, d), 0.05),
        'w_in': nrm(ks[8], (DEPTH_2, d, IN_WIDTH), d ** -0.5),
        'a_sink': nrm(ks[9], (DEPTH_2, A_HEADS), 0.5),
        'ssm_conv_w': nrm(ks[10], (DEPTH_2, SSM_CONV, SSM_XBC), SSM_CONV ** -0.5),
        'ssm_conv_b': nrm(ks[12], (DEPTH_2, SSM_XBC), 0.02),
        'ssm_A_log': jnp.log(jax.random.uniform(ks[13], (DEPTH_2, 2, SSM_HEADS), f32, 1.0, 16.0)),
        'ssm_dt_bias': dt0 + jnp.log(-jnp.expm1(-dt0)),
        'ssm_D': 1.0 + nrm(ks[14], (DEPTH_2, SSM_HEADS), 0.1),
        'ssm_norm': 1.0 + nrm(ks[15], (DEPTH_2, SSM_INNER), 0.05),
        'c_q_norm': 1.0 + nrm(ks[16], (DEPTH_2, HEAD_DIM), 0.05),
        'c_k_norm': 1.0 + nrm(ks[17], (DEPTH_2, HEAD_DIM), 0.05),
        'w_oa': nrm(ks[18], (DEPTH_2, A_Q_W, d), A_Q_W ** -0.5),
        'w_ob': nrm(ks[19], (DEPTH_2, SSM_INNER, d), SSM_INNER ** -0.5),
        'w_oc': nrm(ks[20], (DEPTH_2, C_Q_W, d), C_Q_W ** -0.5),
        'w_out': nrm(ks[21], (DEPTH_2, d, d), d ** -0.5),
        'ffn_w_up': nrm(ks[22], (DEPTH_2, d, D_FF), d ** -0.5),
        'ffn_w_gate': nrm(ks[23], (DEPTH_2, d, D_FF), d ** -0.5),
        'ffn_conv_w': nrm(ks[24], (DEPTH_2, FFN_CONV, D_FF), FFN_CONV ** -0.5),
        'ffn_conv_b': nrm(ks[25], (DEPTH_2, D_FF), 0.02),
        'ffn_w_down': nrm(ks[26], (DEPTH_2, D_FF, d), D_FF ** -0.5),
        'final_norm': 1.0 + nrm(ks[27], (d,), 0.05),
    }

def second_block(x, c, ctx, c_ctx, w_mod, b_mod, norm1, norm2, w_in, a_sink, ssm_conv_w, ssm_conv_b,
              ssm_A_log, ssm_dt_bias, ssm_D, ssm_norm, c_q_norm, c_k_norm, w_oa, w_ob, w_oc, w_out,
              ffn_w_up, ffn_w_gate, ffn_conv_w, ffn_conv_b, ffn_w_down, final_norm):
    rows = x.shape[1] // GRID_W
    cos, sin = grid_rope(rows)
    xc = ctx
    sc = jax.nn.silu(c)
    scc = jax.nn.silu(c_ctx)
    for l in range(DEPTH_2):
        need_ctx_out = l < DEPTH_2 - 1
        n_cmod = 6 * D_MODEL if need_ctx_out else 2 * D_MODEL
        c_mod = sc @ w_mod[l] + b_mod[l]
        cc_mod = scc @ w_mod[l][:, :n_cmod] + b_mod[l][:n_cmod]
        x, xc = hybrid_layer(x, xc, c_mod, cc_mod, cos, sin, w_in[l], norm1[l], norm2[l], a_sink[l],
                             ssm_conv_w[l], ssm_conv_b[l], ssm_A_log[l], ssm_dt_bias[l], ssm_D[l],
                             ssm_norm[l], c_q_norm[l], c_k_norm[l], w_oa[l], w_ob[l], w_oc[l], w_out[l],
                             ffn_w_up[l], ffn_w_gate[l], ffn_conv_w[l], ffn_conv_b[l], ffn_w_down[l],
                             need_ctx_out)
    return rms_norm(x, final_norm)


def setup_inputs(seed=0):
    out = dict(first_inputs(seed))
    for name, value in second_inputs(seed + 1).items():
        if name != "x":
            out[name + "_2"] = value
    return out


def reference(
    x, norm_ffn1, ffn1_w_gate, ffn1_w_up, ffn1_w_down, norm_mix, w_in, shift_mu, rwkv_w0,
    rwkv_w2, rwkv_a0, rwkv_a2, rwkv_g2, rwkv_k_k, rwkv_k_a, rwkv_r_k, rwkv_ln_w, rwkv_ln_b,
    attn_q_norm, attn_k_norm, conv_dw_w, conv_dw_b, conv_ln_w, conv_ln_b, w_out, norm_ffn2,
    ffn2_w_gate, ffn2_w_up, ffn2_w_down, c_2, ctx_2, c_ctx_2, w_mod_2, b_mod_2, norm1_2,
    norm2_2, w_in_2, a_sink_2, ssm_conv_w_2, ssm_conv_b_2, ssm_A_log_2, ssm_dt_bias_2, ssm_D_2,
    ssm_norm_2, c_q_norm_2, c_k_norm_2, w_oa_2, w_ob_2, w_oc_2, w_out_2, ffn_w_up_2,
    ffn_w_gate_2, ffn_conv_w_2, ffn_conv_b_2, ffn_w_down_2, final_norm_2,
):
    x = first_block(
        x, norm_ffn1, ffn1_w_gate, ffn1_w_up, ffn1_w_down, norm_mix, w_in, shift_mu, rwkv_w0,
        rwkv_w2, rwkv_a0, rwkv_a2, rwkv_g2, rwkv_k_k, rwkv_k_a, rwkv_r_k, rwkv_ln_w, rwkv_ln_b,
        attn_q_norm, attn_k_norm, conv_dw_w, conv_dw_b, conv_ln_w, conv_ln_b, w_out, norm_ffn2,
        ffn2_w_gate, ffn2_w_up, ffn2_w_down,
    )
    return second_block(
        x, c_2, ctx_2, c_ctx_2, w_mod_2, b_mod_2, norm1_2, norm2_2, w_in_2, a_sink_2,
        ssm_conv_w_2, ssm_conv_b_2, ssm_A_log_2, ssm_dt_bias_2, ssm_D_2, ssm_norm_2, c_q_norm_2,
        c_k_norm_2, w_oa_2, w_ob_2, w_oc_2, w_out_2, ffn_w_up_2, ffn_w_gate_2, ffn_conv_w_2,
        ffn_conv_b_2, ffn_w_down_2, final_norm_2,
    )


_drawn_inputs = setup_inputs


def setup_inputs(seed=0):
    import zlib

    import numpy as np

    out = dict(_drawn_inputs(seed))
    spreads = {}
    factors = {'rwkv_w2': 4.467,
     'rwkv_k_k': 3.731,
     'rwkv_ln_w': 2.791,
     'rwkv_ln_b': 6.896,
     'attn_q_norm': 5.808,
     'attn_k_norm': 5.654,
     'conv_dw_b': 3.348,
     'conv_ln_b': 7.238,
     'ctx_2': 5.66,
     'b_mod_2': 3.82,
     'norm1_2': 7.196,
     'norm2_2': 5.331,
     'a_sink_2': 8.0,
     'ssm_conv_b_2': 29.576,
     'ssm_D_2': 64.0,
     'ssm_norm_2': 8.0,
     'c_q_norm_2': 8.0,
     'c_k_norm_2': 8.0,
     'ffn_conv_b_2': 8.0}
    for name, (base, spread) in spreads.items():
        noise = np.random.default_rng([zlib.crc32(name.encode()), seed]).standard_normal(out[name].shape)
        drawn = base * np.exp(spread * noise) if base else spread * noise
        out[name] = jnp.asarray(drawn.astype(out[name].dtype))
    for name, factor in factors.items():
        out[name] = (out[name] * factor).astype(out[name].dtype)
    return out
```

```python
import math
from contextlib import ExitStack

import numpy as np

import concourse.bass as bass
import concourse.mybir as mybir
from concourse.alu_op_type import AluOpType as ALU

F32 = mybir.dt.float32
BF16 = mybir.dt.bfloat16
ACT = mybir.ActivationFunctionType
AX = mybir.AxisListType

P = 128
T = 256
DM = 1024
KT = DM // P
FF = 2816
FT = FF // P
DEPTH = 2
HD = 64
NH = 6
JT = NH * HD // P
CH = 64
NC = T // CH
NPROB = NH * NC
TAPS = 31
UNIT = 2048
SLOTS = 6
LAYER_UNITS = 3 * FT // 2 + 12 + 4 + 3 * FT // 2
LAST_UNITS = 24 + 28 + 8 + 4 + 3 * FT // 2
NEG = -1.0e30

def _columns(sizes):
    at, out = 0, {}
    for name, n in sizes:
        out[name] = (at, at + n)
        at += n
    return out, at

LP, LP_N = _columns([("norm_ffn1", KT), ("norm_mix", KT), ("norm_ffn2", KT), ("mu", 10), ("a0", JT),
                     ("k_k", JT), ("k_a", JT), ("r_k", JT), ("ln_w", NH), ("ln_b", NH), ("qn", 1), ("kn", 1),
                     ("conv_w", 2 * TAPS), ("conv_b", 2), ("cln_w", 2), ("cln_b", 2), ("lora", NH * HD),
                     ("w0", NH * HD)])
SP2, SP2_N = _columns([("c", 16), ("b_mod", 48), ("norm1", KT), ("norm2", KT), ("final", KT), ("conv_w", 36),
                       ("conv_b", 12), ("a_log", 32), ("dt_bias", 32), ("d_skip", 16), ("ssm_norm", KT),
                       ("qn", 1), ("kn", 1), ("sink", 8), ("fconv_w", 3 * FT), ("fconv_b", FT),
                       ("w_dt", KT * 32)])
C0, C0_N = _columns([("ident", P), ("heads", P), ("ones", P)])
CL, CL_N = _columns([("cum", 2 * P), ("strict", CH), ("incl", CH), ("level", 6 * CH), ("first", CH),
                     ("bias", NH * 2 * T)])
CS, CS_N = _columns([("window", 2 * T), ("cos", T), ("sin", T), ("rot", P), ("fwd", 2 * T), ("bwd", 2 * T)])


def _slopes(n):
    def pow2(m):
        start = 2.0 ** (-8.0 / m)
        return [start ** (i + 1) for i in range(m)]
    c = 2 ** int(math.floor(math.log2(n)))
    return pow2(n) if c == n else pow2(c) + pow2(2 * c)[0::2][: n - c]


def constants():
    c0 = np.zeros((P, C0_N), np.float32)
    i = np.arange(P)
    c0[:, slice(*C0["ident"])] = np.eye(P)
    c0[:, slice(*C0["heads"])] = i[:, None] // HD == i[None] // HD
    c0[:, slice(*C0["ones"])] = 1.0
    cl = np.zeros((P, CL_N), np.float32)
    same = i[:, None] // CH == i[None] // CH
    a, b = CL["cum"]
    cl[:, a:a + P] = -math.exp(-0.5) * (same & (i[:, None] <= i[None]))
    cl[:, a + P:b] = -math.exp(-0.5) * (same & (i[:, None] < i[None]))
    s = np.arange(CH)
    cl[:CH, slice(*CL["strict"])] = s[:, None] < s[None]
    cl[:CH, slice(*CL["incl"])] = s[:, None] <= s[None]
    for k in range(6):
        w = 1 << k
        m = (s[:, None] // (2 * w) == s[None] // (2 * w)) & (s[:, None] // w % 2 == 1) & (s[None] // w % 2 == 0)
        cl[:CH, CL["level"][0] + k * CH:CL["level"][0] + (k + 1) * CH] = m
        if k == 0:
            cl[:CH, slice(*CL["first"])] = m.T
    t = np.arange(T)
    dist = t[:, None] - t[None]
    count = (((dist >= 0) & (dist <= 128)).astype(int) + ((dist >= 0) & (dist % 4 == 0))
             + ((dist >= 0) & (dist % 16 == 0)))
    for h, slope in enumerate(_slopes(NH)):
        full = np.where(count > 0, -slope * dist + np.log(np.maximum(count, 1)), NEG)
        a = CL["bias"][0] + h * 2 * T
        cl[:, a:a + 2 * T] = full.reshape(2, P, T).transpose(1, 0, 2).reshape(P, 2 * T)
    cs = np.zeros((P, CS_N), np.float32)
    cs[:, slice(*CS["window"])] = np.where(np.abs(dist) <= 128, 0.0, NEG).reshape(2, P, T).transpose(1, 0, 2).reshape(P, -1)
    n = HD // 4
    inv = (np.float32(10000.0) ** (-np.arange(n, dtype=np.float32) / n)).astype(np.float32)
    ang = np.concatenate([(t // 64)[:, None] * inv, (t % 64)[:, None] * inv], axis=-1).astype(np.float32)
    pair = (i % HD) // 2
    cs[:, slice(*CS["cos"])] = np.cos(ang).T[pair]
    cs[:, slice(*CS["sin"])] = np.sin(ang).T[pair]
    rot = np.zeros((P, P))
    rot[i[0::2] + 1, i[0::2]] = -1.0
    rot[i[0::2], i[0::2] + 1] = 1.0
    cs[:, slice(*CS["rot"])] = rot
    for name, m in (("fwd", t[:, None] <= t[None]), ("bwd", t[:, None] >= t[None])):
        cs[:, slice(*CS[name])] = m.reshape(2, P, T).transpose(1, 0, 2).reshape(P, -1)
    return c0, cl, cs


class Engine:

    def __init__(self, eng, sem):
        self.eng, self.sem = eng, sem
        self.restart()

    def restart(self):
        self.n, self.seen = 0, {}

    @property
    def last(self):
        return (self.sem, self.n)

    def wait(self, *results):
        for r in results:
            if r is None or r[1] == 0:
                continue
            if self.seen.get(r[0].num, 0) < r[1]:
                self.eng.wait_ge(r[0], r[1])
                self.seen[r[0].num] = r[1]

    def __call__(self, op, *args, after=(), **kw):
        self.wait(self.last, *after)
        op(*args, **kw).then_inc(self.sem, 1)
        self.n += 1
        return self.last


class Tensor(Engine):

    def restart(self):
        self.n, self.seen, self.pending = 0, {}, 0

    def mm(self, out, lhsT, rhs, start=True, stop=True, mark=False, sem=None, after=(), group=False):
        self.wait(*after)
        ins = self.eng.matmul(out, lhsT, rhs, start=start, stop=stop, skip_group_check=group)
        return self._count(ins, mark, sem)

    def flip(self, out, in_, ident, mark=False, after=()):
        self.wait(*after)
        return self._count(self.eng.transpose(out, in_, ident), mark, None)

    def _count(self, ins, mark, sem):
        if mark:
            ins.then_inc(self.sem, 1)
            self.n += 1
        elif sem is not None:
            ins.then_inc(sem, 1)
        elif self.pending:
            ins.then_inc(self.free, self.pending)
            self.pending = 0
        return self.last

    def flush(self):
        self.eng.drain().then_inc(self.free, self.pending)
        self.pending = 0

    def fence(self):
        self.eng.drain().then_inc(self.sem, 1)
        self.n += 1
        return self.last


class Banks:

    def __init__(self, bufs):
        self.bufs, self.read, self.at = list(bufs), [None] * len(bufs), -1

    def next(self):
        self.at = (self.at + 1) % len(self.bufs)
        return self.at, self.bufs[self.at], self.read[self.at]

    def done(self, at, result):
        self.read[at] = result


def build(nc, xT_in, ctxT_in, w_layers, w_last, p_layers, p_last, c0_in, cl_in, cs_in, out):
    ctx = ExitStack()

    def sb(name, shape, dt=F32, scope=None):
        return (scope or ctx).enter_context(nc.sbuf_tensor(name, shape, dt))

    def sem(name):
        return ctx.enter_context(nc.semaphore(name))

    s_pe, s_act_e, s_dve, s_pool = sem("s_pe"), sem("s_act_e"), sem("s_dve"), sem("s_pool")
    s_free = sem("s_free")
    s_slot = [sem(f"s_slot{k}") for k in range(SLOTS)]
    s_gu = sem("s_gu")
    s_sg = sem("s_sg")
    s_hid = sem("s_hid")
    s_cv = sem("s_cv")
    s_in = sem("s_in")
    s_out = sem("s_out")
    every_sem = [s_pe, s_act_e, s_dve, s_pool, s_free, *s_slot, s_gu, s_sg, s_hid, s_cv, s_in]

    PE, A, V, G = Tensor(nc.tensor, s_pe), Engine(nc.scalar, s_act_e), Engine(nc.vector, s_dve), Engine(nc.gpsimd, s_pool)
    PE.free = s_free
    ring = [sb(f"ring{k}", [P, UNIT]) for k in range(SLOTS)]
    ps = [ctx.enter_context(nc.psum_tensor(f"ps{k}", [P, 512], F32)) for k in range(8)]
    xT = sb("xT", [P, KT, T])
    hT = sb("hT", [P, KT, 2 * T])
    c0 = sb("c0", [P, C0_N])
    sg = sb("sg", [P, 2, T])
    hid = sb("hid", [P, 2, T])
    rstd = sb("rstd", [P, T])
    zeros = sb("zeros", [P, 512], BF16)
    eps = sb("eps", [P, 5])
    EPS6, EPS12, EPSG, EPSC, ONE = (eps[:, k:k + 1] for k in range(5))
    ident, heads, ones = (c0[:, slice(*C0[k])] for k in ("ident", "heads", "ones"))

    tt, ts, stt = nc.vector.tensor_tensor, nc.vector.tensor_scalar, nc.vector.scalar_tensor_tensor
    act = nc.scalar.activation
    load_n = [0]

    def load(dst, src):
        nc.scalar.dma_start(dst, src).then_inc(s_in, 16)
        load_n[0] += 16
        return (s_in, load_n[0])

    def phase():
        PE.fence()
        for e in (PE, A, V, G):
            e.wait(PE.last, A.last, V.last, G.last)

    def three(ap, n):
        return ap.rearrange("p (a b) -> p a b", a=n)

    def wide(ap, shape):
        return ap.unsqueeze(1).to_broadcast(shape)

    def stream(units, source):
        trips = units // SLOTS
        with nc.sync.Fori(0, trips) as i:
            for k in range(SLOTS):
                nc.sync.wait_ge(s_free, i * SLOTS + (k + 1))
                nc.sync.dma_start(ring[k][:, :], source(i * SLOTS + k)).then_inc(s_slot[k], 16)
        for u in range(trips * SLOTS, units):
            nc.sync.wait_ge(s_free, u + 1)
            nc.sync.dma_start(ring[u % SLOTS][:, :], source(u)).then_inc(s_slot[u % SLOTS], 16)

    unit_at = [0]

    def take_unit():
        u = unit_at[0]
        unit_at[0] += 1
        nc.tensor.wait_ge(s_slot[u % SLOTS], 16 * (u // SLOTS + 1))
        return ring[u % SLOTS]

    def give_unit():
        PE.pending += 1

    def rms(src, dst, g, square, shift=None, after=()):
        t = A(act, square, src, ACT.Square, after=after)
        for k in range(KT):
            m = PE.mm(ps[7][:, 0:T], ones, square[:, k, :], start=k == 0, stop=k == KT - 1, mark=k == KT - 1, after=[t, V.last])
        t = A(act, rstd[:, :], ps[7][:, 0:T], ACT.Sqrt, bias=EPS6, scale=1.0 / DM, after=[m, V.last])
        V(nc.vector.reciprocal, rstd[:, :], rstd[:, :], after=[t])
        for k in range(KT):
            t = V(stt, dst[:, k, :], src[:, k, :], g[:, k:k + 1], rstd[:, :], ALU.mult, ALU.mult)
            if shift is not None:
                t = V(ts, dst[:, k, :], dst[:, k, :], shift[:, k:k + 1], None, ALU.add)
        return t

    ffn_at = [0]

    def ffn(h_ready, conv=None):
        u0, base = unit_at[0], ffn_at[0] * FT
        unit_at[0] += 3 * FT // 2
        ffn_at[0] += 1
        nc_t = nc.tensor
        PE.wait(h_ready)
        for b in range(4):
            PE.mm(ps[2 + b][:, :], zeros[:, 0:P], zeros[:, :], start=True, stop=False, group=True)

        def arrived(u, i):
            nc_t.wait_ge(s_slot[u % SLOTS], i * 16 + 16 * (u // SLOTS + 1))

        def gate_up(c, i):
            nc_t.wait_ge(s_hid, i * 4 + (base + c + 1))
            for kind in range(2):
                u = u0 + 3 * (c // 2) + kind
                if c % 2 == 0:
                    arrived(u, i)
                w = three(ring[u % SLOTS][:, :], KT)
                for k in range(KT):
                    last = k == KT - 1
                    if last and kind == 0 and c % 2:
                        give_unit()
                    PE.mm(ps[c % 2][:, kind * T:(kind + 1) * T], w[:, k, (c % 2) * P:(c % 2 + 1) * P], hT[:, k, 0:T],
                          start=k == 0, stop=last, sem=s_gu if last and kind == 1 else None)
                if kind == 1 and c % 2:
                    give_unit()

        def down(c, i, last_tile=False):
            u = u0 + 3 * (c // 2) + 2
            if c % 2 == 0:
                arrived(u, i)
            nc_t.wait_ge(s_hid, i * 4 + (base + c + 3))
            w = three(ring[u % SLOTS][:, :], 2)
            for m in range(KT):
                if m == KT - 1 and c % 2 and not last_tile:
                    give_unit()
                PE.mm(ps[2 + m // 2][:, (m % 2) * T:(m % 2 + 1) * T], w[:, c % 2, m * P:(m + 1) * P], hid[:, c % 2, :],
                      start=False, stop=last_tile, group=True, mark=last_tile and m == KT - 1)

        gate_up(0, 0)
        trips = (FT - 1) // 4
        with nc_t.Fori(0, trips) as i:
            for c in range(4):
                gate_up(c + 1, i)
                down(c, i)
        for c in range(4 * trips, FT):
            if c + 1 < FT:
                gate_up(c + 1, 0)
            down(c, 0, c == FT - 1)
        give_unit()

        def silu_tile(c, i):
            nc.scalar.wait_ge(s_gu, i * 4 + (base + c + 1))
            act(sg[:, c % 2, :], ps[c % 2][:, 0:T], ACT.Silu).then_inc(s_sg, 1)

        def mult_tile(c, i):
            nc.vector.wait_ge(s_sg, i * 4 + (base + c + 1))
            tt(hid[:, c % 2, :], sg[:, c % 2, :], ps[c % 2][:, T:2 * T], ALU.mult).then_inc(s_hid, 1)

        def conv_silu(c, i):
            nc.scalar.wait_ge(s_gu, i * 4 + (base + c + 1))
            act(conv["pad"][:, c % 2, 1:T + 1], ps[c % 2][:, 0:T], ACT.Copy).then_inc(s_sg, 1)
            nc.scalar.wait_ge(s_cv, i * 12 + (3 * c + 3))
            act(sg[:, c % 2, :], conv["sum"][:, c % 2, :], ACT.Silu).then_inc(s_sg, 1)

        def conv_mult(c, i):
            n = i * 4 + c
            pad, total = conv["pad"][:, c % 2, :], conv["sum"][:, c % 2, :]
            w = [conv["w"][:, bass.ds(n * 3 + k, 1)] for k in range(3)]
            nc.vector.wait_ge(s_sg, i * 8 + (2 * c + 1 + base))
            ts(total, pad[:, 1:T + 1], w[1], conv["b"][:, bass.ds(n, 1)], ALU.mult, ALU.add).then_inc(s_cv, 1)
            for k in (0, 2):
                nc.vector.wait_ge(s_cv, i * 12 + (3 * c + 1 + k // 2))
                stt(total, pad[:, k:k + T], w[k], total, ALU.mult, ALU.add).then_inc(s_cv, 1)
            nc.vector.wait_ge(s_sg, i * 8 + (2 * c + 2 + base))
            tt(hid[:, c % 2, :], sg[:, c % 2, :], ps[c % 2][:, T:2 * T], ALU.mult).then_inc(s_hid, 1)

        for eng, step in ((nc.scalar, conv_silu if conv else silu_tile), (nc.vector, conv_mult if conv else mult_tile)):
            with eng.Fori(0, FT // 4) as i:
                for c in range(4):
                    step(c, i)
            for c in range(FT // 4 * 4, FT):
                step(c, 0)
        return PE.last

    def start_engines():
        for e in (PE, A, V, G):
            e.restart()
        unit_at[0] = ffn_at[0] = load_n[0] = 0
        nc.tensor.sem_inc(s_free, SLOTS)
        nc.vector.sem_inc(s_hid, 2)

    def end_stretch():
        nc.all_engine_barrier()
        for s in every_sem:
            nc.gpsimd.sem_clear(s)
        nc.all_engine_barrier()

    def attention(tag, nheads, kt_n, q, k, v, store, scope, scale, bias=None, sink=None, ready=()):
        width = kt_n * P
        nb = width // T
        pr = sb(f"prob_{tag}", [P, 2, 2, width], scope=scope)
        pT = sb(f"probT_{tag}", [P, 2, kt_n, T], scope=scope)
        st = sb(f"stat_{tag}", [P, 2, 8], scope=scope)
        score_read, flip_read, out_read = [None] * 2, None, [None] * 2
        prob_read, pT_read, sm = [None] * 2, [None] * 2, [None] * 2

        def scores(h):
            nonlocal flip_read
            d = h % 2
            def bank(tt_i):
                return ps[nb * d + tt_i][:, 0:width] if nb == 2 else ps[d][:, tt_i * width:(tt_i + 1) * width]
            for ti in range(2):
                m = PE.mm(bank(ti), q(h)[:, ti * P:(ti + 1) * P], k(h), mark=True, after=[score_read[d], *ready])
                s = pr[:, d, ti, :]
                b = bias(h, ti) if bias else None
                if b is not None:
                    n = b.shape[-1]
                    V(stt, s[:, 0:n], bank(ti)[:, 0:n], scale, b, ALU.mult, ALU.add, after=[m, prob_read[d]])
                    if n < width:
                        V(ts, s[:, n:width], bank(ti)[:, n:width], scale, None, ALU.mult)
                else:
                    V(ts, s, bank(ti), scale, None, ALU.mult, after=[m, prob_read[d]])
                score_read[d] = V.last
            mx, neg, sm_c, e_sink, inv = (st[:, d, k2:k2 + 2] if k2 < 8 else None for k2 in (0, 2, 4, 6, 4))
            V(nc.vector.tensor_reduce, mx, pr[:, d, :, :], AX.X, ALU.max)
            if sink is not None:
                V(ts, mx, mx, sink[:, h:h + 1], None, ALU.max)
            t = V(ts, neg, mx, -1.0, None, ALU.mult)
            for ti in range(2):
                e = A(act, pr[:, d, ti, :], pr[:, d, ti, :], ACT.Exp, bias=neg[:, ti:ti + 1], accum_out=sm_c[:, ti:ti + 1], after=[t])
            if sink is not None:
                e = A(act, e_sink, neg, ACT.Exp, bias=sink[:, h:h + 1])
                V(tt, sm_c, sm_c, e_sink, ALU.add, after=[e])
            V(nc.vector.reciprocal, inv, sm_c, after=[e])
            for ti in range(2):
                sm[d] = V(ts, pr[:, d, ti, :], pr[:, d, ti, :], inv[:, ti:ti + 1], None, ALU.mult)

        def finish(h):
            nonlocal flip_read
            d = h % 2
            for kt in range(kt_n):
                bank = ps[4 + kt // 2]
                for ti in range(2):
                    m = PE.flip(bank[:, (kt % 2) * T + ti * P:(kt % 2) * T + (ti + 1) * P], pr[:, d, ti, kt * P:(kt + 1) * P],
                                ident, mark=True, after=[sm[d], flip_read])
            prob_read[d] = m
            for b in range(kt_n // 2):
                c = A(act, pT[:, d, 2 * b:2 * b + 2, :], three(ps[4 + b][:, :], 2), ACT.Copy, after=[m, pT_read[d]])
            flip_read = c
            o = ps[6 + d][0:HD, 0:T]
            for kt in range(kt_n):
                m = PE.mm(o, v(h, kt), pT[:, d, kt, :], start=kt == 0, stop=kt == kt_n - 1, mark=kt == kt_n - 1,
                          after=[c, out_read[d]])
            pT_read[d] = m
            out_read[d] = A(act, store(h), o, ACT.Copy, after=[m])

        for h in range(nheads + 1):
            if h < nheads:
                scores(h)
            if h > 0:
                finish(h - 1)

    for c, v in enumerate((1e-6, 1e-12, 64e-5, 1e-5, 1.0)):
        V(nc.vector.memset, eps[:, c:c + 1], v)
    V(nc.vector.memset, zeros[:, :], 0.0)
    load(c0[:, :], c0_in)
    load(xT[:, :, :], xT_in)
    nc.scalar.wait_ge(s_in, 32)
    end_stretch()

    with nc.Fori(0, DEPTH) as layer:
        start_engines()
        lay = ExitStack()
        pl = sb("pl", [P, LP_N], scope=lay)
        mixT = sb("mixT", [P, KT, T], scope=lay)
        t_pl = load(pl[:, :], p_layers[layer, :, :])
        stream(LAYER_UNITS, lambda u: w_layers[layer, u, :, :])
        for e in (V, PE, A):
            e.wait(t_pl)

        def col(name):
            return pl[:, slice(*LP[name])]

        def half_residual(done):
            for b in range(4):
                t = V(stt, xT[:, 2 * b:2 * b + 2, :], three(ps[2 + b][:, :], 2), 0.5, xT[:, 2 * b:2 * b + 2, :], ALU.mult, ALU.add, after=[done])
            return t

        h = rms(xT[:, :, :], hT[:, :, 0:T], col("norm_ffn1"), hT[:, :, T:2 * T])
        h = half_residual(ffn(h))
        phase()

        h = rms(xT[:, :, :], hT[:, :, 0:T], col("norm_mix"), hT[:, :, T:2 * T])
        mix = ExitStack()
        rkv = sb("rkv", [P, 10, T], scope=mix)
        m1 = ExitStack()
        cl = sb("cl", [P, CL_N - CL["bias"][0]], scope=m1)
        t_cl = load(cl[:, :], cl_in[:, slice(*CL["bias"])])
        raw = sb("raw", [P, 10, T + 1], scope=m1)
        qk = sb("qk", [P, 2 * JT, T], scope=m1)
        vtok = sb("vtok", [P, 2, NH * HD], scope=m1)
        cz = sb("cz", [P, 2, TAPS - 1 + T], scope=m1)
        cu = sb("cu", [P, 2, T], scope=m1)
        V(nc.vector.memset, raw[:, :, 0:1], 0.0)
        V(nc.vector.memset, cz[:, :, 0:TAPS - 1], 0.0)
        banks = Banks(ps[0:6])
        w_at = {}

        def columns(tile):
            if tile // 2 not in w_at:
                w_at[tile // 2] = take_unit()
            return three(w_at[tile // 2][:, :], KT)[:, :, (tile % 2) * P:(tile % 2 + 1) * P]

        for tile in range(23):
            w = columns(tile)
            at, bank, read = banks.next()
            if 16 <= tile < 19:
                for ti in range(2):
                    for k in range(KT):
                        m = PE.mm(bank[:, ti * T:ti * T + P], hT[:, k, ti * P:(ti + 1) * P], w[:, k, :],
                                  start=k == 0, stop=k == KT - 1, mark=ti == 1 and k == KT - 1, after=[read, h])
                t = A(act, vtok[:, :, (tile - 16) * P:(tile - 15) * P], three(bank[:, :], 2)[:, :, 0:P], ACT.Copy, after=[m])
            else:
                for k in range(KT):
                    m = PE.mm(bank[:, 0:T], w[:, k, :], hT[:, k, 0:T], start=k == 0, stop=k == KT - 1, mark=k == KT - 1,
                              after=[read, h])
                if tile < 10:
                    t = A(act, raw[:, tile, 1:T + 1], bank[:, 0:T], ACT.Copy, after=[m])
                elif tile < 16:
                    t = A(act, qk[:, tile - 10, :], bank[:, 0:T], ACT.Copy, after=[m])
                elif tile < 21:
                    t = A(act, cu[:, tile - 19, :], bank[:, 0:T], ACT.Copy, after=[m])
                else:
                    t = A(act, cz[:, tile - 21, TAPS - 1:TAPS - 1 + T], bank[:, 0:T], ACT.Sigmoid, after=[m])
            banks.done(at, t)
            if tile % 2 or tile == 22:
                give_unit()
        proj = t

        V(tt, rkv[:, :, :], raw[:, :, 0:T], raw[:, :, 1:T + 1], ALU.subtract, after=[proj])
        mu = col("mu")
        for j in range(10):
            V(stt, rkv[:, j, :], rkv[:, j, :], mu[:, j:j + 1], raw[:, j, 1:T + 1], ALU.mult, ALU.add)

        qh = sb("qh", [HD, NH, T], scope=m1)
        kh = sb("kh", [HD, NH, T], scope=m1)
        rq = sb("rq", [P, JT, T], scope=m1)
        for which, dst, g in ((0, qh, "qn"), (1, kh, "kn")):
            src = qk[:, which * JT:(which + 1) * JT, :]
            sq = A(act, rq[:, :, :], src, ACT.Square, after=[V.last])
            for j in range(JT):
                m = PE.mm(ps[6][:, 0:T], heads, rq[:, j, :], mark=True, after=[sq, A.last])
                A(act, rq[:, j, :], ps[6][:, 0:T], ACT.Sqrt, bias=EPS6, scale=1.0 / HD, after=[m])
            V(nc.vector.reciprocal, rq[:, :, :], rq[:, :, :], after=[A.last])
            for p in range(2):
                r = slice(p * HD, (p + 1) * HD)
                V(stt, dst[:, p::2, :], src[r, :, :], col(g)[r, :], rq[r, :, :], ALU.mult, ALU.mult)
        V.wait(t_cl)

        def mix_rows(h):
            return mixT[(h % 2) * HD:(h % 2 + 1) * HD, JT + h // 2, :]

        attention("l", NH, 2, lambda h: qh[:, h, :], lambda h: kh[:, h, :], lambda h, kt: vtok[:, kt, h * HD:(h + 1) * HD],
                  mix_rows, m1, HD ** -0.5, bias=lambda h, ti: cl[:, (2 * h + ti) * T:(2 * h + ti + 1) * T], ready=[V.last])

        cc = sb("cc", [P, 2, T], scope=m1)
        csq = sb("csq", [P, 2, T], scope=m1)
        V(tt, cz[:, :, TAPS - 1:], cz[:, :, TAPS - 1:], cu[:, :, :], ALU.mult)
        for j in range(2):
            w = col("conv_w")[:, j * TAPS:(j + 1) * TAPS]
            V(ts, cc[:, j, :], cz[:, j, 0:T], w[:, 0:1], col("conv_b")[:, j:j + 1], ALU.mult, ALU.add)
            for k in range(1, TAPS):
                V(stt, cc[:, j, :], cz[:, j, k:k + T], w[:, k:k + 1], cc[:, j, :], ALU.mult, ALU.add)
        for step in range(2):
            if step:
                A(act, csq[:, :, :], cc[:, :, :], ACT.Square, after=[V.last])
            src = csq if step else cc
            for j in range(2):
                m = PE.mm(ps[6][:, 0:T], ones, src[:, j, :], start=j == 0, stop=j == 1, mark=j == 1, after=[V.last, A.last])
            if step == 0:
                for j in range(2):
                    V(stt, cc[:, j, :], ps[6][:, 0:T], -1.0 / (2 * P), cc[:, j, :], ALU.mult, ALU.add, after=[m])
        t = A(act, rstd[:, :], ps[6][:, 0:T], ACT.Sqrt, bias=EPSC, scale=1.0 / (2 * P), after=[m])
        V(nc.vector.reciprocal, rstd[:, :], rstd[:, :], after=[t])
        for j in range(2):
            V(stt, cc[:, j, :], cc[:, j, :], col("cln_w")[:, j:j + 1], rstd[:, :], ALU.mult, ALU.mult)
            A(act, mixT[:, 2 * JT + j, :], cc[:, j, :], ACT.Silu, bias=col("cln_b")[:, j:j + 1], after=[V.last])
        phase()
        m1.close()

        m3 = ExitStack()
        cr = sb("cr", [P, CL["bias"][0]], scope=m3)
        t_cr = load(cr[:, :], cl_in[:, 0:CL["bias"][0]])
        arh = sb("arh", [HD, NH, NC, 2, CH], scope=m3)
        bh = sb("bh", [HD, NH, T], scope=m3)
        kh2 = sb("kh2", [HD, NH, T], scope=m3)
        btok = sb("btok", [CH, NC, NH * HD], scope=m3)
        ktok = sb("ktok", [CH, NC, NH * HD], scope=m3)
        vtk = sb("vtk", [CH, NC, NH * HD], scope=m3)
        dch = sb("dch", [HD, NH, NC], scope=m3)
        bonus = sb("bonus", [P, JT, T], scope=m3)
        gate = sb("gate", [P, JT, T], scope=m3)
        m2 = ExitStack()
        lo = sb("lo", [P, T], scope=m2)
        sgw = sb("sgw", [P, 2, NH * HD], scope=m2)
        d_in = sb("d_in", [P, JT, T], scope=m2)
        d_ex = sb("d_ex", [P, JT, T], scope=m2)
        d_inv = sb("d_inv", [P, JT, T], scope=m2)
        aT = sb("aT", [P, JT, T], scope=m2)
        kk = sb("kk", [P, JT, T], scope=m2)
        knew = sb("knew", [P, JT, T], scope=m2)
        tmp = sb("tmp", [P, JT, T], scope=m2)
        for e in (V, PE):
            e.wait(t_cr)
        lora = col("lora")
        r_, k_, v_ = (rkv[:, j * JT:(j + 1) * JT, :] for j in range(3))
        A(act, lo[0:32, :], rkv[0:32, 9, :], ACT.Tanh)
        A(act, lo[32:64, :], rkv[32:64, 9, :], ACT.Copy)
        t = A(act, lo[64:128, :], rkv[64:128, 9, :], ACT.Sigmoid)
        for ti in range(2):
            m = PE.mm(ps[ti][:, 0:NH * HD], lo[0:32, ti * P:(ti + 1) * P], lora[0:32, :], mark=True, after=[t])
            V(tt, sgw[:, ti, :], ps[ti][:, 0:NH * HD], col("w0"), ALU.add, after=[m])
        t = A(act, sgw[:, :, :], sgw[:, :, :], ACT.Sigmoid, after=[V.last])
        for j in range(JT):
            for ti in range(2):
                m = PE.mm(ps[2 + j][:, ti * T:(ti + 1) * T], sgw[:, ti, j * P:(j + 1) * P], cr[:, 0:T], mark=True, after=[t])
            cum = ps[2 + j][:, :].rearrange("p (t e s) -> p e t s", t=2, e=2)
            for dst, e, sign in ((d_in, 0, 1.0), (d_ex, 1, 1.0), (d_inv, 0, -1.0)):
                A(act, three(dst[:, j, :], 2), cum[:, e, :, :], ACT.Exp, scale=sign, after=[m])
        for j in range(JT):
            m = PE.mm(ps[5][:, 0:T], lora[32:64, j * P:(j + 1) * P], lo[32:64, :], mark=True, after=[A.last])
            A(act, aT[:, j, :], ps[5][:, 0:T], ACT.Sigmoid, bias=col("a0")[:, j:j + 1], after=[m])
        for j in range(JT):
            m = PE.mm(ps[6][:, 0:T], lora[64:128, j * P:(j + 1) * P], lo[64:128, :], mark=True, after=[A.last])
            A(act, gate[:, j, :], ps[6][:, 0:T], ACT.Copy, after=[m])
        for j in range(JT):
            V(ts, kk[:, j, :], k_[:, j, :], col("k_k")[:, j:j + 1], None, ALU.mult)
        A(act, tmp[:, :, :], kk[:, :, :], ACT.Square, after=[V.last])
        for j in range(JT):
            m = PE.mm(ps[7][:, 0:T], heads, tmp[:, j, :], mark=True, after=[A.last])
            A(act, tmp[:, j, :], ps[7][:, 0:T], ACT.Sqrt, bias=EPS12, after=[m])
        V(nc.vector.reciprocal, tmp[:, :, :], tmp[:, :, :], after=[A.last])
        V(tt, kk[:, :, :], kk[:, :, :], tmp[:, :, :], ALU.mult)
        for j in range(JT):
            V(ts, knew[:, j, :], aT[:, j, :], 1.0, col("k_a")[:, j:j + 1], ALU.subtract, ALU.mult)
        V(stt, knew[:, :, :], knew[:, :, :], 1.0, k_, ALU.add, ALU.mult)
        for j in range(JT):
            V(stt, tmp[:, j, :], r_[:, j, :], col("r_k")[:, j:j + 1], knew[:, j, :], ALU.mult, ALU.mult)
        for j in range(JT):
            m = PE.mm(ps[j % 2][:, 0:T], heads, tmp[:, j, :], mark=True, after=[V.last])
            V(tt, bonus[:, j, :], v_[:, j, :], ps[j % 2][:, 0:T], ALU.mult, after=[m])
        V(tt, d_ex[:, :, :], kk[:, :, :], d_ex[:, :, :], ALU.mult)
        V(stt, kk[:, :, :], kk[:, :, :], -1.0, aT[:, :, :], ALU.mult, ALU.mult)
        for p in range(2):
            r = slice(p * HD, (p + 1) * HD)
            for j in range(JT):
                h_i = 2 * j + p
                V(nc.vector.tensor_copy, arh[:, h_i, :, 0, :], three(d_ex[r, j, :], NC))
                V(tt, arh[:, h_i, :, 1, :], three(r_[r, j, :], NC), three(d_in[r, j, :], NC), ALU.mult)
                V(nc.vector.tensor_copy, dch[:, h_i, :], three(d_in[r, j, :], NC)[:, :, CH - 1])
            V(tt, bh[:, p::2, :], kk[r, :, :], d_inv[r, :, :], ALU.mult)
            V(tt, kh2[:, p::2, :], knew[r, :, :], d_inv[r, :, :], ALU.mult)
        banks = Banks(ps[0:6])
        for c in range(NC):
            for src, dst in ((bh, btok), (kh2, ktok), (None, vtk)):
                at, bank, read = banks.next()
                if src is not None:
                    for h_i in range(NH):
                        m = PE.flip(bank[0:CH, h_i * HD:(h_i + 1) * HD], src[:, h_i, c * CH:(c + 1) * CH], ident[0:HD, 0:HD],
                                    mark=h_i == NH - 1, after=[read, V.last])
                else:
                    for j in range(JT):
                        m = PE.flip(bank[0:CH, j * P:(j + 1) * P], v_[:, j, c * CH:(c + 1) * CH], ident, mark=j == JT - 1, after=[read])
                banks.done(at, A(act, dst[:, c, :], bank[0:CH, 0:NH * HD], ACT.Copy, after=[m]))
        phase()
        m2.close()

        m4 = ExitStack()
        mb = sb("mb", [CH, NPROB, 2 * CH], scope=m4)
        mk = sb("mk", [CH, NPROB, 2 * CH], scope=m4)
        lw = sb("lw", [CH, NPROB, CH], scope=m4)
        yi = sb("yi", [CH, NPROB, CH], scope=m4)
        xi = sb("xi", [CH, NPROB, CH], scope=m4)
        yT = sb("yT", [HD, NH, T], scope=m4)
        state = sb("state", [HD, NH, HD], scope=m4)
        gs = sb("gs", [CH, NH * HD], scope=m4)
        us = sb("us", [CH, NH * HD], scope=m4)
        flat = hT[:, :, :].rearrange("p a b -> p (a b)")
        lev = flat[0:CH, 0:NPROB * CH].rearrange("p (a b) -> p a b", a=NPROB)
        pr1 = flat[0:CH, NPROB * CH:2 * NPROB * CH].rearrange("p (a b) -> p a b", a=NPROB)
        masks = {n: cr[0:CH, slice(*CL[n])] for n in ("strict", "incl", "first")}
        both = cr[0:CH, CL["strict"][0]:CL["incl"][1]]
        level = [cr[0:CH, CL["level"][0] + k * CH:CL["level"][0] + (k + 1) * CH] for k in range(6)]
        banks = Banks(ps[0:8])
        for src, dst in ((bh, mb), (kh2, mk)):
            for b in range(NPROB // 4):
                at, bank, read = banks.next()
                for q in range(4):
                    h_i, c = divmod(4 * b + q, NC)
                    m = PE.mm(bank[0:CH, q * 2 * CH:(q + 1) * 2 * CH], src[:, h_i, c * CH:(c + 1) * CH],
                              arh[:, h_i, c, :, :], mark=q == 3, after=[read])
                banks.done(at, V(tt, dst[:, 4 * b:4 * b + 4, :], three(bank[0:CH, :], 4), wide(both, [CH, 4, 2 * CH]), ALU.mult, after=[m]))
        for b in range(NPROB // 8):
            at, bank, read = banks.next()
            for q in range(8):
                h_i, c = divmod(8 * b + q, NC)
                m = PE.mm(bank[0:CH, q * CH:(q + 1) * CH], arh[:, h_i, c, 0, :], bh[:, h_i, c * CH:(c + 1) * CH], mark=q == 7, after=[read])
            banks.done(at, V(nc.vector.tensor_copy, lw[:, 8 * b:8 * b + 8, :], three(bank[0:CH, :], 8), after=[m]))

        all3 = [CH, NPROB, CH]
        V(tt, xi[:, :, :], lw[:, :, :], wide(level[0], all3), ALU.mult)
        V(tt, xi[:, :, :], xi[:, :, :], wide(ident[0:CH, 0:CH], all3), ALU.add)
        V(tt, yi[:, :, :], mb[:, :, 0:CH], wide(masks["first"], all3), ALU.mult)
        V(tt, yi[:, :, :], yi[:, :, :], wide(ident[0:CH, 0:CH], all3), ALU.add)
        for k in range(1, 6):
            t_lev = V(tt, lev, lw[:, :, :], wide(level[k], all3), ALU.mult, after=[PE.last])
            ready = []
            for b in range(3):
                at, bank, read = banks.next()
                for q in range(8):
                    n = 8 * b + q
                    m = PE.mm(bank[0:CH, q * CH:(q + 1) * CH], lev[:, n, :], yi[:, n, :], mark=q == 7, after=[read, t_lev])
                t = A(act, pr1[:, 8 * b:8 * b + 8, :], three(bank[0:CH, :], 8), ACT.Copy, after=[m])
                banks.done(at, t)
                ready.append(t)
            sums = []
            for b in range(3):
                for w, dst in ((0, yi), (1, xi)) if k < 5 else ((0, yi),):
                    at, bank, read = banks.next()
                    for q in range(8):
                        n = 8 * b + q
                        l, r = (xi[:, n, :], pr1[:, n, :]) if w == 0 else (pr1[:, n, :], xi[:, n, :])
                        m = PE.mm(bank[0:CH, q * CH:(q + 1) * CH], l, r, mark=q == 7, after=[read, ready[b]])
                    sums.append((at, bank, m, dst, b))
                for at, bank, _, dst, b2 in sums[-2:] if k < 5 else sums[-1:]:
                    banks.done(at, V(tt, dst[:, 8 * b2:8 * b2 + 8, :], three(bank[0:CH, :], 8), dst[:, 8 * b2:8 * b2 + 8, :], ALU.add, after=[m]))

        y_read = [None] * 2
        for c in range(NC):
            g_ps, u_ps, y_ps, s_ps = ps[0:4] if c % 2 == 0 else ps[4:8]
            for h_i in range(NH):
                n, o = h_i * NC + c, slice(h_i * HD, (h_i + 1) * HD)
                if c:
                    PE.mm(g_ps[0:CH, o], arh[:, h_i, c, 0, :], state[:, h_i, :], start=True, stop=False, after=[V.last])
                m = PE.mm(g_ps[0:CH, o], mk[:, n, 0:CH], vtk[:, c, o], start=c == 0, stop=True, mark=h_i == NH - 1, after=[V.last])
            t = V(nc.vector.tensor_copy, gs[:, :], g_ps[0:CH, 0:NH * HD], after=[m])
            for h_i in range(NH):
                n, o = h_i * NC + c, slice(h_i * HD, (h_i + 1) * HD)
                m = PE.mm(u_ps[0:CH, o], yi[:, n, :], gs[:, o], mark=h_i == NH - 1, after=[t])
            t = V(nc.vector.tensor_copy, us[:, :], u_ps[0:CH, 0:NH * HD], after=[m])
            PE.wait(y_read[c % 2])
            if c < NC - 1:
                for h_i in range(NH):
                    o = slice(h_i * HD, (h_i + 1) * HD)
                    PE.mm(s_ps[0:HD, o], btok[:, c, o], us[:, o], start=True, stop=False, after=[t])
                    m = PE.mm(s_ps[0:HD, o], ktok[:, c, o], vtk[:, c, o], start=False, stop=True, mark=h_i == NH - 1)
            for h_i in range(NH):
                n, o = h_i * NC + c, slice(h_i * HD, (h_i + 1) * HD)
                if c:
                    PE.mm(y_ps[0:HD, h_i * CH:(h_i + 1) * CH], state[:, h_i, :], arh[:, h_i, c, 1, :], start=True, stop=False)
                PE.mm(y_ps[0:HD, h_i * CH:(h_i + 1) * CH], us[:, o], mb[:, n, CH:2 * CH], start=c == 0, stop=False, after=[t])
                m2_ = PE.mm(y_ps[0:HD, h_i * CH:(h_i + 1) * CH], vtk[:, c, o], mk[:, n, CH:2 * CH], start=False, stop=True, mark=h_i == NH - 1)
            y_read[c % 2] = A(act, yT[:, :, c * CH:(c + 1) * CH], three(y_ps[0:HD, 0:NH * CH], NH), ACT.Copy, after=[m2_])
            if c < NC - 1:
                s3 = three(s_ps[0:HD, 0:NH * HD], NH)
                decay = dch[:, :, c:c + 1].to_broadcast([HD, NH, HD])
                if c:
                    V(tt, state[:, :, :], s3, state[:, :, :], ALU.add, after=[m, m2_])
                    V(tt, state[:, :, :], state[:, :, :], decay, ALU.mult)
                else:
                    V(tt, state[:, :, :], s3, decay, ALU.mult, after=[m])

        yf = yT[:, :, :].rearrange("p a b -> p (a b)")
        sqf = lev.rearrange("p a b -> p (a b)")
        for b in range(3):
            s = slice(b * 512, (b + 1) * 512)
            m = PE.mm(ps[b][0:HD, :], heads[0:HD, 0:HD], yf[:, s], mark=True, after=[A.last, V.last])
            V(stt, yf[:, s], ps[b][0:HD, :], -1.0 / HD, yf[:, s], ALU.mult, ALU.add, after=[m])
        A(act, sqf, yf, ACT.Square, after=[V.last])
        for b in range(3):
            s = slice(b * 512, (b + 1) * 512)
            m = PE.mm(ps[3 + b][0:HD, :], heads[0:HD, 0:HD], sqf[:, s], mark=True, after=[A.last])
            A(act, sqf[:, s], ps[3 + b][0:HD, :], ACT.Sqrt, bias=EPSG[0:HD, :], scale=1.0 / HD, after=[m])
        V(nc.vector.reciprocal, sqf, sqf, after=[A.last])
        V(tt, yf, yf, sqf, ALU.mult)
        for h_i in range(NH):
            r = slice((h_i % 2) * HD, (h_i % 2 + 1) * HD)
            V(ts, mixT[r, h_i // 2, :], yT[:, h_i, :], col("ln_w")[0:HD, h_i:h_i + 1], col("ln_b")[0:HD, h_i:h_i + 1], ALU.mult, ALU.add)
        V(tt, mixT[:, 0:JT, :], mixT[:, 0:JT, :], bonus[:, :, :], ALU.add)
        h = V(tt, mixT[:, 0:JT, :], mixT[:, 0:JT, :], gate[:, :, :], ALU.mult)
        phase()
        m4.close()
        m3.close()
        mix.close()

        banks = Banks(ps[0:4])
        for m_i in range(KT):
            if m_i % 2 == 0:
                w = three(take_unit()[:, :], KT)
            at, bank, read = banks.next()
            for k in range(KT):
                m = PE.mm(bank[:, 0:T], w[:, k, (m_i % 2) * P:(m_i % 2 + 1) * P], mixT[:, k, :], start=k == 0, stop=k == KT - 1,
                          mark=k == KT - 1, after=[read])
            if m_i % 2:
                give_unit()
            banks.done(at, V(tt, xT[:, m_i, :], bank[:, 0:T], xT[:, m_i, :], ALU.add, after=[m]))

        h = rms(xT[:, :, :], hT[:, :, 0:T], col("norm_ffn2"), hT[:, :, T:2 * T], after=[V.last])
        half_residual(ffn(h))
        phase()
        lay.close()
        end_stretch()

    start_engines()
    pp = sb("pp", [P, SP2_N])
    cs = sb("cs", [P, CS_N])
    sc = sb("sc", [P, 16])
    mod = sb("mod", [P, 48])
    cmod = sb("cmod", [P, 16])
    scale_x = sb("scale_x", [P, KT])
    scale_c = sb("scale_c", [P, KT])
    scale_2 = sb("scale_2", [P, KT])
    cx = ExitStack()
    ctxT = sb("ctxT", [P, KT, T], scope=cx)
    sq8 = sb("sq8", [P, KT, T], scope=cx)
    load(pp[:, :], p_last)
    load(cs[:, :], cs_in)
    t_in = load(ctxT[:, :, :], ctxT_in)
    stream(LAST_UNITS, lambda u: w_last[u, :, :])
    for e in (V, PE, A):
        e.wait(t_in)

    def col2(name):
        return pp[:, slice(*SP2[name])]

    def const(name):
        return cs[:, slice(*CS[name])]

    t = A(act, sc[:, :], col2("c"), ACT.Silu)
    for m_i in range(48):
        if m_i % 2 == 0:
            w = three(take_unit()[:, :], KT)
        for k in range(KT):
            m = PE.mm(ps[0][:, 2 * m_i:2 * m_i + 2], w[:, k, (m_i % 2) * P:(m_i % 2 + 1) * P], sc[:, 2 * k:2 * k + 2],
                      start=k == 0, stop=k == KT - 1, mark=m_i == 47 and k == KT - 1, after=[t])
        if m_i % 2:
            give_unit()
    mod_ps = ps[0][:, 0:96].rearrange("p (a b) -> p a b", b=2)
    V(tt, mod[:, :], mod_ps[:, :, 0], col2("b_mod"), ALU.add, after=[m])
    V(tt, cmod[:, :], mod_ps[:, 0:16, 1], col2("b_mod")[:, 0:16], ALU.add)
    shift1, gate1, shift2, gate2 = mod[:, 0:8], mod[:, 16:24], mod[:, 24:32], mod[:, 40:48]
    V(stt, scale_x[:, :], mod[:, 8:16], 1.0, col2("norm1"), ALU.add, ALU.mult)
    V(stt, scale_c[:, :], cmod[:, 8:16], 1.0, col2("norm1"), ALU.add, ALU.mult)
    V(stt, scale_2[:, :], mod[:, 32:40], 1.0, col2("norm2"), ALU.add, ALU.mult)
    rms(xT[:, :, :], hT[:, :, 0:T], scale_x, sq8[:, :, :], shift=shift1)
    h = rms(ctxT[:, :, :], hT[:, :, T:2 * T], scale_c, sq8[:, :, :], shift=cmod[:, 0:8], after=[PE.last])
    phase()
    cx.close()

    yaT = sb("yaT", [P, 4, T])
    ygT = sb("ygT", [P, 4, T])
    ysT = sb("ysT", [P, KT, T])
    atn = ExitStack()
    ssd = ExitStack()

    def project(dst_bank, w, width, after, mark=True):
        for k in range(KT):
            m = PE.mm(dst_bank[:, 0:width], w[:, k, :], hT[:, k, 0:width], start=k == 0, stop=k == KT - 1, mark=k == KT - 1, after=after)
        return m

    def half(w, j):
        return w[:, :, j * P:(j + 1) * P]

    kr = sb("kr", [P, 2, 2 * T], scope=atn)
    vt2 = sb("vt2", [P, 4, 2 * P], scope=atn)
    q8 = sb("q8", [P, 8, T], scope=atn)
    banks = Banks(ps[0:6])
    w = three(take_unit()[:, :], KT)
    for j in range(2):
        at, bank, read = banks.next()
        m = project(bank, half(w, j), 2 * T, [read, h])
        banks.done(at, A(act, kr[:, j, :], bank[:, :], ACT.Copy, after=[m]))
    give_unit()
    w = three(take_unit()[:, :], KT)
    for ti in range(4):
        at, bank, read = banks.next()
        for k in range(KT):
            m = PE.mm(bank[:, 0:2 * P], hT[:, k, ti * P:(ti + 1) * P], w[:, k, :], start=k == 0, stop=k == KT - 1, mark=k == KT - 1, after=[read])
        banks.done(at, A(act, vt2[:, ti, :], bank[:, 0:2 * P], ACT.Copy, after=[m]))
    give_unit()
    for j in range(8):
        if j % 2 == 0:
            w = three(take_unit()[:, :], KT)
        at, bank, read = banks.next()
        m = project(bank, half(w, j % 2), T, [read])
        banks.done(at, A(act, q8[:, j, :], bank[:, 0:T], ACT.Copy, after=[m]))
        if j % 2:
            give_unit()

    nrm = sb("nrm", [P, 512], scope=atn)
    rtmp = sb("rtmp", [P, T], scope=atn)
    for j in range(5):
        src, width = (q8[:, 4 + j, :], T) if j < 4 else (kr[:, 1, :], 2 * T)
        t = A(act, nrm[:, 0:width], src, ACT.Square, after=[V.last])
        m = PE.mm(ps[6][:, 0:width], heads, nrm[:, 0:width], mark=True, after=[t])
        t = A(act, nrm[:, 0:width], ps[6][:, 0:width], ACT.Sqrt, bias=EPS6, scale=1.0 / HD, after=[m])
        V(nc.vector.reciprocal, nrm[:, 0:width], nrm[:, 0:width], after=[t])
        V(stt, src, src, col2("qn" if j < 4 else "kn"), nrm[:, 0:width], ALU.mult, ALU.mult)
    qs = sb("qs", [HD, 16, T], scope=atn)
    ks = sb("ks", [HD, 4, 2 * T], scope=atn)
    for j in range(10):
        src = q8[:, j, :] if j < 8 else kr[:, j - 8, 0:T]
        m = PE.mm(ps[7][:, 0:T], const("rot"), src, mark=True, after=[V.last, A.last])
        V(tt, rtmp[:, :], ps[7][:, 0:T], const("sin"), ALU.mult, after=[m])
        V(tt, src, src, const("cos"), ALU.mult)
        for p in range(2):
            r = slice(p * HD, (p + 1) * HD)
            dst = qs[:, 2 * j + p, :] if j < 8 else ks[:, 2 * (j - 8) + p, 0:T]
            V(tt, dst, src[r, :], rtmp[r, :], ALU.add)
            if j >= 8:
                V(nc.vector.tensor_copy, ks[:, 2 * (j - 8) + p, T:2 * T], kr[r, j - 8, T:2 * T])
    for kind, dst in ((0, yaT), (1, ygT)):
        phase()
        window = kind == 0
        attn_scope = ExitStack()
        attention(f"w{kind}", 8, 4, lambda h_i: qs[:, 8 * kind + h_i, :], lambda h_i: ks[:, 2 * kind + h_i // 4, :],
                  lambda h_i, kt: vt2[:, kt, kind * P + (h_i // 4) * HD:kind * P + (h_i // 4 + 1) * HD],
                  lambda h_i: dst[(h_i % 2) * HD:(h_i % 2 + 1) * HD, h_i // 2, :], attn_scope, HD ** -0.5,
                  bias=(lambda h_i, ti: const("window")[:, ti * T:(ti + 1) * T]) if window else None,
                  sink=col2("sink") if window else None)
        phase()
        attn_scope.close()
    atn.close()

    bT = sb("bT", [P, 2, T], scope=ssd)
    cT = sb("cT", [P, 2, T], scope=ssd)
    xs = sb("xs", [P, 2, DM], scope=ssd)
    dt = sb("dt", [P, 4, 32], scope=ssd)
    da = sb("da", [P, 4, 32], scope=ssd)
    acs = sb("acs", [P, 4, 32], scope=ssd)
    eac = sb("eac", [P, 4, 32], scope=ssd)
    s2 = ExitStack()
    h0 = sb("h0", [P, 2, DM], scope=ssd)
    xc = sb("xc", [P, 2, DM], scope=s2)
    bc = sb("bc", [P, 2, 2 * P], scope=s2)
    bcT = sb("bcT", [P, 2, T], scope=s2)
    cpad = sb("cpad", [P, 2, 2, T + 2], scope=s2)
    cout = sb("cout", [P, 2, 2, T], scope=s2)
    dtmp = sb("dtmp", [P, 3, 128], scope=s2)
    xw = sb("xw", [P, 2, DM], scope=s2)
    V(nc.vector.memset, cpad[:, :, :, :], 0.0)
    read_pad, read_out = [V.last] * 2, [None] * 2
    fbanks = Banks(ps[4:8])
    banks = Banks(ps[0:4])
    for j in range(12):
        d = j % 2
        if j % 2 == 0:
            w = three(take_unit()[:, :], KT)
        at, bank, read = banks.next()
        m = project(bank, half(w, d), 2 * T, [read])
        if d:
            give_unit()
        t = A(act, cpad[:, d, :, 1:T + 1], three(bank[:, :], 2), ACT.Copy, after=[m, read_pad[d]])
        banks.done(at, t)
        cw = [col2("conv_w")[:, 3 * j + k:3 * j + k + 1] for k in range(3)]
        V(ts, cout[:, d, :, :], cpad[:, d, :, 1:T + 1], cw[1], col2("conv_b")[:, j:j + 1], ALU.mult, ALU.add, after=[t, read_out[d]])
        V(stt, cout[:, d, :, :], cpad[:, d, :, 0:T], cw[0], cout[:, d, :, :], ALU.mult, ALU.add)
        read_pad[d] = V(stt, cout[:, d, :, :], cpad[:, d, :, 2:T + 2], cw[2], cout[:, d, :, :], ALU.mult, ALU.add)
        if j < 8:
            t = A(act, cout[:, d, :, :], cout[:, d, :, :], ACT.Silu, after=[V.last])
            at, bank, read = fbanks.next()
            for ti in range(4):
                m = PE.flip(bank[:, ti * P:(ti + 1) * P], cout[:, d, ti // 2, (ti % 2) * P:(ti % 2 + 1) * P], ident, mark=ti == 3, after=[t, read])
            read_out[d] = m
            A(act, xs[:, :, j * P:(j + 1) * P], three(bank[:, :], 4)[:, 0:2, :], ACT.Copy, after=[m])
            fbanks.done(at, A(act, xc[:, :, j * P:(j + 1) * P], three(bank[:, :], 4)[:, 2:4, :], ACT.Copy))
        elif j < 10:
            A(act, bT[:, j - 8, :], cout[:, d, 0, :], ACT.Silu, after=[V.last])
            t = A(act, bcT[:, j - 8, :], cout[:, d, 1, :], ACT.Silu)
            at, bank, read = fbanks.next()
            for ti in range(2):
                m = PE.flip(bank[:, ti * P:(ti + 1) * P], bcT[:, j - 8, ti * P:(ti + 1) * P], ident, mark=ti == 1, after=[t, read])
            fbanks.done(at, A(act, bc[:, :, (j - 8) * P:(j - 7) * P], three(bank[:, 0:T], 2), ACT.Copy, after=[m]))
            read_out[d] = A.last
        else:
            read_out[d] = A(act, cT[:, j - 10, :], cout[:, d, 0, :], ACT.Silu, after=[V.last])

    w_dt = three(col2("w_dt"), KT)
    at, bank, read = banks.next()
    for ti in range(4):
        for k in range(KT):
            m = PE.mm(bank[:, ti * 32:(ti + 1) * 32], hT[:, k, ti * P:(ti + 1) * P], w_dt[:, k, :], start=k == 0, stop=k == KT - 1,
                      mark=ti == 3 and k == KT - 1, after=[read])
    dt_f = dt[:, :, :].rearrange("p a b -> p (a b)")
    e_, u_, l_ = dtmp[:, 0, :], dtmp[:, 1, :], dtmp[:, 2, :]
    V(tt, dt[:, :, :], three(bank[:, 0:128], 4), wide(col2("dt_bias"), [P, 4, 32]), ALU.add, after=[m])
    t = V(stt, e_, dt_f, -1.0, dt_f, ALU.mult, ALU.max)
    t = A(act, e_, e_, ACT.Exp, scale=-1.0, after=[t])
    V(ts, u_, e_, 2.0, None, ALU.add, after=[t])
    V(nc.vector.reciprocal, u_, u_)
    V(tt, u_, u_, e_, ALU.mult)
    V(tt, e_, u_, u_, ALU.mult)
    V(ts, l_, e_, 1.0 / 15, None, ALU.mult)
    for n in (13, 11, 9, 7, 5, 3):
        V(stt, l_, l_, 1.0 / n, e_, ALU.add, ALU.mult)
    V(stt, l_, l_, 1.0, u_, ALU.add, ALU.mult)
    V(ts, l_, l_, 2.0, None, ALU.mult)
    V(stt, dt_f, dt_f, 0.0, l_, ALU.max, ALU.add)
    acoef = sb("acoef", [P, 32], scope=s2)
    t = A(act, acoef[:, :], col2("a_log"), ACT.Exp)
    t = V(stt, da[:, :, :], dt[:, :, :], -1.0, wide(acoef[:, :], [P, 4, 32]), ALU.mult, ALU.mult, after=[t])
    order = [three(const("fwd"), 2), three(const("bwd"), 2)]
    at, bank, read = banks.next()
    for g in range(2):
        for ti in range(2):
            for d in range(2):
                o = (2 * g + ti) * 32 + d * 16
                for st in range(2):
                    m = PE.mm(bank[:, o:o + 16], order[d][:, st, ti * P:(ti + 1) * P], da[:, 2 * g + st, d * 16:(d + 1) * 16],
                              start=st == 0, stop=st == 1, mark=True, after=[t, read])
    V(nc.vector.tensor_copy, acs[:, :, :], three(bank[:, 0:128], 4), after=[m])
    for st in range(2):
        m = PE.mm(bank[:, 128:160], ones, da[:, 2 + st, :], start=st == 0, stop=st == 1, mark=st == 1, after=[V.last])
    dec = sb("dec", [P, 2, 32], scope=s2)
    for ti in range(2):
        t = V(tt, dec[:, ti, :], bank[:, 128:160], acs[:, 2 + ti, :], ALU.subtract, after=[m])
    A(act, dec[:, :, :], dec[:, :, :], ACT.Exp, after=[t])
    t = A(act, eac[:, :, :], acs[:, :, :], ACT.Exp)
    V(tt, dec[:, :, :], dec[:, :, :], dt[:, 2:4, :], ALU.mult, after=[t])
    for d in range(2):
        for ti in range(2):
            V(tt, three(xw[:, ti, :], 16), three(xc[:, ti, :], 16), dec[:, ti, d * 16:(d + 1) * 16].unsqueeze(2).to_broadcast([P, 16, HD]),
              ALU.mult, after=[PE.last, A.last])
        for g in range(2):
            at, bank, read = banks.next()
            for ti in range(2):
                m = PE.mm(bank[:, :], bc[:, ti, g * P:(g + 1) * P], xw[:, ti, g * 512:(g + 1) * 512], start=ti == 0, stop=ti == 1, mark=ti == 1,
                          after=[read, V.last])
            banks.done(at, A(act, h0[:, d, g * 512:(g + 1) * 512], bank[:, :], ACT.Copy, after=[m]))
    phase()
    s2.close()

    s3_ = ExitStack()
    y = sb("y", [P, 2, DM], scope=ssd)
    cbm = sb("cbm", [P, 2, 2, 2 * T], scope=s3_)
    xdt = sb("xdt", [P, 2, 2, DM], scope=s3_)
    arow = sb("arow", [32, T], scope=s3_)
    lm = sb("lm", [P, 2, 2, T], scope=s3_)
    for g in range(2):
        for st in range(2):
            m = PE.mm(ps[g][:, st * T:(st + 1) * T], bT[:, g, st * P:(st + 1) * P], cT[:, g, :], mark=True)
        for d in range(2):
            V(tt, cbm[:, d, g, :], ps[g][:, :], const("fwd" if d == 0 else "bwd"), ALU.mult, after=[m])
    for d in range(2):
        for ti in range(2):
            V(tt, three(xdt[:, d, ti, :], 16), three(xs[:, ti, :], 16), dt[:, ti, d * 16:(d + 1) * 16].unsqueeze(2).to_broadcast([P, 16, HD]), ALU.mult)
    for ti in range(2):
        V(tt, three(y[:, ti, :], 16), three(xs[:, ti, :], 16), col2("d_skip").unsqueeze(2).to_broadcast([P, 16, HD]), ALU.mult)
    off = sb("off", [P, 512], scope=s3_)
    banks = Banks(ps[2:4])
    for d in range(2):
        for g in range(2):
            for ti in range(2):
                at, bank, read = banks.next()
                m = PE.mm(bank[:, :], cT[:, g, ti * P:(ti + 1) * P], h0[:, d, g * 512:(g + 1) * 512], mark=True, after=[read])
                t = V(tt, three(off[:, :], 8), three(bank[:, :], 8),
                      eac[:, ti, d * 16 + g * 8:d * 16 + (g + 1) * 8].unsqueeze(2).to_broadcast([P, 8, HD]), ALU.mult, after=[m])
                banks.done(at, t)
                V(tt, y[:, ti, g * 512:(g + 1) * 512], y[:, ti, g * 512:(g + 1) * 512], off[:, :], ALU.add)
    m = None
    for d in range(2):
        for st in range(2):
            m = PE.mm(ps[4][0:32, d * T:(d + 1) * T], da[:, st, :], order[d][:, st, :], start=st == 0, stop=st == 1, mark=True)
    arow2 = sb("arow2", [32, 2, T], scope=s3_)
    t_row = V(nc.vector.tensor_copy, arow2[:, :, :], three(ps[4][0:32, :], 2), after=[m])
    banks = Banks(ps[5:7])
    lm_read = [None] * 2
    acc = [ps[0], ps[1], ps[2], ps[3]]
    PE.wait(V.last)
    for b in range(4):
        PE.mm(acc[b][:, :], zeros[:, 0:P], zeros[:, :], start=True, stop=False, group=True)
    queue = []

    def diag(hd):
        d, h_i = divmod(hd, 16)
        b = hd % 2
        at, bank, read = banks.next()
        m = PE.mm(bank[:, 0:T], ident[0:32, hd:hd + 1].to_broadcast([32, P]), arow2[:, d, :], mark=True, after=[read, t_row])
        for st in range(2):
            t = V(ts, lm[:, b, st, :], bank[:, 0:T], acs[:, st, hd:hd + 1], 0.0, ALU.subtract, ALU.min, after=[m, lm_read[b]])
        banks.done(at, t)
        t = A(act, lm[:, b, :, :], lm[:, b, :, :], ACT.Exp, after=[t])
        return V(tt, lm[:, b, :, :], lm[:, b, :, :], three(cbm[:, d, h_i // 8, :], 2), ALU.mult, after=[t])

    def diag_sum(hd, t):
        d, h_i = divmod(hd, 16)
        b = hd % 2
        for ti in range(2):
            tiles = [0] if (d, ti) == (0, 0) else [1] if (d, ti) == (1, 1) else [0, 1]
            for st in tiles:
                m = PE.mm(acc[2 * ti + h_i // 8][:, (h_i % 8) * HD:(h_i % 8 + 1) * HD], lm[:, b, st, ti * P:(ti + 1) * P],
                          xdt[:, d, st, h_i * HD:(h_i + 1) * HD], start=False, stop=hd == 31, group=True,
                          mark=ti == 1 and st == tiles[-1], after=[t])
        lm_read[b] = m

    before = None
    for hd in range(32):
        t = diag(hd)
        if before:
            diag_sum(*before)
        before = (hd, t)
    diag_sum(*before)
    for ti in range(2):
        for g in range(2):
            V(tt, y[:, ti, g * 512:(g + 1) * 512], acc[2 * ti + g][:, :], y[:, ti, g * 512:(g + 1) * 512], ALU.add, after=[PE.last])
    phase()
    s3_.close()
    s4 = ExitStack()
    zs = sb("zs", [P, 2, DM], scope=s4)
    st4 = sb("st4", [P, 4], scope=s4)
    banks = Banks(ps[0:4])
    for u in range(4):
        w = three(take_unit()[:, :], KT)
        for ti in range(2):
            at, bank, read = banks.next()
            for k in range(KT):
                m = PE.mm(bank[:, 0:T], hT[:, k, ti * P:(ti + 1) * P], w[:, k, :], start=k == 0, stop=k == KT - 1, mark=k == KT - 1, after=[read])
            banks.done(at, A(act, zs[:, ti, u * T:(u + 1) * T], bank[:, 0:T], ACT.Silu, after=[m]))
        give_unit()
    V(tt, y[:, :, :], y[:, :, :], zs[:, :, :], ALU.mult, after=[A.last])
    for ti in range(2):
        A(act, zs[:, ti, :], y[:, ti, :], ACT.Square, accum_out=st4[:, ti:ti + 1], after=[V.last])
    t = A(act, st4[:, 2:4], st4[:, 0:2], ACT.Sqrt, bias=EPS6, scale=1.0 / DM)
    V(nc.vector.reciprocal, st4[:, 2:4], st4[:, 2:4], after=[t])
    for ti in range(2):
        t = V(ts, y[:, ti, :], y[:, ti, :], st4[:, 2 + ti:3 + ti], None, ALU.mult)
    banks = Banks(ps[4:8])
    for j in range(KT):
        at, bank, read = banks.next()
        for ti in range(2):
            m = PE.flip(bank[:, ti * P:(ti + 1) * P], y[:, ti, j * P:(j + 1) * P], ident, mark=ti == 1, after=[read, t])
        banks.done(at, V(ts, ysT[:, j, :], bank[:, 0:T], col2("ssm_norm")[:, j:j + 1], None, ALU.mult, after=[m]))
    phase()
    s4.close()
    ssd.close()

    mg = ExitStack()
    gates = sb("gates", [P, 24, T], scope=mg)
    mT = sb("mT", [P, KT, T], scope=mg)
    prod = sb("prod", [P, 2, T], scope=mg)
    banks = Banks(ps[0:2])
    for j in range(24):
        if j % 2 == 0:
            w = three(take_unit()[:, :], KT)
        at, bank, read = banks.next()
        m = project(bank, half(w, j % 2), T, [read])
        banks.done(at, A(act, gates[:, j, :], bank[:, 0:T], ACT.Sigmoid, after=[m]))
        if j % 2:
            give_unit()
    banks = Banks(ps[2:8])
    for hf in range(2):
        w_a, w_c = three(take_unit()[:, :], 4), three(take_unit()[:, :], 4)
        w_b = [three(take_unit()[:, :], KT) for _ in range(2)]
        for mi in range(4):
            m_i = 4 * hf + mi
            o = slice(mi * P, (mi + 1) * P)
            parts = [(w_a[:, :, o], yaT, 4), (w_b[mi // 2][:, :, (mi % 2) * P:(mi % 2 + 1) * P], ysT, KT), (w_c[:, :, o], ygT, 4)]
            for b, (wv, src, nk) in enumerate(parts):
                at, bank, read = banks.next()
                for k in range(nk):
                    m = PE.mm(bank[:, 0:T], wv[:, k, :], src[:, k, :], start=k == 0, stop=k == nk - 1, mark=k == nk - 1, after=[read])
                dst = mT[:, m_i, :] if b == 0 else prod[:, b - 1, :]
                banks.done(at, V(tt, dst, gates[:, b * KT + m_i, :], bank[:, 0:T], ALU.mult, after=[m, A.last]))
                if b:
                    t = V(tt, mT[:, m_i, :], mT[:, m_i, :], dst, ALU.add)
        PE.pending += 4
        PE.flush()
    banks = Banks(ps[0:4])
    PE.wait(A.last)
    for m_i in range(KT):
        if m_i % 2 == 0:
            w = three(take_unit()[:, :], KT)
        at, bank, read = banks.next()
        for k in range(KT):
            m = PE.mm(bank[:, 0:T], w[:, k, (m_i % 2) * P:(m_i % 2 + 1) * P], mT[:, k, :], start=k == 0, stop=k == KT - 1, mark=k == KT - 1,
                      after=[read, t])
        if m_i % 2:
            give_unit()
        banks.done(at, V(stt, xT[:, m_i, :], bank[:, 0:T], gate1[:, m_i:m_i + 1], xT[:, m_i, :], ALU.mult, ALU.add, after=[m]))
    phase()
    mg.close()

    sq9 = sb("sq9", [P, KT, T])
    pad = sb("pad", [P, 2, T + 2])
    csum = sb("csum", [P, 2, T])
    V(nc.vector.memset, pad[:, :, :], 0.0)
    h = rms(xT[:, :, :], hT[:, :, 0:T], scale_2, sq9[:, :, :], shift=shift2, after=[V.last])
    A.wait(V.last)
    done = ffn(h, conv={"pad": pad, "sum": csum, "w": col2("fconv_w"), "b": col2("fconv_b")})
    for m_i in range(KT):
        V(stt, xT[:, m_i, :], ps[2 + m_i // 2][:, (m_i % 2) * T:(m_i % 2 + 1) * T], gate2[:, m_i:m_i + 1], xT[:, m_i, :],
          ALU.mult, ALU.add, after=[done])
    t = rms(xT[:, :, :], hT[:, :, 0:T], col2("final"), sq9[:, :, :], after=[V.last])
    A.wait(t)
    nc.scalar.dma_start(out, hT[:, :, 0:T]).then_inc(s_out, 16)
    nc.scalar.wait_ge(s_out, 16)
    nc.all_engine_barrier()
    ctx.close()


def _cols(v, n=None):
    v = np.asarray(v)
    return np.moveaxis(v.reshape(*v.shape[:-1], -1, P), -1, -2)


def _in_units(w, cols):
    k = w.shape[0] // P
    return w.reshape(k, P, -1, cols).transpose(2, 1, 0, 3).reshape(-1, P, k * cols)


def _ffn_units(g, u, d):
    gu = [_in_units(w, 2 * P) for w in (g, u)]
    dn = d.reshape(FT // 2, 2, P, DM).transpose(0, 2, 1, 3).reshape(FT // 2, P, UNIT)
    return np.stack([*gu, dn], axis=1).reshape(-1, P, UNIT)


def kernel(**inputs):
    import concourse.bacc as _bacc
    from concourse.bass_utils import run_bass_kernel_spmd as _run

    a = {k: np.asarray(v) for k, v in inputs.items()}
    f = np.float32
    w_layers, p_layers = [], []
    for l in range(DEPTH):
        w_in = np.concatenate([a["w_in"][l], np.zeros((DM, P), f)], axis=1)
        w_layers.append(np.concatenate([
            _ffn_units(a["ffn1_w_gate"][l], a["ffn1_w_up"][l], a["ffn1_w_down"][l]),
            _in_units(w_in, 2 * P), _in_units(a["w_out"][l], 2 * P),
            _ffn_units(a["ffn2_w_gate"][l], a["ffn2_w_up"][l], a["ffn2_w_down"][l])]))
        p = np.zeros((P, LP_N), f)

        def put(name, v):
            p[:v.shape[0], slice(*LP[name])] = v

        for n in ("norm_ffn1", "norm_mix", "norm_ffn2"):
            put(n, _cols(a[n][l]))
        put("mu", _cols(a["shift_mu"][l]))
        put("a0", _cols(a["rwkv_a0"][l]))
        put("k_k", _cols(a["rwkv_k_k"][l]))
        put("k_a", _cols(a["rwkv_k_a"][l]))
        put("r_k", _cols(a["rwkv_r_k"][l].reshape(-1)))
        put("ln_w", a["rwkv_ln_w"][l].reshape(NH, HD).T)
        put("ln_b", a["rwkv_ln_b"][l].reshape(NH, HD).T)
        put("qn", np.tile(a["attn_q_norm"][l], 2)[:, None])
        put("kn", np.tile(a["attn_k_norm"][l], 2)[:, None])
        put("conv_w", a["conv_dw_w"][l].reshape(TAPS, 2, P).transpose(2, 1, 0).reshape(P, 2 * TAPS))
        put("conv_b", _cols(a["conv_dw_b"][l]))
        put("cln_w", _cols(a["conv_ln_w"][l]))
        put("cln_b", _cols(a["conv_ln_b"][l]))
        put("lora", np.concatenate([a["rwkv_w2"][l], a["rwkv_a2"][l], a["rwkv_g2"][l]], axis=0))
        put("w0", np.broadcast_to(a["rwkv_w0"][l], (P, NH * HD)))
        p_layers.append(p)
    w_layers, p_layers = np.stack(w_layers), np.stack(p_layers)

    b = {k[:-2]: (v[0] if v.ndim > 1 and k not in ("c_2", "ctx_2") else v) for k, v in a.items() if k.endswith("_2")}
    w2 = b["w_in"]
    at, span = 0, {}
    for n, width in (("a_q", 512), ("a_k", 128), ("a_v", 128), ("z", 1024), ("xbc", 1536), ("dt", 32), ("c_q", 512),
                     ("c_k", 128), ("c_v", 128), ("gates", 3072)):
        span[n] = w2[:, at:at + width]
        at += width
    pair = lambda x, y: _in_units(np.concatenate([span[x], span[y]], axis=1), 2 * P)
    oa, oc, ob = _in_units(b["w_oa"], 512), _in_units(b["w_oc"], 512), _in_units(b["w_ob"], 2 * P)
    w_last = np.concatenate([
        _in_units(b["w_mod"], 2 * P), pair("a_k", "c_k"), pair("a_v", "c_v"), _in_units(span["a_q"], 2 * P),
        _in_units(span["c_q"], 2 * P), _in_units(span["xbc"], 2 * P), _in_units(span["z"], 2 * P),
        _in_units(span["gates"], 2 * P), oa[0:1], oc[0:1], ob[0:2], oa[1:2], oc[1:2], ob[2:4],
        _in_units(b["w_out"], 2 * P), _ffn_units(b["ffn_w_gate"], b["ffn_w_up"], b["ffn_w_down"])])
    p = np.zeros((P, SP2_N), f)

    def put2(name, v):
        p[:, slice(*SP2[name])] = v

    put2("c", np.stack([_cols(b["c"].reshape(-1)), _cols(b["c_ctx"])], axis=2).reshape(P, 16))
    put2("b_mod", _cols(b["b_mod"]))
    put2("norm1", _cols(b["norm1"]))
    put2("norm2", _cols(b["norm2"]))
    put2("final", _cols(b["final_norm"]))
    put2("conv_w", b["ssm_conv_w"].reshape(3, 12, P).transpose(2, 1, 0).reshape(P, 36))
    put2("conv_b", _cols(b["ssm_conv_b"]))
    put2("a_log", np.broadcast_to(b["ssm_A_log"].reshape(1, 32), (P, 32)))
    put2("dt_bias", np.broadcast_to(b["ssm_dt_bias"].reshape(1, 32), (P, 32)))
    put2("d_skip", np.broadcast_to(b["ssm_D"].reshape(1, 16), (P, 16)))
    put2("ssm_norm", _cols(b["ssm_norm"]))
    put2("qn", np.tile(b["c_q_norm"], 2)[:, None])
    put2("kn", np.tile(b["c_k_norm"], 2)[:, None])
    put2("sink", np.broadcast_to(b["a_sink"].reshape(1, 8), (P, 8)))
    put2("fconv_w", b["ffn_conv_w"].reshape(3, FT, P).transpose(2, 1, 0).reshape(P, 3 * FT))
    put2("fconv_b", _cols(b["ffn_conv_b"]))
    put2("w_dt", span["dt"].reshape(KT, P, 32).transpose(1, 0, 2).reshape(P, KT * 32))
    c0, cl, cs = constants()

    def chan(x):
        return x.reshape(T, KT, P).transpose(2, 1, 0)

    arrays = {"xT": chan(a["x"]), "ctxT": chan(b["ctx"]), "w_layers": w_layers, "w_last": w_last, "p_layers": p_layers,
              "p_last": p, "c0": c0, "cl": cl, "cs": cs}
    arrays = {k: np.ascontiguousarray(v) for k, v in arrays.items()}
    nc = _bacc.Bacc("TRN2", target_bir_lowering=False, num_devices=1)
    args = [nc.dram_tensor("in_" + k, v.shape, F32, kind="ExternalInput").ap() for k, v in arrays.items()]
    out = nc.dram_tensor("out_x", (P, KT, T), F32, kind="ExternalOutput").ap()
    build(nc, *args, out)
    r = _run(nc, [{"in_" + k: v for k, v in arrays.items()}], core_ids=[0])
    return np.ascontiguousarray(r.results[0]["out_x"].transpose(2, 1, 0)).reshape(1, T, DM)
```

```python
import math
from contextlib import ExitStack

import numpy as np

import concourse.bass as bass
import concourse.mybir as mybir
from concourse.alu_op_type import AluOpType as ALU

F32 = mybir.dt.float32
BF16 = mybir.dt.bfloat16
F32R = mybir.dt.float32r
ACT = mybir.ActivationFunctionType
AX = mybir.AxisListType

P = 128
T = 256
DM = 1024
KT = DM // P
FF = 2816
FT = FF // P
DEPTH = 2
HD = 64
NH = 6
JT = NH * HD // P
CH = 64
NC = T // CH
NPROB = 2 * NH
TAPS = 31
UNIT = 2048
SLOTS = 6
LAYER_UNITS = 3 * FT // 2 + 12 + 4 + 3 * FT // 2
LAST_UNITS = 24 + 28 + 8 + 4 + 3 * FT // 2
NEG = -1.0e30

def _columns(sizes):
    at, out = 0, {}
    for name, n in sizes:
        out[name] = (at, at + n)
        at += n
    return out, at

LP, LP_N = _columns([("norm_ffn1", KT), ("norm_mix", KT), ("norm_ffn2", KT), ("mu", 10), ("a0", JT),
                     ("k_k", JT), ("k_a", JT), ("r_k", JT), ("ln_w", NH), ("ln_b", NH), ("qn", 1), ("kn", 1),
                     ("conv_w", 2 * TAPS), ("conv_b", 2), ("cln_w", 2), ("cln_b", 2), ("lora", NH * HD),
                     ("w0", NH * HD)])
SP2, SP2_N = _columns([("c", 16), ("b_mod", 48), ("norm1", KT), ("norm2", KT), ("final", KT), ("conv_w", 36),
                       ("conv_b", 12), ("a_log", 32), ("dt_bias", 32), ("d_skip", 16), ("ssm_norm", KT),
                       ("qn", 1), ("kn", 1), ("sink", 8), ("fconv_w", 3 * FT), ("fconv_b", FT),
                       ("w_dt", KT * 32)])
C0, C0_N = _columns([("ident", P), ("heads", P), ("ones", P)])
CL, CL_N = _columns([("cum", 2 * P), ("strict", P), ("incl", P), ("level", 6 * P), ("first", P),
                     ("bias", NH * 2 * T)])
CS, CS_N = _columns([("window", 2 * T), ("cos", T), ("sin", T), ("rot", P), ("fwd", 2 * T), ("bwd", 2 * T)])


def _slopes(n):
    def pow2(m):
        start = 2.0 ** (-8.0 / m)
        return [start ** (i + 1) for i in range(m)]
    c = 2 ** int(math.floor(math.log2(n)))
    return pow2(n) if c == n else pow2(c) + pow2(2 * c)[0::2][: n - c]


def constants():
    c0 = np.zeros((P, C0_N), np.float32)
    i = np.arange(P)
    c0[:, slice(*C0["ident"])] = np.eye(P)
    c0[:, slice(*C0["heads"])] = i[:, None] // HD == i[None] // HD
    c0[:, slice(*C0["ones"])] = 1.0
    cl = np.zeros((P, CL_N), np.float32)
    same = i[:, None] // CH == i[None] // CH
    a, b = CL["cum"]
    cl[:, a:a + P] = -math.exp(-0.5) * (same & (i[:, None] <= i[None]))
    cl[:, a + P:b] = -math.exp(-0.5) * (same & (i[:, None] < i[None]))
    r, c = i[:, None], i[None]
    cl[:, slice(*CL["strict"])] = same & (r < c)
    cl[:, slice(*CL["incl"])] = same & (r <= c)
    for k in range(6):
        w = 1 << k
        m = (r // (2 * w) == c // (2 * w)) & (r // w % 2 == 1) & (c // w % 2 == 0)
        cl[:, CL["level"][0] + k * P:CL["level"][0] + (k + 1) * P] = m
        if k == 0:
            cl[:, slice(*CL["first"])] = m.T
    t = np.arange(T)
    dist = t[:, None] - t[None]
    count = (((dist >= 0) & (dist <= 128)).astype(int) + ((dist >= 0) & (dist % 4 == 0))
             + ((dist >= 0) & (dist % 16 == 0)))
    for h, slope in enumerate(_slopes(NH)):
        full = np.where(count > 0, -slope * dist + np.log(np.maximum(count, 1)), NEG)
        a = CL["bias"][0] + h * 2 * T
        cl[:, a:a + 2 * T] = full.reshape(2, P, T).transpose(1, 0, 2).reshape(P, 2 * T)
    cs = np.zeros((P, CS_N), np.float32)
    cs[:, slice(*CS["window"])] = np.where(np.abs(dist) <= 128, 0.0, NEG).reshape(2, P, T).transpose(1, 0, 2).reshape(P, -1)
    n = HD // 4
    inv = (np.float32(10000.0) ** (-np.arange(n, dtype=np.float32) / n)).astype(np.float32)
    ang = np.concatenate([(t // 64)[:, None] * inv, (t % 64)[:, None] * inv], axis=-1).astype(np.float32)
    pair = (i % HD) // 2
    cs[:, slice(*CS["cos"])] = np.cos(ang).T[pair]
    cs[:, slice(*CS["sin"])] = np.sin(ang).T[pair]
    rot = np.zeros((P, P))
    rot[i[0::2] + 1, i[0::2]] = -1.0
    rot[i[0::2], i[0::2] + 1] = 1.0
    cs[:, slice(*CS["rot"])] = rot
    for name, m in (("fwd", t[:, None] <= t[None]), ("bwd", t[:, None] >= t[None])):
        cs[:, slice(*CS[name])] = m.reshape(2, P, T).transpose(1, 0, 2).reshape(P, -1)
    return c0, cl, cs


class Engine:

    def __init__(self, eng, sem):
        self.eng, self.sem = eng, sem
        self.restart()

    def restart(self):
        self.n, self.seen = 0, {}

    @property
    def last(self):
        return (self.sem, self.n)

    def wait(self, *results):
        for r in results:
            if r is None or r[1] == 0:
                continue
            if self.seen.get(r[0].num, 0) < r[1]:
                self.eng.wait_ge(r[0], r[1])
                self.seen[r[0].num] = r[1]

    def __call__(self, op, *args, after=(), **kw):
        self.wait(self.last, *after)
        op(*args, **kw).then_inc(self.sem, 1)
        self.n += 1
        return self.last


class Tensor(Engine):

    def restart(self):
        self.n, self.seen, self.pending = 0, {}, 0

    def mm(self, out, lhsT, rhs, start=True, stop=True, mark=False, sem=None, after=(), group=False):
        self.wait(*after)
        ins = self.eng.matmul(out, lhsT, rhs, start=start, stop=stop, skip_group_check=group)
        return self._count(ins, mark, sem)

    def flip(self, out, in_, ident, mark=False, after=()):
        self.wait(*after)
        return self._count(self.eng.transpose(out, in_, ident), mark, None)

    def _count(self, ins, mark, sem):
        if mark:
            ins.then_inc(self.sem, 1)
            self.n += 1
        elif sem is not None:
            ins.then_inc(sem, 1)
        elif self.pending:
            ins.then_inc(self.free, self.pending)
            self.pending = 0
        return self.last

    def flush(self):
        if self.pending:
            self.eng.drain().then_inc(self.free, self.pending)
        self.pending = 0

    def fence(self):
        self.eng.drain().then_inc(self.sem, 1)
        self.n += 1
        return self.last


class Banks:

    def __init__(self, bufs):
        self.bufs, self.read, self.at = list(bufs), [None] * len(bufs), -1

    def next(self):
        self.at = (self.at + 1) % len(self.bufs)
        return self.at, self.bufs[self.at], self.read[self.at]

    def done(self, at, result):
        self.read[at] = result


def build(nc, xT_in, ctxT_in, w_layers, w_last, p_layers, p_last, c0_in, cl_in, cs_in, out):
    ctx = ExitStack()

    def sb(name, shape, dt=F32, scope=None):
        return (scope or ctx).enter_context(nc.sbuf_tensor(name, shape, dt))

    def sem(name):
        return ctx.enter_context(nc.semaphore(name))

    s_pe, s_act_e, s_dve, s_pool = sem("s_pe"), sem("s_act_e"), sem("s_dve"), sem("s_pool")
    s_free = sem("s_free")
    s_slot = [sem(f"s_slot{k}") for k in range(SLOTS)]
    s_gu = sem("s_gu")
    s_sg = sem("s_sg")
    s_hid = sem("s_hid")
    s_cv = sem("s_cv")
    s_hi = sem("s_hi")
    s_lo = sem("s_lo")
    s_ch = sem("s_ch")
    s_in = sem("s_in")
    s_out = sem("s_out")
    every_sem = [s_pe, s_act_e, s_dve, s_pool, s_free, *s_slot, s_gu, s_sg, s_hid, s_cv, s_hi, s_lo, s_ch, s_in]

    PE, A, V, G = Tensor(nc.tensor, s_pe), Engine(nc.scalar, s_act_e), Engine(nc.vector, s_dve), Engine(nc.gpsimd, s_pool)
    PE.free = s_free
    ring = [sb(f"ring{k}", [P, UNIT]) for k in range(SLOTS)]
    ps = [ctx.enter_context(nc.psum_tensor(f"ps{k}", [P, 512], F32)) for k in range(8)]
    xT = sb("xT", [P, KT, T])
    hT = sb("hT", [P, KT, 2 * T])
    c0 = sb("c0", [P, C0_N])
    rstd = sb("rstd", [P, T])
    zeros = sb("zeros", [P, 512], BF16)
    eps = sb("eps", [P, 5])
    EPS6, EPS12, EPSG, EPSC, ONE = (eps[:, k:k + 1] for k in range(5))
    ident, heads, ones = (c0[:, slice(*C0[k])] for k in ("ident", "heads", "ones"))

    tt, ts, stt = nc.vector.tensor_tensor, nc.vector.tensor_scalar, nc.vector.scalar_tensor_tensor
    act = nc.scalar.activation
    load_n = [0]

    def load(dst, src):
        nc.scalar.dma_start(dst, src).then_inc(s_in, 16)
        load_n[0] += 16
        return (s_in, load_n[0])

    def phase():
        PE.fence()
        for e in (PE, A, V, G):
            e.wait(PE.last, A.last, V.last, G.last)

    def three(ap, n):
        return ap.rearrange("p (a b) -> p a b", a=n)

    def wide(ap, shape):
        return ap.unsqueeze(1).to_broadcast(shape)

    def stream(units, source):
        trips = units // SLOTS
        with nc.sync.Fori(0, trips) as i:
            for k in range(SLOTS):
                nc.sync.wait_ge(s_free, i * SLOTS + (k + 1))
                nc.sync.dma_start(ring[k][:, :], source(i * SLOTS + k)).then_inc(s_slot[k], 16)
        for u in range(trips * SLOTS, units):
            nc.sync.wait_ge(s_free, u + 1)
            nc.sync.dma_start(ring[u % SLOTS][:, :], source(u)).then_inc(s_slot[u % SLOTS], 16)

    unit_at = [0]

    def take_unit():
        u = unit_at[0]
        unit_at[0] += 1
        nc.tensor.wait_ge(s_slot[u % SLOTS], 16 * (u // SLOTS + 1))
        return ring[u % SLOTS]

    def give_unit():
        PE.pending += 1

    def rms(src, dst, g, square, shift=None, after=()):
        t = A(act, square, src, ACT.Square, after=after)
        for k in range(KT):
            m = PE.mm(ps[7][:, 0:T], ones, square[:, k, :], start=k == 0, stop=k == KT - 1, mark=k == KT - 1, after=[t, V.last])
        t = A(act, rstd[:, :], ps[7][:, 0:T], ACT.Sqrt, bias=EPS6, scale=1.0 / DM, after=[m, V.last])
        V(nc.vector.reciprocal, rstd[:, :], rstd[:, :], after=[t])
        for k in range(KT):
            t = V(stt, dst[:, k, :], src[:, k, :], g[:, k:k + 1], rstd[:, :], ALU.mult, ALU.mult)
            if shift is not None:
                t = V(ts, dst[:, k, :], dst[:, k, :], shift[:, k:k + 1], None, ALU.add)
        return t

    ffn_at = [0]
    SPLITS = 3 * FT

    def split_h(h_ready, hh, hl):
        for k in range(KT):
            t = A(act, hh[:, k, :], hT[:, k, 0:T], ACT.Copy, after=[h_ready])
            V(tt, hl[:, k, :], hT[:, k, 0:T], hh[:, k, :].bitcast(F32), ALU.subtract, after=[t])
        return V.last

    def ffn(tag, h_ready, conv=None):
        scope = ExitStack()
        hh, hl = (sb(f"{n}_{tag}", [P, KT, T], F32R, scope) for n in ("h_hi", "h_lo"))
        wh, wl = (sb(f"{n}_{tag}", [P, 2, 2, KT, P], F32R, scope) for n in ("gu_hi", "gu_lo"))
        dh, dl = (sb(f"{n}_{tag}", [P, 4, DM], F32R, scope) for n in ("down_hi", "down_lo"))
        sg, hid = (sb(f"{n}_{tag}", [P, 2, T], F32, scope) for n in ("silu", "hid"))
        xh, xl = (sb(f"{n}_{tag}", [P, 2, T], F32R, scope) for n in ("hid_hi", "hid_lo"))
        u0, base = unit_at[0], ffn_at[0] * FT
        sbase, cbase = ffn_at[0] * SPLITS, ffn_at[0] * 2 * FT
        unit_at[0] += 3 * FT // 2
        ffn_at[0] += 1
        nc_t = nc.tensor
        PE.flush()
        PE.wait(split_h(h_ready, hh, hl))
        for b in range(4):
            PE.mm(ps[2 + b][:, :], zeros[:, 0:P], zeros[:, :], start=True, stop=False, group=True)

        def number(kind, c):
            if kind == 2:
                return 3 * c + 5 if c < FT - 1 else SPLITS
            return 3 * c + kind if c else 1 + kind

        def parts(kind, c):
            raw = ring[(u0 + 3 * (c // 2) + kind) % SLOTS]
            if kind == 2:
                return three(raw[:, :], 2)[:, c % 2, :], dh[:, c % 4, :], dl[:, c % 4, :]
            return three(raw[:, :], KT)[:, :, (c % 2) * P:(c % 2 + 1) * P], wh[:, c % 2, kind, :, :], wl[:, c % 2, kind, :, :]

        def round_part(kind, c, i):
            src, hi, _ = parts(kind, c)
            if c % 2 == 0:
                u = u0 + 3 * (c // 2) + kind
                nc.scalar.wait_ge(s_slot[u % SLOTS], i * 16 + 16 * (u // SLOTS + 1))
            act(hi, src, ACT.Copy).then_inc(s_hi, 1)

        def rest_part(kind, c, i):
            src, hi, lo = parts(kind, c)
            nc.vector.wait_ge(s_hi, i * 12 + (sbase + number(kind, c)))
            tt(lo, src, hi.bitcast(F32), ALU.subtract).then_inc(s_lo, 1)
            if c % 2 and kind:
                nc.vector.drain().then_inc(s_free, 2 if kind == 1 else 1)

        def passes(hi, lo, xhi, xlo):
            return (hi, xhi), (hi, xlo), (lo, xhi)

        def gate_up(c, i):
            nc_t.wait_ge(s_hid, i * 4 + (base + c + 1))
            nc_t.wait_ge(s_lo, i * 12 + (sbase + number(1, c)))
            for kind in range(2):
                for k in range(KT):
                    for n, (w, x) in enumerate(passes(wh[:, c % 2, kind, k, :], wl[:, c % 2, kind, k, :], hh[:, k, :], hl[:, k, :])):
                        last = k == KT - 1 and n == 2
                        PE.mm(ps[c % 2][:, kind * T:(kind + 1) * T], w, x, start=k == 0 and n == 0, stop=last,
                              sem=s_gu if last and kind == 1 else None)

        def down(c, i, last_tile=False):
            nc_t.wait_ge(s_lo, i * 12 + (sbase + number(2, c)))
            nc_t.wait_ge(s_hid, i * 4 + (base + c + 3))
            for m in range(KT):
                o = slice(m * P, (m + 1) * P)
                for n, (w, x) in enumerate(passes(dh[:, c % 4, o], dl[:, c % 4, o], xh[:, c % 2, :], xl[:, c % 2, :])):
                    PE.mm(ps[2 + m // 2][:, (m % 2) * T:(m % 2 + 1) * T], w, x,
                          start=False, stop=last_tile, group=True, mark=last_tile and m == KT - 1 and n == 2)

        gate_up(0, 0)
        trips = (FT - 1) // 4
        with nc_t.Fori(0, trips) as i:
            for c in range(4):
                gate_up(c + 1, i)
                down(c, i)
        for c in range(4 * trips, FT):
            if c + 1 < FT:
                gate_up(c + 1, 0)
            down(c, 0, c == FT - 1)

        def silu_tile(c, i):
            nc.scalar.wait_ge(s_gu, i * 4 + (base + c + 1))
            if conv is None:
                act(sg[:, c % 2, :], ps[c % 2][:, 0:T], ACT.Silu).then_inc(s_sg, 1)
                return
            act(conv["pad"][:, c % 2, 1:T + 1], ps[c % 2][:, 0:T], ACT.Copy).then_inc(s_sg, 1)
            nc.scalar.wait_ge(s_cv, i * 12 + (3 * c + 3))
            act(sg[:, c % 2, :], conv["sum"][:, c % 2, :], ACT.Silu).then_inc(s_sg, 1)

        def conv_tile(c, i):
            n = i * 4 + c
            pad, total = conv["pad"][:, c % 2, :], conv["sum"][:, c % 2, :]
            w = [conv["w"][:, bass.ds(n * 3 + k, 1)] for k in range(3)]
            nc.vector.wait_ge(s_sg, i * 8 + (2 * c + 1))
            ts(total, pad[:, 1:T + 1], w[1], conv["b"][:, bass.ds(n, 1)], ALU.mult, ALU.add).then_inc(s_cv, 1)
            for k in (0, 2):
                nc.vector.wait_ge(s_cv, i * 12 + (3 * c + 1 + k // 2))
                stt(total, pad[:, k:k + T], w[k], total, ALU.mult, ALU.add).then_inc(s_cv, 1)

        def hidden_tile(c, i):
            if conv is None:
                nc.vector.wait_ge(s_sg, i * 4 + (base + c + 1))
            else:
                conv_tile(c, i)
                nc.vector.wait_ge(s_sg, i * 8 + (2 * c + 2))
            tt(hid[:, c % 2, :], sg[:, c % 2, :], ps[c % 2][:, T:2 * T], ALU.mult).then_inc(s_ch, 1)
            nc.vector.wait_ge(s_ch, i * 8 + (cbase + 2 * c + 1))
            nc.vector.tensor_copy(xh[:, c % 2, :], hid[:, c % 2, :]).then_inc(s_ch, 1)
            nc.vector.wait_ge(s_ch, i * 8 + (cbase + 2 * c + 2))
            tt(xl[:, c % 2, :], hid[:, c % 2, :], xh[:, c % 2, :].bitcast(F32), ALU.subtract).then_inc(s_hid, 1)

        for eng, step, split in ((nc.scalar, silu_tile, round_part), (nc.vector, hidden_tile, rest_part)):
            for kind, c in ((0, 0), (1, 0), (0, 1), (1, 1), (2, 0)):
                split(kind, c, 0)
            with eng.Fori(0, trips) as i:
                for c in range(4):
                    step(c, i)
                    for kind, ahead in ((0, 2), (1, 2), (2, 1)):
                        split(kind, c + ahead, i)
            step(FT - 2, 0)
            split(2, FT - 1, 0)
            step(FT - 1, 0)
        return PE.last, scope

    def start_engines():
        for e in (PE, A, V, G):
            e.restart()
        unit_at[0] = ffn_at[0] = load_n[0] = 0
        nc.tensor.sem_inc(s_free, SLOTS)
        nc.vector.sem_inc(s_hid, 2)

    def end_stretch():
        nc.all_engine_barrier()
        for s in every_sem:
            nc.gpsimd.sem_clear(s)
        nc.all_engine_barrier()

    def first_steps(stream, n):
        for _ in range(n):
            if next(stream, "end") == "end":
                return
            yield

    def interleave(*streams):
        live = [list(x) for x in streams]
        while live:
            for x in list(live):
                for _ in range(x[1]):
                    if next(x[0], "end") == "end":
                        live.remove(x)
                        break

    def attention(tag, nheads, kt_n, q, k, v, store, scope, scale, score_banks, flip_banks, out_bank, bias=None,
                  sink=None, ready=()):
        width = kt_n * P
        nb = width // T
        pr = sb(f"prob_{tag}", [P, 2, 2, width], scope=scope)
        pT = sb(f"probT_{tag}", [P, 1, kt_n, T], scope=scope)
        st = sb(f"stat_{tag}", [P, 2, 8], scope=scope)
        sets = len(score_banks) // nb
        score_read, flip_read, out_read = [None] * sets, None, None
        prob_read, pT_read, sm = [None] * 2, None, [None] * 2

        def scores(h):
            d, d2 = h % 2, h % sets

            def bank(ti):
                b = score_banks[nb * d2 + (ti if nb == 2 else 0)]
                return b[:, 0:width] if nb == 2 else b[:, ti * width:(ti + 1) * width]

            for ti in range(2):
                m = PE.mm(bank(ti), q(h)[:, ti * P:(ti + 1) * P], k(h), mark=True, after=[score_read[d2], *ready])
            for ti in range(2):
                s = pr[:, d, ti, :]
                b = bias(h, ti) if bias else None
                if b is not None:
                    n = b.shape[-1]
                    V(stt, s[:, 0:n], bank(ti)[:, 0:n], scale, b, ALU.mult, ALU.add, after=[m, prob_read[d]])
                    if n < width:
                        V(ts, s[:, n:width], bank(ti)[:, n:width], scale, None, ALU.mult)
                else:
                    V(ts, s, bank(ti), scale, None, ALU.mult, after=[m, prob_read[d]])
            score_read[d2] = V.last
            yield
            mx, neg, total, e_sink = (st[:, d, 2 * k2:2 * k2 + 2] for k2 in range(4))
            V(nc.vector.tensor_reduce, mx, pr[:, d, :, :], AX.X, ALU.max)
            if sink is not None:
                V(ts, mx, mx, sink[:, h:h + 1], None, ALU.max)
            t = V(ts, neg, mx, -1.0, None, ALU.mult)
            for ti in range(2):
                e = A(act, pr[:, d, ti, :], pr[:, d, ti, :], ACT.Exp, bias=neg[:, ti:ti + 1], accum_out=total[:, ti:ti + 1], after=[t])
            if sink is not None:
                e = A(act, e_sink, neg, ACT.Exp, bias=sink[:, h:h + 1])
            yield
            if sink is not None:
                V(tt, total, total, e_sink, ALU.add, after=[e])
            V(nc.vector.reciprocal, total, total, after=[e])
            for ti in range(2):
                sm[d] = V(ts, pr[:, d, ti, :], pr[:, d, ti, :], total[:, ti:ti + 1], None, ALU.mult)

        def finish(h):
            nonlocal flip_read, pT_read, out_read
            d = h % 2
            for kt in range(kt_n):
                bank = flip_banks[kt // 2]
                for ti in range(2):
                    m = PE.flip(bank[:, (kt % 2) * T + ti * P:(kt % 2) * T + (ti + 1) * P], pr[:, d, ti, kt * P:(kt + 1) * P],
                                ident, mark=True, after=[sm[d], flip_read])
            prob_read[d] = m
            yield
            for b in range(kt_n // 2):
                c = A(act, pT[:, 0, 2 * b:2 * b + 2, :], three(flip_banks[b][:, :], 2), ACT.Copy, after=[m, pT_read])
            flip_read = c
            yield
            o = out_bank[0:HD, 0:T]
            for kt in range(kt_n):
                m = PE.mm(o, v(h, kt), pT[:, 0, kt, :], start=kt == 0, stop=kt == kt_n - 1, mark=kt == kt_n - 1,
                          after=[c, out_read])
            pT_read = m
            out_read = A(act, store(h), o, ACT.Copy, after=[m])

        for h in range(nheads + 1):
            if h < nheads:
                yield from scores(h)
                yield
            if h > 0:
                yield from finish(h - 1)
                yield

    for c, v in enumerate((1e-6, 1e-12, 64e-5, 1e-5, 1.0)):
        V(nc.vector.memset, eps[:, c:c + 1], v)
    V(nc.vector.memset, zeros[:, :], 0.0)
    load(c0[:, :], c0_in)
    load(xT[:, :, :], xT_in)
    nc.scalar.wait_ge(s_in, 32)
    end_stretch()

    with nc.Fori(0, DEPTH) as layer:
        start_engines()
        lay = ExitStack()
        pl = sb("pl", [P, LP_N], scope=lay)
        mixT = sb("mixT", [P, KT, T], scope=lay)
        t_pl = load(pl[:, :], p_layers[layer, :, :])
        stream(LAYER_UNITS, lambda u: w_layers[layer, u, :, :])
        for e in (V, PE, A):
            e.wait(t_pl)

        def col(name):
            return pl[:, slice(*LP[name])]

        def half_residual(ran):
            done, scope = ran
            for b in range(4):
                t = V(stt, xT[:, 2 * b:2 * b + 2, :], three(ps[2 + b][:, :], 2), 0.5, xT[:, 2 * b:2 * b + 2, :], ALU.mult, ALU.add, after=[done])
            phase()
            scope.close()
            return t

        h = rms(xT[:, :, :], hT[:, :, 0:T], col("norm_ffn1"), hT[:, :, T:2 * T])
        h = half_residual(ffn('ffn1', h))

        h = rms(xT[:, :, :], hT[:, :, 0:T], col("norm_mix"), hT[:, :, T:2 * T])
        mix = ExitStack()
        rkv = sb("rkv", [P, 10, T], scope=mix)
        cr = sb("cr", [P, CL["bias"][0]], scope=mix)
        arh = sb("arh", [HD, NH, 2, 2, P], scope=mix)
        bh = sb("bh", [HD, NH, T], scope=mix)
        kh2 = sb("kh2", [HD, NH, T], scope=mix)
        dch = sb("dch", [HD, NH, NC], scope=mix)
        bonus = sb("bonus", [P, JT, T], scope=mix)
        gate = sb("gate", [P, JT, T], scope=mix)
        m1 = ExitStack()
        bias_sb = sb("bias_sb", [P, NH * 2 * T], scope=m1)
        load(cr[:, :], cl_in[:, 0:CL["bias"][0]])
        t_bias = t_cr = load(bias_sb[:, :], cl_in[:, slice(*CL["bias"])])
        raw = sb("raw", [P, 3, T + 1], scope=m1)
        qk = sb("qk", [P, 2 * JT, T], scope=m1)
        vtok = sb("vtok", [P, 2, NH * HD], scope=m1)
        cz = sb("cz", [P, 2, TAPS - 1 + T], scope=m1)
        cu = sb("cu", [P, 2, T], scope=m1)
        cc = sb("cc", [P, 2, T], scope=m1)
        csq = sb("csq", [P, 2, T], scope=m1)
        qh = hT[0:HD, 0:NH, T:2 * T]
        kh = sb("kh", [HD, NH, T], scope=m1)
        rq = sb("rq", [P, JT, T], scope=m1)
        lo = sb("lo", [P, T], scope=m1)
        sgw = sb("sgw", [P, 2, NH * HD], scope=m1)
        d_in = sb("d_in", [P, JT, T], scope=m1)
        d_ex = sb("d_ex", [P, JT, T], scope=m1)
        d_inv = sb("d_inv", [P, JT, T], scope=m1)
        aT = sb("aT", [P, JT, T], scope=m1)
        kk = sb("kk", [P, JT, T], scope=m1)
        knew = sb("knew", [P, JT, T], scope=m1)
        tmp = rq
        V(nc.vector.memset, raw[:, :, 0:1], 0.0)
        V(nc.vector.memset, cz[:, :, 0:TAPS - 1], 0.0)
        w_at = {}

        def columns(tile):
            if tile // 2 not in w_at:
                w_at[tile // 2] = take_unit()
            return three(w_at[tile // 2][:, :], KT)[:, :, (tile % 2) * P:(tile % 2 + 1) * P]

        proj = {}
        mu = col("mu")

        def project_tiles():
            banks = Banks(ps[0:2])
            raw_read = [None] * 3
            for tile in range(23):
                w = columns(tile)
                at, bank, read = banks.next()
                if 16 <= tile < 19:
                    for ti in range(2):
                        for k in range(KT):
                            m = PE.mm(bank[:, ti * T:ti * T + P], hT[:, k, ti * P:(ti + 1) * P], w[:, k, :],
                                      start=k == 0, stop=k == KT - 1, mark=ti == 1 and k == KT - 1, after=[read, h])
                    t = A(act, vtok[:, :, (tile - 16) * P:(tile - 15) * P], three(bank[:, :], 2)[:, :, 0:P], ACT.Copy, after=[m])
                else:
                    for k in range(KT):
                        m = PE.mm(bank[:, 0:T], w[:, k, :], hT[:, k, 0:T], start=k == 0, stop=k == KT - 1, mark=k == KT - 1,
                                  after=[read, h])
                    if tile < 10:
                        b = tile % 3
                        t = A(act, raw[:, b, 1:T + 1], bank[:, 0:T], ACT.Copy, after=[m, raw_read[b]])
                        V(tt, rkv[:, tile, :], raw[:, b, 0:T], raw[:, b, 1:T + 1], ALU.subtract, after=[t])
                        raw_read[b] = V(stt, rkv[:, tile, :], rkv[:, tile, :], mu[:, tile:tile + 1], raw[:, b, 1:T + 1], ALU.mult, ALU.add)
                    elif tile < 16:
                        t = A(act, qk[:, tile - 10, :], bank[:, 0:T], ACT.Copy, after=[m])
                    elif tile < 21:
                        t = A(act, cu[:, tile - 19, :], bank[:, 0:T], ACT.Copy, after=[m])
                    else:
                        t = A(act, cz[:, tile - 21, TAPS - 1:TAPS - 1 + T], bank[:, 0:T], ACT.Sigmoid, after=[m])
                banks.done(at, t)
                proj[tile] = raw_read[tile % 3] if tile < 10 else t
                if tile % 2 or tile == 22:
                    give_unit()
                yield

        small = Banks(ps[6:8])

        def attend():
            for which, dst, g in ((0, qh, "qn"), (1, kh, "kn")):
                src = qk[:, which * JT:(which + 1) * JT, :]
                sq = A(act, prn, src, ACT.Square, after=[proj[15], t_norm[0]])
                for j in range(JT):
                    at, bank, read = small.next()
                    m = PE.mm(bank[:, 0:T], heads, prn[:, j, :], mark=True, after=[sq, read])
                    t = A(act, prn[:, j, :], bank[:, 0:T], ACT.Sqrt, bias=EPS6, scale=1.0 / HD, after=[m])
                    small.done(at, t)
                    yield
                V(nc.vector.reciprocal, prn, prn, after=[t])
                for p in range(2):
                    r = slice(p * HD, (p + 1) * HD)
                    t_norm[0] = V(stt, dst[:, p::2, :], src[r, :, :], col(g)[r, :], prn[r, :, :], ALU.mult, ALU.mult)
                yield
            V.wait(t_bias)
            yield from attention("l", NH, 2, lambda h: qh[:, h, :], lambda h: kh[:, h, :], lambda h, kt: vtok[:, kt, h * HD:(h + 1) * HD],
                                 lambda h: mixT[(h % 2) * HD:(h % 2 + 1) * HD, JT + h // 2, :], m1, HD ** -0.5,
                                 [ps[2], ps[3]], [ps[4]], ps[5], bias=lambda h, ti: bias_sb[:, (2 * h + ti) * T:(2 * h + ti + 1) * T],
                                 ready=[t_norm[0], proj[18]])

        prn = sb("prn", [P, JT, T], scope=m1)[:, :, :]
        t_norm = [None]

        def convolve():
            V(tt, cz[:, :, TAPS - 1:], cz[:, :, TAPS - 1:], cu[:, :, :], ALU.mult, after=[proj[22]])
            for j in range(2):
                w = col("conv_w")[:, j * TAPS:(j + 1) * TAPS]
                t = V(ts, cc[:, j, :], cz[:, j, 0:T], w[:, 0:1], col("conv_b")[:, j:j + 1], ALU.mult, ALU.add)
                for k in range(1, TAPS):
                    t = V(stt, cc[:, j, :], cz[:, j, k:k + T], w[:, k:k + 1], cc[:, j, :], ALU.mult, ALU.add)
                    if k % 3 == 0:
                        yield
            for step in range(2):
                if step:
                    t = A(act, csq[:, :, :], cc[:, :, :], ACT.Square, after=[t])
                src = csq if step else cc
                at, bank, read = small.next()
                for j in range(2):
                    m = PE.mm(bank[:, 0:T], ones, src[:, j, :], start=j == 0, stop=j == 1, mark=j == 1, after=[t, read])
                if step == 0:
                    for j in range(2):
                        t = V(stt, cc[:, j, :], bank[:, 0:T], -1.0 / (2 * P), cc[:, j, :], ALU.mult, ALU.add, after=[m])
                    small.done(at, t)
                yield
            t = A(act, rstd[:, :], bank[:, 0:T], ACT.Sqrt, bias=EPSC, scale=1.0 / (2 * P), after=[m])
            small.done(at, t)
            V(nc.vector.reciprocal, rstd[:, :], rstd[:, :], after=[t])
            for j in range(2):
                t = V(stt, cc[:, j, :], cc[:, j, :], col("cln_w")[:, j:j + 1], rstd[:, :], ALU.mult, ALU.mult)
                A(act, mixT[:, 2 * JT + j, :], cc[:, j, :], ACT.Silu, bias=col("cln_b")[:, j:j + 1], after=[t])

        def prepare():
            lora = col("lora")
            r_, k_, v_ = (rkv[:, j * JT:(j + 1) * JT, :] for j in range(3))
            V.wait(t_cr)
            PE.wait(t_cr)
            A(act, lo[0:32, :], rkv[0:32, 9, :], ACT.Tanh, after=[proj[9]])
            A(act, lo[32:64, :], rkv[32:64, 9, :], ACT.Copy)
            t_lo = A(act, lo[64:128, :], rkv[64:128, 9, :], ACT.Sigmoid)
            for ti in range(2):
                at, bank, read = small.next()
                m = PE.mm(bank[:, 0:NH * HD], lo[0:32, ti * P:(ti + 1) * P], lora[0:32, :], mark=True, after=[t_lo, read])
                t = V(tt, sgw[:, ti, :], bank[:, 0:NH * HD], col("w0"), ALU.add, after=[m])
                small.done(at, t)
            yield
            for j in range(JT):
                t_kk = V(ts, kk[:, j, :], k_[:, j, :], col("k_k")[:, j:j + 1], None, ALU.mult)
            t_sg = A(act, sgw[:, :, :], sgw[:, :, :], ACT.Sigmoid, after=[t])
            for j in range(JT):
                at, bank, read = small.next()
                m = PE.mm(bank[:, 0:T], lora[32:64, j * P:(j + 1) * P], lo[32:64, :], mark=True, after=[read])
                t_a = A(act, aT[:, j, :], bank[:, 0:T], ACT.Sigmoid, bias=col("a0")[:, j:j + 1], after=[m])
                small.done(at, t_a)
                yield
            for j in range(JT):
                at, bank, read = small.next()
                m = PE.mm(bank[:, 0:T], lora[64:128, j * P:(j + 1) * P], lo[64:128, :], mark=True, after=[read])
                small.done(at, A(act, gate[:, j, :], bank[:, 0:T], ACT.Copy, after=[m]))
                yield
            for j in range(JT):
                at, bank, read = small.next()
                for ti in range(2):
                    m = PE.mm(bank[:, ti * T:(ti + 1) * T], sgw[:, ti, j * P:(j + 1) * P], cr[:, 0:T], mark=True, after=[t_sg, read])
                cum = bank[:, :].rearrange("p (t e s) -> p e t s", t=2, e=2)
                for dst, e, sign in ((d_in, 0, 1.0), (d_ex, 1, 1.0), (d_inv, 0, -1.0)):
                    t_d = A(act, three(dst[:, j, :], 2), cum[:, e, :, :], ACT.Exp, scale=sign, after=[m])
                small.done(at, t_d)
                yield
            t = A(act, tmp[:, :, :], kk[:, :, :], ACT.Square, after=[t_kk])
            for j in range(JT):
                at, bank, read = small.next()
                m = PE.mm(bank[:, 0:T], heads, tmp[:, j, :], mark=True, after=[t, read])
                t2 = A(act, tmp[:, j, :], bank[:, 0:T], ACT.Sqrt, bias=EPS12, after=[m])
                small.done(at, t2)
                yield
            V(nc.vector.reciprocal, tmp[:, :, :], tmp[:, :, :], after=[t2])
            V(tt, kk[:, :, :], kk[:, :, :], tmp[:, :, :], ALU.mult)
            yield
            for j in range(JT):
                V(ts, knew[:, j, :], aT[:, j, :], 1.0, col("k_a")[:, j:j + 1], ALU.subtract, ALU.mult, after=[t_a])
            V(stt, knew[:, :, :], knew[:, :, :], 1.0, k_, ALU.add, ALU.mult)
            yield
            for j in range(JT):
                t = V(stt, tmp[:, j, :], r_[:, j, :], col("r_k")[:, j:j + 1], knew[:, j, :], ALU.mult, ALU.mult)
            yield
            for j in range(JT):
                at, bank, read = small.next()
                m = PE.mm(bank[:, 0:T], heads, tmp[:, j, :], mark=True, after=[t, read])
                small.done(at, V(tt, bonus[:, j, :], v_[:, j, :], bank[:, 0:T], ALU.mult, after=[m]))
                yield
            V(tt, d_ex[:, :, :], kk[:, :, :], d_ex[:, :, :], ALU.mult, after=[t_d])
            V(stt, kk[:, :, :], kk[:, :, :], -1.0, aT[:, :, :], ALU.mult, ALU.mult)
            for p in range(2):
                yield
                r = slice(p * HD, (p + 1) * HD)
                tiles = [ap[r, :, :].rearrange("p j (t s) -> p j t s", t=2) for ap in (d_ex, r_, d_in)]
                V(nc.vector.tensor_copy, arh[:, p::2, :, 0, :], tiles[0])
                V(tt, arh[:, p::2, :, 1, :], tiles[1], tiles[2], ALU.mult)
                V(nc.vector.tensor_copy, dch[:, p::2, :], d_in[r, :, :].rearrange("p j (c s) -> p j c s", c=NC)[:, :, :, CH - 1])
                yield
                V(tt, bh[:, p::2, :], kk[r, :, :], d_inv[r, :, :], ALU.mult)
                V(tt, kh2[:, p::2, :], knew[r, :, :], d_inv[r, :, :], ALU.mult)

        tiles = project_tiles()
        for _ in range(10):
            next(tiles)
        prep = prepare()
        interleave((tiles, 1), (first_steps(prep, 26), 2))
        interleave((attend(), 2), (convolve(), 1), (prep, 1))
        phase()
        m1.close()

        m4 = ExitStack()
        mb = sb("mb", [P, NPROB, 2 * P], scope=m4)
        mk = sb("mk", [P, NPROB, 2 * P], scope=m4)
        lw = sb("lw", [P, NPROB, P], scope=m4)
        yi = sb("yi", [P, NPROB, P], scope=m4)
        xi = sb("xi", [P, NPROB, P], scope=m4)
        yT = sb("yT", [HD, NH, T], scope=m4)
        state = sb("state", [HD, NH, HD], scope=m4)
        gs = sb("gs", [P, NH * HD], scope=m4)
        us = sb("us", [P, NH * HD], scope=m4)
        flat = hT[:, :, :].rearrange("p a b -> p (a b)")
        lev = three(flat[:, 0:NPROB * P], NPROB)
        pr1 = three(flat[:, NPROB * P:2 * NPROB * P], NPROB)
        both = cr[:, CL["strict"][0]:CL["incl"][1]]
        level = [cr[:, CL["level"][0] + k * P:CL["level"][0] + (k + 1) * P] for k in range(6)]
        V(nc.vector.memset, gs[:, :], 0.0)
        V(nc.vector.memset, us[:, :], 0.0)
        btok = sb("btok", [P, 2, NH * HD], scope=m4)
        ktok = sb("ktok", [P, 2, NH * HD], scope=m4)
        vtk = sb("vtk", [P, 2, NH * HD], scope=m4)
        banks = Banks(ps[0:8])

        def token_major():
            for ti in range(2):
                t_s = slice(ti * P, (ti + 1) * P)
                for src, dst in ((None, vtk), (bh, btok), (kh2, ktok)):
                    at, bank, read = banks.next()
                    if src is not None:
                        for h_i in range(NH):
                            m = PE.flip(bank[:, h_i * HD:(h_i + 1) * HD], src[:, h_i, t_s], ident[0:HD, 0:HD], mark=h_i == NH - 1, after=[read])
                    else:
                        for j in range(JT):
                            m = PE.flip(bank[:, j * P:(j + 1) * P], rkv[:, 2 * JT + j, t_s], ident, mark=j == JT - 1, after=[read])
                    banks.done(at, A(act, dst[:, ti, :], bank[:, 0:NH * HD], ACT.Copy, after=[m]))
                    yield

        copies = token_major()
        for b in range(NPROB // 2):
            for src, dst in ((bh, mb), (kh2, mk)):
                at, bank, read = banks.next()
                for q in range(2):
                    h_i, ti = divmod(2 * b + q, 2)
                    m = PE.mm(bank[:, q * T:(q + 1) * T], src[:, h_i, ti * P:(ti + 1) * P], arh[:, h_i, ti, :, :], mark=q == 1, after=[read])
                banks.done(at, V(tt, dst[:, 2 * b:2 * b + 2, :], three(bank[:, :], 2), wide(both, [P, 2, T]), ALU.mult, after=[m]))
        for b in range(NPROB // 4):
            at, bank, read = banks.next()
            for q in range(4):
                h_i, ti = divmod(4 * b + q, 2)
                m = PE.mm(bank[:, q * P:(q + 1) * P], arh[:, h_i, ti, 0, :], bh[:, h_i, ti * P:(ti + 1) * P], mark=q == 3, after=[read])
            banks.done(at, A(act, lw[:, 4 * b:4 * b + 4, :], three(bank[:, :], 4), ACT.Copy, after=[m]))

        quad = [P, 4, P]
        built, added = [None] * 3, [None] * 3
        for b in range(3):
            s = slice(4 * b, 4 * b + 4)
            V(tt, xi[:, s, :], lw[:, s, :], wide(level[0], quad), ALU.mult, after=[A.last])
            V(tt, xi[:, s, :], xi[:, s, :], wide(ident, quad), ALU.add)
            V(tt, yi[:, s, :], mb[:, s, 0:P], wide(cr[:, slice(*CL["first"])], quad), ALU.mult)
            added[b] = V(tt, yi[:, s, :], yi[:, s, :], wide(ident, quad), ALU.add)
        for k in range(1, 6):
            for b in range(3):
                s = slice(4 * b, 4 * b + 4)
                t_lev = V(tt, lev[:, s, :], lw[:, s, :], wide(level[k], quad), ALU.mult, after=[built[b]])
                at, bank, read = banks.next()
                for q in range(4):
                    n = 4 * b + q
                    m = PE.mm(bank[:, q * P:(q + 1) * P], lev[:, n, :], yi[:, n, :], mark=q == 3, after=[read, t_lev, added[b]])
                built[b] = A(act, pr1[:, s, :], three(bank[:, :], 4), ACT.Copy, after=[m])
                banks.done(at, built[b])
            next(copies, None)
            for b in range(3):
                s = slice(4 * b, 4 * b + 4)
                got = []
                for dst in (yi, xi) if k < 5 else (yi,):
                    at, bank, read = banks.next()
                    for q in range(4):
                        n = 4 * b + q
                        l, r = (xi[:, n, :], pr1[:, n, :]) if dst is yi else (pr1[:, n, :], xi[:, n, :])
                        m = PE.mm(bank[:, q * P:(q + 1) * P], l, r, mark=q == 3, after=[read, built[b]])
                    got.append((at, bank, dst))
                built[b] = m
                for at, bank, dst in got:
                    added[b] = V(tt, dst[:, s, :], three(bank[:, :], 4), dst[:, s, :], ALU.add, after=[m])
                    banks.done(at, added[b])

        for _ in copies:
            pass

        PE.wait(A.last)
        y_read = [None] * 2
        for c in range(NC):
            ti, r = c // 2, slice((c % 2) * CH, (c % 2 + 1) * CH)
            rr = slice(P + r.start, P + r.stop)
            g_ps, u_ps, y_ps, s_ps = ps[0:4] if c % 2 == 0 else ps[4:8]
            for h_i in range(NH):
                n, o = 2 * h_i + ti, slice(h_i * HD, (h_i + 1) * HD)
                if c:
                    PE.mm(g_ps[r, o], arh[:, h_i, ti, 0, r], state[:, h_i, :], start=True, stop=False, after=[V.last])
                m = PE.mm(g_ps[r, o], mk[:, n, r], vtk[:, ti, o], start=c == 0, stop=True, mark=h_i == NH - 1, after=[V.last])
            t = V(nc.vector.tensor_copy, gs[r, :], g_ps[r, 0:NH * HD], after=[m])
            for h_i in range(NH):
                n, o = 2 * h_i + ti, slice(h_i * HD, (h_i + 1) * HD)
                m = PE.mm(u_ps[r, o], yi[:, n, r], gs[:, o], mark=h_i == NH - 1, after=[t])
            t = V(nc.vector.tensor_copy, us[r, :], u_ps[r, 0:NH * HD], after=[m])
            PE.wait(y_read[c % 2])
            if c < NC - 1:
                for h_i in range(NH):
                    o = slice(h_i * HD, (h_i + 1) * HD)
                    PE.mm(s_ps[0:HD, o], btok[r, ti, o], us[r, o], start=True, stop=False, after=[t])
                    m = PE.mm(s_ps[0:HD, o], ktok[r, ti, o], vtk[r, ti, o], start=False, stop=True, mark=h_i == NH - 1)
            for h_i in range(NH):
                n, o = 2 * h_i + ti, slice(h_i * HD, (h_i + 1) * HD)
                y_o = y_ps[0:HD, h_i * CH:(h_i + 1) * CH]
                if c:
                    PE.mm(y_o, state[:, h_i, :], arh[:, h_i, ti, 1, r], start=True, stop=False)
                PE.mm(y_o, us[:, o], mb[:, n, rr], start=c == 0, stop=False, after=[t])
                my = PE.mm(y_o, vtk[:, ti, o], mk[:, n, rr], start=False, stop=True, mark=h_i == NH - 1)
            y_read[c % 2] = A(act, yT[:, :, c * CH:(c + 1) * CH], three(y_ps[0:HD, 0:NH * CH], NH), ACT.Copy, after=[my])
            if c < NC - 1:
                s3 = three(s_ps[0:HD, 0:NH * HD], NH)
                decay = dch[:, :, c:c + 1].to_broadcast([HD, NH, HD])
                if c:
                    V(tt, state[:, :, :], s3, state[:, :, :], ALU.add, after=[m, my])
                    V(tt, state[:, :, :], state[:, :, :], decay, ALU.mult)
                else:
                    V(tt, state[:, :, :], s3, decay, ALU.mult, after=[m])

        yf = yT[:, :, :].rearrange("p a b -> p (a b)")
        sqf = flat[0:HD, 0:NH * T]
        for b in range(3):
            s = slice(b * 512, (b + 1) * 512)
            m = PE.mm(ps[b][0:HD, :], heads[0:HD, 0:HD], yf[:, s], mark=True, after=[A.last, V.last])
            V(stt, yf[:, s], ps[b][0:HD, :], -1.0 / HD, yf[:, s], ALU.mult, ALU.add, after=[m])
        A(act, sqf, yf, ACT.Square, after=[V.last])
        for b in range(3):
            s = slice(b * 512, (b + 1) * 512)
            m = PE.mm(ps[3 + b][0:HD, :], heads[0:HD, 0:HD], sqf[:, s], mark=True, after=[A.last])
            A(act, sqf[:, s], ps[3 + b][0:HD, :], ACT.Sqrt, bias=EPSG[0:HD, :], scale=1.0 / HD, after=[m])
        V(nc.vector.reciprocal, sqf, sqf, after=[A.last])
        V(tt, yf, yf, sqf, ALU.mult)
        for h_i in range(NH):
            r = slice((h_i % 2) * HD, (h_i % 2 + 1) * HD)
            V(ts, mixT[r, h_i // 2, :], yT[:, h_i, :], col("ln_w")[0:HD, h_i:h_i + 1], col("ln_b")[0:HD, h_i:h_i + 1], ALU.mult, ALU.add)
        V(tt, mixT[:, 0:JT, :], mixT[:, 0:JT, :], bonus[:, :, :], ALU.add)
        h = V(tt, mixT[:, 0:JT, :], mixT[:, 0:JT, :], gate[:, :, :], ALU.mult)
        phase()
        m4.close()
        mix.close()

        banks = Banks(ps[0:4])
        for m_i in range(KT):
            if m_i % 2 == 0:
                w = three(take_unit()[:, :], KT)
            at, bank, read = banks.next()
            for k in range(KT):
                m = PE.mm(bank[:, 0:T], w[:, k, (m_i % 2) * P:(m_i % 2 + 1) * P], mixT[:, k, :], start=k == 0, stop=k == KT - 1,
                          mark=k == KT - 1, after=[read])
            if m_i % 2:
                give_unit()
            banks.done(at, V(tt, xT[:, m_i, :], bank[:, 0:T], xT[:, m_i, :], ALU.add, after=[m]))

        h = rms(xT[:, :, :], hT[:, :, 0:T], col("norm_ffn2"), hT[:, :, T:2 * T], after=[V.last])
        half_residual(ffn('ffn2', h))
        phase()
        lay.close()
        end_stretch()

    start_engines()
    pp = sb("pp", [P, SP2_N])
    cs = sb("cs", [P, CS_N])
    sc = sb("sc", [P, 16])
    mod = sb("mod", [P, 48])
    cmod = sb("cmod", [P, 16])
    scale_x = sb("scale_x", [P, KT])
    scale_c = sb("scale_c", [P, KT])
    scale_2 = sb("scale_2", [P, KT])
    cx = ExitStack()
    ctxT = sb("ctxT", [P, KT, T], scope=cx)
    sq8 = sb("sq8", [P, KT, T], scope=cx)
    load(pp[:, :], p_last)
    load(cs[:, :], cs_in)
    t_in = load(ctxT[:, :, :], ctxT_in)
    stream(LAST_UNITS, lambda u: w_last[u, :, :])
    for e in (V, PE, A):
        e.wait(t_in)

    def col2(name):
        return pp[:, slice(*SP2[name])]

    def const(name):
        return cs[:, slice(*CS[name])]

    t = A(act, sc[:, :], col2("c"), ACT.Silu)
    for m_i in range(48):
        if m_i % 2 == 0:
            w = three(take_unit()[:, :], KT)
        for k in range(KT):
            m = PE.mm(ps[0][:, 2 * m_i:2 * m_i + 2], w[:, k, (m_i % 2) * P:(m_i % 2 + 1) * P], sc[:, 2 * k:2 * k + 2],
                      start=k == 0, stop=k == KT - 1, mark=m_i == 47 and k == KT - 1, after=[t])
        if m_i % 2:
            give_unit()
    mod_ps = ps[0][:, 0:96].rearrange("p (a b) -> p a b", b=2)
    V(tt, mod[:, :], mod_ps[:, :, 0], col2("b_mod"), ALU.add, after=[m])
    V(tt, cmod[:, :], mod_ps[:, 0:16, 1], col2("b_mod")[:, 0:16], ALU.add)
    shift1, gate1, shift2, gate2 = mod[:, 0:8], mod[:, 16:24], mod[:, 24:32], mod[:, 40:48]
    V(stt, scale_x[:, :], mod[:, 8:16], 1.0, col2("norm1"), ALU.add, ALU.mult)
    V(stt, scale_c[:, :], cmod[:, 8:16], 1.0, col2("norm1"), ALU.add, ALU.mult)
    V(stt, scale_2[:, :], mod[:, 32:40], 1.0, col2("norm2"), ALU.add, ALU.mult)
    rms(xT[:, :, :], hT[:, :, 0:T], scale_x, sq8[:, :, :], shift=shift1)
    h = rms(ctxT[:, :, :], hT[:, :, T:2 * T], scale_c, sq8[:, :, :], shift=cmod[:, 0:8], after=[PE.last])
    phase()
    cx.close()

    yaT = sb("yaT", [P, 4, T])
    ygT = sb("ygT", [P, 4, T])
    ysT = sb("ysT", [P, KT, T])
    atn = ExitStack()
    ssd = ExitStack()

    def project(dst_bank, w, width, after, mark=True):
        for k in range(KT):
            m = PE.mm(dst_bank[:, 0:width], w[:, k, :], hT[:, k, 0:width], start=k == 0, stop=k == KT - 1, mark=k == KT - 1, after=after)
        return m

    def half(w, j):
        return w[:, :, j * P:(j + 1) * P]

    kr = sb("kr", [P, 2, 2 * T], scope=atn)
    vt2 = sb("vt2", [P, 4, 2 * P], scope=atn)
    q8 = sb("q8", [P, 8, T], scope=atn)
    banks = Banks(ps[0:6])
    w = three(take_unit()[:, :], KT)
    for j in range(2):
        at, bank, read = banks.next()
        m = project(bank, half(w, j), 2 * T, [read, h])
        banks.done(at, A(act, kr[:, j, :], bank[:, :], ACT.Copy, after=[m]))
    give_unit()
    w = three(take_unit()[:, :], KT)
    for ti in range(4):
        at, bank, read = banks.next()
        for k in range(KT):
            m = PE.mm(bank[:, 0:2 * P], hT[:, k, ti * P:(ti + 1) * P], w[:, k, :], start=k == 0, stop=k == KT - 1, mark=k == KT - 1, after=[read])
        banks.done(at, A(act, vt2[:, ti, :], bank[:, 0:2 * P], ACT.Copy, after=[m]))
    give_unit()
    for j in range(8):
        if j % 2 == 0:
            w = three(take_unit()[:, :], KT)
        at, bank, read = banks.next()
        m = project(bank, half(w, j % 2), T, [read])
        banks.done(at, A(act, q8[:, j, :], bank[:, 0:T], ACT.Copy, after=[m]))
        if j % 2:
            give_unit()

    nrm = sb("nrm", [P, 512], scope=atn)
    rtmp = sb("rtmp", [P, T], scope=atn)
    for j in range(5):
        src, width = (q8[:, 4 + j, :], T) if j < 4 else (kr[:, 1, :], 2 * T)
        t = A(act, nrm[:, 0:width], src, ACT.Square, after=[V.last])
        m = PE.mm(ps[6][:, 0:width], heads, nrm[:, 0:width], mark=True, after=[t])
        t = A(act, nrm[:, 0:width], ps[6][:, 0:width], ACT.Sqrt, bias=EPS6, scale=1.0 / HD, after=[m])
        V(nc.vector.reciprocal, nrm[:, 0:width], nrm[:, 0:width], after=[t])
        V(stt, src, src, col2("qn" if j < 4 else "kn"), nrm[:, 0:width], ALU.mult, ALU.mult)
    qs = sb("qs", [HD, 16, T], scope=atn)
    ks = sb("ks", [HD, 4, 2 * T], scope=atn)
    for j in range(10):
        src = q8[:, j, :] if j < 8 else kr[:, j - 8, 0:T]
        m = PE.mm(ps[7][:, 0:T], const("rot"), src, mark=True, after=[V.last, A.last])
        V(tt, rtmp[:, :], ps[7][:, 0:T], const("sin"), ALU.mult, after=[m])
        V(tt, src, src, const("cos"), ALU.mult)
        for p in range(2):
            r = slice(p * HD, (p + 1) * HD)
            dst = qs[:, 2 * j + p, :] if j < 8 else ks[:, 2 * (j - 8) + p, 0:T]
            V(tt, dst, src[r, :], rtmp[r, :], ALU.add)
            if j >= 8:
                V(nc.vector.tensor_copy, ks[:, 2 * (j - 8) + p, T:2 * T], kr[r, j - 8, T:2 * T])
    for kind, dst in ((0, yaT), (1, ygT)):
        phase()
        window = kind == 0
        attn_scope = ExitStack()
        for _ in attention(f"w{kind}", 8, 4, lambda h_i: qs[:, 8 * kind + h_i, :], lambda h_i: ks[:, 2 * kind + h_i // 4, :],
                  lambda h_i, kt: vt2[:, kt, kind * P + (h_i // 4) * HD:kind * P + (h_i // 4 + 1) * HD],
                  lambda h_i: dst[(h_i % 2) * HD:(h_i % 2 + 1) * HD, h_i // 2, :], attn_scope, HD ** -0.5,
                  [ps[0], ps[1], ps[2], ps[3]], [ps[4], ps[5]], ps[6], bias=(lambda h_i, ti: const("window")[:, ti * T:(ti + 1) * T]) if window else None,
                  sink=col2("sink") if window else None):
            pass
        phase()
        attn_scope.close()
    atn.close()

    bT = sb("bT", [P, 2, T], scope=ssd)
    cT = sb("cT", [P, 2, T], scope=ssd)
    xs = sb("xs", [P, 2, DM], scope=ssd)
    dt = sb("dt", [P, 4, 32], scope=ssd)
    da = sb("da", [P, 4, 32], scope=ssd)
    acs = sb("acs", [P, 4, 32], scope=ssd)
    eac = sb("eac", [P, 4, 32], scope=ssd)
    s2 = ExitStack()
    h0 = sb("h0", [P, 2, DM], scope=ssd)
    xc = sb("xc", [P, 2, DM], scope=s2)
    bc = sb("bc", [P, 2, 2 * P], scope=s2)
    bcT = sb("bcT", [P, 2, T], scope=s2)
    cpad = sb("cpad", [P, 2, 2, T + 2], scope=s2)
    cout = sb("cout", [P, 2, 2, T], scope=s2)
    dtmp = sb("dtmp", [P, 3, 128], scope=s2)
    xw = sb("xw", [P, 2, DM], scope=s2)
    V(nc.vector.memset, cpad[:, :, :, :], 0.0)
    read_pad, read_out = [V.last] * 2, [None] * 2
    fbanks = Banks(ps[4:8])
    banks = Banks(ps[0:4])
    for j in range(12):
        d = j % 2
        if j % 2 == 0:
            w = three(take_unit()[:, :], KT)
        at, bank, read = banks.next()
        m = project(bank, half(w, d), 2 * T, [read])
        if d:
            give_unit()
        t = A(act, cpad[:, d, :, 1:T + 1], three(bank[:, :], 2), ACT.Copy, after=[m, read_pad[d]])
        banks.done(at, t)
        cw = [col2("conv_w")[:, 3 * j + k:3 * j + k + 1] for k in range(3)]
        V(ts, cout[:, d, :, :], cpad[:, d, :, 1:T + 1], cw[1], col2("conv_b")[:, j:j + 1], ALU.mult, ALU.add, after=[t, read_out[d]])
        V(stt, cout[:, d, :, :], cpad[:, d, :, 0:T], cw[0], cout[:, d, :, :], ALU.mult, ALU.add)
        read_pad[d] = V(stt, cout[:, d, :, :], cpad[:, d, :, 2:T + 2], cw[2], cout[:, d, :, :], ALU.mult, ALU.add)
        if j < 8:
            t = A(act, cout[:, d, :, :], cout[:, d, :, :], ACT.Silu, after=[V.last])
            at, bank, read = fbanks.next()
            for ti in range(4):
                m = PE.flip(bank[:, ti * P:(ti + 1) * P], cout[:, d, ti // 2, (ti % 2) * P:(ti % 2 + 1) * P], ident, mark=ti == 3, after=[t, read])
            read_out[d] = m
            A(act, xs[:, :, j * P:(j + 1) * P], three(bank[:, :], 4)[:, 0:2, :], ACT.Copy, after=[m])
            fbanks.done(at, A(act, xc[:, :, j * P:(j + 1) * P], three(bank[:, :], 4)[:, 2:4, :], ACT.Copy))
        elif j < 10:
            A(act, bT[:, j - 8, :], cout[:, d, 0, :], ACT.Silu, after=[V.last])
            t = A(act, bcT[:, j - 8, :], cout[:, d, 1, :], ACT.Silu)
            at, bank, read = fbanks.next()
            for ti in range(2):
                m = PE.flip(bank[:, ti * P:(ti + 1) * P], bcT[:, j - 8, ti * P:(ti + 1) * P], ident, mark=ti == 1, after=[t, read])
            fbanks.done(at, A(act, bc[:, :, (j - 8) * P:(j - 7) * P], three(bank[:, 0:T], 2), ACT.Copy, after=[m]))
            read_out[d] = A.last
        else:
            read_out[d] = A(act, cT[:, j - 10, :], cout[:, d, 0, :], ACT.Silu, after=[V.last])

    w_dt = three(col2("w_dt"), KT)
    at, bank, read = banks.next()
    for ti in range(4):
        for k in range(KT):
            m = PE.mm(bank[:, ti * 32:(ti + 1) * 32], hT[:, k, ti * P:(ti + 1) * P], w_dt[:, k, :], start=k == 0, stop=k == KT - 1,
                      mark=ti == 3 and k == KT - 1, after=[read])
    dt_f = dt[:, :, :].rearrange("p a b -> p (a b)")
    e_, u_, l_ = dtmp[:, 0, :], dtmp[:, 1, :], dtmp[:, 2, :]
    V(tt, dt[:, :, :], three(bank[:, 0:128], 4), wide(col2("dt_bias"), [P, 4, 32]), ALU.add, after=[m])
    t = V(stt, e_, dt_f, -1.0, dt_f, ALU.mult, ALU.max)
    t = A(act, e_, e_, ACT.Exp, scale=-1.0, after=[t])
    V(ts, u_, e_, 2.0, None, ALU.add, after=[t])
    V(nc.vector.reciprocal, u_, u_)
    V(tt, u_, u_, e_, ALU.mult)
    V(tt, e_, u_, u_, ALU.mult)
    V(ts, l_, e_, 1.0 / 15, None, ALU.mult)
    for n in (13, 11, 9, 7, 5, 3):
        V(stt, l_, l_, 1.0 / n, e_, ALU.add, ALU.mult)
    V(stt, l_, l_, 1.0, u_, ALU.add, ALU.mult)
    V(ts, l_, l_, 2.0, None, ALU.mult)
    V(stt, dt_f, dt_f, 0.0, l_, ALU.max, ALU.add)
    acoef = sb("acoef", [P, 32], scope=s2)
    t = A(act, acoef[:, :], col2("a_log"), ACT.Exp)
    t = V(stt, da[:, :, :], dt[:, :, :], -1.0, wide(acoef[:, :], [P, 4, 32]), ALU.mult, ALU.mult, after=[t])
    order = [three(const("fwd"), 2), three(const("bwd"), 2)]
    at, bank, read = banks.next()
    for g in range(2):
        for ti in range(2):
            for d in range(2):
                o = (2 * g + ti) * 32 + d * 16
                for st in range(2):
                    m = PE.mm(bank[:, o:o + 16], order[d][:, st, ti * P:(ti + 1) * P], da[:, 2 * g + st, d * 16:(d + 1) * 16],
                              start=st == 0, stop=st == 1, mark=True, after=[t, read])
    V(nc.vector.tensor_copy, acs[:, :, :], three(bank[:, 0:128], 4), after=[m])
    for st in range(2):
        m = PE.mm(bank[:, 128:160], ones, da[:, 2 + st, :], start=st == 0, stop=st == 1, mark=st == 1, after=[V.last])
    dec = sb("dec", [P, 2, 32], scope=s2)
    for ti in range(2):
        t = V(tt, dec[:, ti, :], bank[:, 128:160], acs[:, 2 + ti, :], ALU.subtract, after=[m])
    A(act, dec[:, :, :], dec[:, :, :], ACT.Exp, after=[t])
    t = A(act, eac[:, :, :], acs[:, :, :], ACT.Exp)
    V(tt, dec[:, :, :], dec[:, :, :], dt[:, 2:4, :], ALU.mult, after=[t])
    for d in range(2):
        for ti in range(2):
            V(tt, three(xw[:, ti, :], 16), three(xc[:, ti, :], 16), dec[:, ti, d * 16:(d + 1) * 16].unsqueeze(2).to_broadcast([P, 16, HD]),
              ALU.mult, after=[PE.last, A.last])
        for g in range(2):
            at, bank, read = banks.next()
            for ti in range(2):
                m = PE.mm(bank[:, :], bc[:, ti, g * P:(g + 1) * P], xw[:, ti, g * 512:(g + 1) * 512], start=ti == 0, stop=ti == 1, mark=ti == 1,
                          after=[read, V.last])
            banks.done(at, A(act, h0[:, d, g * 512:(g + 1) * 512], bank[:, :], ACT.Copy, after=[m]))
    phase()
    s2.close()

    s3_ = ExitStack()
    y = sb("y", [P, 2, DM], scope=ssd)
    cbm = sb("cbm", [P, 2, 2, 2 * T], scope=s3_)
    xdt = sb("xdt", [P, 2, 2, DM], scope=s3_)
    arow = sb("arow", [32, T], scope=s3_)
    lm = sb("lm", [P, 2, 2, T], scope=s3_)
    for g in range(2):
        for st in range(2):
            m = PE.mm(ps[g][:, st * T:(st + 1) * T], bT[:, g, st * P:(st + 1) * P], cT[:, g, :], mark=True)
        for d in range(2):
            V(tt, cbm[:, d, g, :], ps[g][:, :], const("fwd" if d == 0 else "bwd"), ALU.mult, after=[m])
    for d in range(2):
        for ti in range(2):
            V(tt, three(xdt[:, d, ti, :], 16), three(xs[:, ti, :], 16), dt[:, ti, d * 16:(d + 1) * 16].unsqueeze(2).to_broadcast([P, 16, HD]), ALU.mult)
    for ti in range(2):
        V(tt, three(y[:, ti, :], 16), three(xs[:, ti, :], 16), col2("d_skip").unsqueeze(2).to_broadcast([P, 16, HD]), ALU.mult)
    off = sb("off", [P, 512], scope=s3_)
    banks = Banks(ps[2:4])
    for d in range(2):
        for g in range(2):
            for ti in range(2):
                at, bank, read = banks.next()
                m = PE.mm(bank[:, :], cT[:, g, ti * P:(ti + 1) * P], h0[:, d, g * 512:(g + 1) * 512], mark=True, after=[read])
                t = V(tt, three(off[:, :], 8), three(bank[:, :], 8),
                      eac[:, ti, d * 16 + g * 8:d * 16 + (g + 1) * 8].unsqueeze(2).to_broadcast([P, 8, HD]), ALU.mult, after=[m])
                banks.done(at, t)
                V(tt, y[:, ti, g * 512:(g + 1) * 512], y[:, ti, g * 512:(g + 1) * 512], off[:, :], ALU.add)
    m = None
    for d in range(2):
        for st in range(2):
            m = PE.mm(ps[4][0:32, d * T:(d + 1) * T], da[:, st, :], order[d][:, st, :], start=st == 0, stop=st == 1, mark=True)
    arow2 = sb("arow2", [32, 2, T], scope=s3_)
    t_row = V(nc.vector.tensor_copy, arow2[:, :, :], three(ps[4][0:32, :], 2), after=[m])
    banks = Banks(ps[5:7])
    lm_read = [None] * 2
    acc = [ps[0], ps[1], ps[2], ps[3]]
    PE.wait(V.last)
    for b in range(4):
        PE.mm(acc[b][:, :], zeros[:, 0:P], zeros[:, :], start=True, stop=False, group=True)
    queue = []

    def diag(hd):
        d, h_i = divmod(hd, 16)
        b = hd % 2
        at, bank, read = banks.next()
        m = PE.mm(bank[:, 0:T], ident[0:32, hd:hd + 1].to_broadcast([32, P]), arow2[:, d, :], mark=True, after=[read, t_row])
        for st in range(2):
            t = V(ts, lm[:, b, st, :], bank[:, 0:T], acs[:, st, hd:hd + 1], 0.0, ALU.subtract, ALU.min, after=[m, lm_read[b]])
        banks.done(at, t)
        t = A(act, lm[:, b, :, :], lm[:, b, :, :], ACT.Exp, after=[t])
        return V(tt, lm[:, b, :, :], lm[:, b, :, :], three(cbm[:, d, h_i // 8, :], 2), ALU.mult, after=[t])

    def diag_sum(hd, t):
        d, h_i = divmod(hd, 16)
        b = hd % 2
        for ti in range(2):
            tiles = [0] if (d, ti) == (0, 0) else [1] if (d, ti) == (1, 1) else [0, 1]
            for st in tiles:
                m = PE.mm(acc[2 * ti + h_i // 8][:, (h_i % 8) * HD:(h_i % 8 + 1) * HD], lm[:, b, st, ti * P:(ti + 1) * P],
                          xdt[:, d, st, h_i * HD:(h_i + 1) * HD], start=False, stop=hd == 31, group=True,
                          mark=ti == 1 and st == tiles[-1], after=[t])
        lm_read[b] = m

    before = None
    for hd in range(32):
        t = diag(hd)
        if before:
            diag_sum(*before)
        before = (hd, t)
    diag_sum(*before)
    for ti in range(2):
        for g in range(2):
            V(tt, y[:, ti, g * 512:(g + 1) * 512], acc[2 * ti + g][:, :], y[:, ti, g * 512:(g + 1) * 512], ALU.add, after=[PE.last])
    phase()
    s3_.close()
    s4 = ExitStack()
    zs = sb("zs", [P, 2, DM], scope=s4)
    st4 = sb("st4", [P, 4], scope=s4)
    banks = Banks(ps[0:4])
    for u in range(4):
        w = three(take_unit()[:, :], KT)
        for ti in range(2):
            at, bank, read = banks.next()
            for k in range(KT):
                m = PE.mm(bank[:, 0:T], hT[:, k, ti * P:(ti + 1) * P], w[:, k, :], start=k == 0, stop=k == KT - 1, mark=k == KT - 1, after=[read])
            banks.done(at, A(act, zs[:, ti, u * T:(u + 1) * T], bank[:, 0:T], ACT.Silu, after=[m]))
        give_unit()
    V(tt, y[:, :, :], y[:, :, :], zs[:, :, :], ALU.mult, after=[A.last])
    for ti in range(2):
        A(act, zs[:, ti, :], y[:, ti, :], ACT.Square, accum_out=st4[:, ti:ti + 1], after=[V.last])
    t = A(act, st4[:, 2:4], st4[:, 0:2], ACT.Sqrt, bias=EPS6, scale=1.0 / DM)
    V(nc.vector.reciprocal, st4[:, 2:4], st4[:, 2:4], after=[t])
    for ti in range(2):
        t = V(ts, y[:, ti, :], y[:, ti, :], st4[:, 2 + ti:3 + ti], None, ALU.mult)
    banks = Banks(ps[4:8])
    for j in range(KT):
        at, bank, read = banks.next()
        for ti in range(2):
            m = PE.flip(bank[:, ti * P:(ti + 1) * P], y[:, ti, j * P:(j + 1) * P], ident, mark=ti == 1, after=[read, t])
        banks.done(at, V(ts, ysT[:, j, :], bank[:, 0:T], col2("ssm_norm")[:, j:j + 1], None, ALU.mult, after=[m]))
    phase()
    s4.close()
    ssd.close()

    mg = ExitStack()
    gates = sb("gates", [P, 24, T], scope=mg)
    mT = sb("mT", [P, KT, T], scope=mg)
    prod = sb("prod", [P, 2, T], scope=mg)
    banks = Banks(ps[0:2])
    for j in range(24):
        if j % 2 == 0:
            w = three(take_unit()[:, :], KT)
        at, bank, read = banks.next()
        m = project(bank, half(w, j % 2), T, [read])
        banks.done(at, A(act, gates[:, j, :], bank[:, 0:T], ACT.Sigmoid, after=[m]))
        if j % 2:
            give_unit()
    banks = Banks(ps[2:8])
    for hf in range(2):
        w_a, w_c = three(take_unit()[:, :], 4), three(take_unit()[:, :], 4)
        w_b = [three(take_unit()[:, :], KT) for _ in range(2)]
        for mi in range(4):
            m_i = 4 * hf + mi
            o = slice(mi * P, (mi + 1) * P)
            parts = [(w_a[:, :, o], yaT, 4), (w_b[mi // 2][:, :, (mi % 2) * P:(mi % 2 + 1) * P], ysT, KT), (w_c[:, :, o], ygT, 4)]
            for b, (wv, src, nk) in enumerate(parts):
                at, bank, read = banks.next()
                for k in range(nk):
                    m = PE.mm(bank[:, 0:T], wv[:, k, :], src[:, k, :], start=k == 0, stop=k == nk - 1, mark=k == nk - 1, after=[read])
                dst = mT[:, m_i, :] if b == 0 else prod[:, b - 1, :]
                banks.done(at, V(tt, dst, gates[:, b * KT + m_i, :], bank[:, 0:T], ALU.mult, after=[m, A.last]))
                if b:
                    t = V(tt, mT[:, m_i, :], mT[:, m_i, :], dst, ALU.add)
        PE.pending += 4
        PE.flush()
    banks = Banks(ps[0:4])
    PE.wait(A.last)
    for m_i in range(KT):
        if m_i % 2 == 0:
            w = three(take_unit()[:, :], KT)
        at, bank, read = banks.next()
        for k in range(KT):
            m = PE.mm(bank[:, 0:T], w[:, k, (m_i % 2) * P:(m_i % 2 + 1) * P], mT[:, k, :], start=k == 0, stop=k == KT - 1, mark=k == KT - 1,
                      after=[read, t])
        if m_i % 2:
            give_unit()
        banks.done(at, V(stt, xT[:, m_i, :], bank[:, 0:T], gate1[:, m_i:m_i + 1], xT[:, m_i, :], ALU.mult, ALU.add, after=[m]))
    phase()
    mg.close()

    sq9 = sb("sq9", [P, KT, T])
    pad = sb("pad", [P, 2, T + 2])
    csum = sb("csum", [P, 2, T])
    V(nc.vector.memset, pad[:, :, :], 0.0)
    h = rms(xT[:, :, :], hT[:, :, 0:T], scale_2, sq9[:, :, :], shift=shift2, after=[V.last])
    A.wait(V.last)
    done, ffn_scope = ffn('ffn3', h, conv={"pad": pad, "sum": csum, "w": col2("fconv_w"), "b": col2("fconv_b")})
    for m_i in range(KT):
        V(stt, xT[:, m_i, :], ps[2 + m_i // 2][:, (m_i % 2) * T:(m_i % 2 + 1) * T], gate2[:, m_i:m_i + 1], xT[:, m_i, :],
          ALU.mult, ALU.add, after=[done])
    t = rms(xT[:, :, :], hT[:, :, 0:T], col2("final"), sq9[:, :, :], after=[V.last])
    A.wait(t)
    nc.scalar.dma_start(out, hT[:, :, 0:T]).then_inc(s_out, 16)
    nc.scalar.wait_ge(s_out, 16)
    nc.all_engine_barrier()
    ffn_scope.close()
    ctx.close()


def _cols(v, n=None):
    v = np.asarray(v)
    return np.moveaxis(v.reshape(*v.shape[:-1], -1, P), -1, -2)


def _in_units(w, cols):
    k = w.shape[0] // P
    return w.reshape(k, P, -1, cols).transpose(2, 1, 0, 3).reshape(-1, P, k * cols)


def _ffn_units(g, u, d):
    gu = [_in_units(w, 2 * P) for w in (g, u)]
    dn = d.reshape(FT // 2, 2, P, DM).transpose(0, 2, 1, 3).reshape(FT // 2, P, UNIT)
    return np.stack([*gu, dn], axis=1).reshape(-1, P, UNIT)


def kernel(**inputs):
    import concourse.bacc as _bacc
    from concourse.bass_utils import run_bass_kernel_spmd as _run

    a = {k: np.asarray(v) for k, v in inputs.items()}
    f = np.float32
    w_layers, p_layers = [], []
    for l in range(DEPTH):
        w_in = np.concatenate([a["w_in"][l], np.zeros((DM, P), f)], axis=1)
        w_layers.append(np.concatenate([
            _ffn_units(a["ffn1_w_gate"][l], a["ffn1_w_up"][l], a["ffn1_w_down"][l]),
            _in_units(w_in, 2 * P), _in_units(a["w_out"][l], 2 * P),
            _ffn_units(a["ffn2_w_gate"][l], a["ffn2_w_up"][l], a["ffn2_w_down"][l])]))
        p = np.zeros((P, LP_N), f)

        def put(name, v):
            p[:v.shape[0], slice(*LP[name])] = v

        for n in ("norm_ffn1", "norm_mix", "norm_ffn2"):
            put(n, _cols(a[n][l]))
        put("mu", _cols(a["shift_mu"][l]))
        put("a0", _cols(a["rwkv_a0"][l]))
        put("k_k", _cols(a["rwkv_k_k"][l]))
        put("k_a", _cols(a["rwkv_k_a"][l]))
        put("r_k", _cols(a["rwkv_r_k"][l].reshape(-1)))
        put("ln_w", a["rwkv_ln_w"][l].reshape(NH, HD).T)
        put("ln_b", a["rwkv_ln_b"][l].reshape(NH, HD).T)
        put("qn", np.tile(a["attn_q_norm"][l], 2)[:, None])
        put("kn", np.tile(a["attn_k_norm"][l], 2)[:, None])
        put("conv_w", a["conv_dw_w"][l].reshape(TAPS, 2, P).transpose(2, 1, 0).reshape(P, 2 * TAPS))
        put("conv_b", _cols(a["conv_dw_b"][l]))
        put("cln_w", _cols(a["conv_ln_w"][l]))
        put("cln_b", _cols(a["conv_ln_b"][l]))
        put("lora", np.concatenate([a["rwkv_w2"][l], a["rwkv_a2"][l], a["rwkv_g2"][l]], axis=0))
        put("w0", np.broadcast_to(a["rwkv_w0"][l], (P, NH * HD)))
        p_layers.append(p)
    w_layers, p_layers = np.stack(w_layers), np.stack(p_layers)

    b = {k[:-2]: (v[0] if v.ndim > 1 and k not in ("c_2", "ctx_2") else v) for k, v in a.items() if k.endswith("_2")}
    w2 = b["w_in"]
    at, span = 0, {}
    for n, width in (("a_q", 512), ("a_k", 128), ("a_v", 128), ("z", 1024), ("xbc", 1536), ("dt", 32), ("c_q", 512),
                     ("c_k", 128), ("c_v", 128), ("gates", 3072)):
        span[n] = w2[:, at:at + width]
        at += width
    pair = lambda x, y: _in_units(np.concatenate([span[x], span[y]], axis=1), 2 * P)
    oa, oc, ob = _in_units(b["w_oa"], 512), _in_units(b["w_oc"], 512), _in_units(b["w_ob"], 2 * P)
    w_last = np.concatenate([
        _in_units(b["w_mod"], 2 * P), pair("a_k", "c_k"), pair("a_v", "c_v"), _in_units(span["a_q"], 2 * P),
        _in_units(span["c_q"], 2 * P), _in_units(span["xbc"], 2 * P), _in_units(span["z"], 2 * P),
        _in_units(span["gates"], 2 * P), oa[0:1], oc[0:1], ob[0:2], oa[1:2], oc[1:2], ob[2:4],
        _in_units(b["w_out"], 2 * P), _ffn_units(b["ffn_w_gate"], b["ffn_w_up"], b["ffn_w_down"])])
    p = np.zeros((P, SP2_N), f)

    def put2(name, v):
        p[:, slice(*SP2[name])] = v

    put2("c", np.stack([_cols(b["c"].reshape(-1)), _cols(b["c_ctx"])], axis=2).reshape(P, 16))
    put2("b_mod", _cols(b["b_mod"]))
    put2("norm1", _cols(b["norm1"]))
    put2("norm2", _cols(b["norm2"]))
    put2("final", _cols(b["final_norm"]))
    put2("conv_w", b["ssm_conv_w"].reshape(3, 12, P).transpose(2, 1, 0).reshape(P, 36))
    put2("conv_b", _cols(b["ssm_conv_b"]))
    put2("a_log", np.broadcast_to(b["ssm_A_log"].reshape(1, 32), (P, 32)))
    put2("dt_bias", np.broadcast_to(b["ssm_dt_bias"].reshape(1, 32), (P, 32)))
    put2("d_skip", np.broadcast_to(b["ssm_D"].reshape(1, 16), (P, 16)))
    put2("ssm_norm", _cols(b["ssm_norm"]))
    put2("qn", np.tile(b["c_q_norm"], 2)[:, None])
    put2("kn", np.tile(b["c_k_norm"], 2)[:, None])
    put2("sink", np.broadcast_to(b["a_sink"].reshape(1, 8), (P, 8)))
    put2("fconv_w", b["ffn_conv_w"].reshape(3, FT, P).transpose(2, 1, 0).reshape(P, 3 * FT))
    put2("fconv_b", _cols(b["ffn_conv_b"]))
    put2("w_dt", span["dt"].reshape(KT, P, 32).transpose(1, 0, 2).reshape(P, KT * 32))
    c0, cl, cs = constants()

    def chan(x):
        return x.reshape(T, KT, P).transpose(2, 1, 0)

    arrays = {"xT": chan(a["x"]), "ctxT": chan(b["ctx"]), "w_layers": w_layers, "w_last": w_last, "p_layers": p_layers,
              "p_last": p, "c0": c0, "cl": cl, "cs": cs}
    arrays = {k: np.ascontiguousarray(v) for k, v in arrays.items()}
    nc = _bacc.Bacc("TRN2", target_bir_lowering=False, num_devices=1)
    args = [nc.dram_tensor("in_" + k, v.shape, F32, kind="ExternalInput").ap() for k, v in arrays.items()]
    out = nc.dram_tensor("out_x", (P, KT, T), F32, kind="ExternalOutput").ap()
    build(nc, *args, out)
    r = _run(nc, [{"in_" + k: v for k, v in arrays.items()}], core_ids=[0])
    return np.ascontiguousarray(r.results[0]["out_x"].transpose(2, 1, 0)).reshape(1, T, DM)
```

```python
import math
from contextlib import ExitStack

import numpy as np

import concourse.bass as bass
import concourse.mybir as mybir
from concourse.alu_op_type import AluOpType as ALU

F32 = mybir.dt.float32
BF16 = mybir.dt.bfloat16
F32R = mybir.dt.float32r
ACT = mybir.ActivationFunctionType
AX = mybir.AxisListType

P = 128
T = 256
DM = 1024
KT = DM // P
FF = 2816
FT = FF // P
DEPTH = 2
HD = 64
NH = 6
JT = NH * HD // P
CH = 64
NC = T // CH
NPROB = 2 * NH
TAPS = 31
UNIT = 2048
SLOTS = 6
LAYER_UNITS = 3 * FT // 2 + 12 + 4 + 3 * FT // 2
LAST_UNITS = 24 + 28 + 8 + 4 + 3 * FT // 2
NEG = -1.0e30

def _columns(sizes):
    at, out = 0, {}
    for name, n in sizes:
        out[name] = (at, at + n)
        at += n
    return out, at

LP, LP_N = _columns([("norm_ffn1", KT), ("norm_mix", KT), ("norm_ffn2", KT), ("mu", 10), ("a0", JT),
                     ("k_k", JT), ("k_a", JT), ("r_k", JT), ("ln_w", NH), ("ln_b", NH), ("qn", 1), ("kn", 1),
                     ("conv_w", 2 * TAPS), ("conv_b", 2), ("cln_w", 2), ("cln_b", 2), ("lora", NH * HD),
                     ("w0", NH * HD)])
SP2, SP2_N = _columns([("c", 16), ("b_mod", 48), ("norm1", KT), ("norm2", KT), ("final", KT), ("conv_w", 36),
                       ("conv_b", 12), ("a_log", 32), ("dt_bias", 32), ("d_skip", 16), ("ssm_norm", KT),
                       ("qn", 1), ("kn", 1), ("sink", 8), ("fconv_w", 3 * FT), ("fconv_b", FT),
                       ("w_dt", KT * 32)])
C0, C0_N = _columns([("ident", P), ("heads", P), ("ones", P)])
CL, CL_N = _columns([("cum", 2 * P), ("strict", P), ("incl", P), ("level", 6 * P), ("first", P),
                     ("bias", NH * 2 * T)])
CS, CS_N = _columns([("window", 2 * T), ("cos", T), ("sin", T), ("rot", P), ("fwd", 2 * T), ("bwd", 2 * T)])


def _slopes(n):
    def pow2(m):
        start = 2.0 ** (-8.0 / m)
        return [start ** (i + 1) for i in range(m)]
    c = 2 ** int(math.floor(math.log2(n)))
    return pow2(n) if c == n else pow2(c) + pow2(2 * c)[0::2][: n - c]


def constants():
    c0 = np.zeros((P, C0_N), np.float32)
    i = np.arange(P)
    c0[:, slice(*C0["ident"])] = np.eye(P)
    c0[:, slice(*C0["heads"])] = i[:, None] // HD == i[None] // HD
    c0[:, slice(*C0["ones"])] = 1.0
    cl = np.zeros((P, CL_N), np.float32)
    same = i[:, None] // CH == i[None] // CH
    a, b = CL["cum"]
    cl[:, a:a + P] = -math.exp(-0.5) * (same & (i[:, None] <= i[None]))
    cl[:, a + P:b] = -math.exp(-0.5) * (same & (i[:, None] < i[None]))
    r, c = i[:, None], i[None]
    cl[:, slice(*CL["strict"])] = same & (r < c)
    cl[:, slice(*CL["incl"])] = same & (r <= c)
    for k in range(6):
        w = 1 << k
        m = (r // (2 * w) == c // (2 * w)) & (r // w % 2 == 1) & (c // w % 2 == 0)
        cl[:, CL["level"][0] + k * P:CL["level"][0] + (k + 1) * P] = m
        if k == 0:
            cl[:, slice(*CL["first"])] = m.T
    t = np.arange(T)
    dist = t[:, None] - t[None]
    count = (((dist >= 0) & (dist <= 128)).astype(int) + ((dist >= 0) & (dist % 4 == 0))
             + ((dist >= 0) & (dist % 16 == 0)))
    for h, slope in enumerate(_slopes(NH)):
        full = np.where(count > 0, -slope * dist + np.log(np.maximum(count, 1)), NEG)
        a = CL["bias"][0] + h * 2 * T
        cl[:, a:a + 2 * T] = full.reshape(2, P, T).transpose(1, 0, 2).reshape(P, 2 * T)
    cs = np.zeros((P, CS_N), np.float32)
    cs[:, slice(*CS["window"])] = np.where(np.abs(dist) <= 128, 0.0, NEG).reshape(2, P, T).transpose(1, 0, 2).reshape(P, -1)
    n = HD // 4
    inv = (np.float32(10000.0) ** (-np.arange(n, dtype=np.float32) / n)).astype(np.float32)
    ang = np.concatenate([(t // 64)[:, None] * inv, (t % 64)[:, None] * inv], axis=-1).astype(np.float32)
    pair = (i % HD) // 2
    cs[:, slice(*CS["cos"])] = np.cos(ang).T[pair]
    cs[:, slice(*CS["sin"])] = np.sin(ang).T[pair]
    rot = np.zeros((P, P))
    rot[i[0::2] + 1, i[0::2]] = -1.0
    rot[i[0::2], i[0::2] + 1] = 1.0
    cs[:, slice(*CS["rot"])] = rot
    for name, m in (("fwd", t[:, None] <= t[None]), ("bwd", t[:, None] >= t[None])):
        cs[:, slice(*CS[name])] = m.reshape(2, P, T).transpose(1, 0, 2).reshape(P, -1)
    return c0, cl, cs


class Engine:

    def __init__(self, eng, sem):
        self.eng, self.sem = eng, sem
        self.restart()

    def restart(self):
        self.n, self.seen = 0, {}

    @property
    def last(self):
        return (self.sem, self.n)

    def wait(self, *results):
        for r in results:
            if r is None or r[1] == 0:
                continue
            if self.seen.get(r[0].num, 0) < r[1]:
                self.eng.wait_ge(r[0], r[1])
                self.seen[r[0].num] = r[1]

    def __call__(self, op, *args, after=(), **kw):
        self.wait(self.last, *after)
        op(*args, **kw).then_inc(self.sem, 1)
        self.n += 1
        return self.last


class Tensor(Engine):

    def restart(self):
        self.n, self.seen, self.pending = 0, {}, 0

    def mm(self, out, lhsT, rhs, start=True, stop=True, mark=False, sem=None, after=(), group=False):
        self.wait(*after)
        ins = self.eng.matmul(out, lhsT, rhs, start=start, stop=stop, skip_group_check=group)
        return self._count(ins, mark, sem)

    def flip(self, out, in_, ident, mark=False, after=()):
        self.wait(*after)
        return self._count(self.eng.transpose(out, in_, ident), mark, None)

    def _count(self, ins, mark, sem):
        if mark:
            ins.then_inc(self.sem, 1)
            self.n += 1
        elif sem is not None:
            ins.then_inc(sem, 1)
        elif self.pending:
            ins.then_inc(self.free, self.pending)
            self.pending = 0
        return self.last

    def flush(self):
        if self.pending:
            self.eng.drain().then_inc(self.free, self.pending)
        self.pending = 0

    def fence(self):
        self.eng.drain().then_inc(self.sem, 1)
        self.n += 1
        return self.last


class Banks:

    def __init__(self, bufs):
        self.bufs, self.read, self.at = list(bufs), [None] * len(bufs), -1

    def next(self):
        self.at = (self.at + 1) % len(self.bufs)
        return self.at, self.bufs[self.at], self.read[self.at]

    def done(self, at, result):
        self.read[at] = result


def build(nc, xT_in, ctxT_in, w_layers, w_last, p_layers, p_last, c0_in, cl_in, cs_in, out):
    ctx = ExitStack()

    def sb(name, shape, dt=F32, scope=None):
        return (scope or ctx).enter_context(nc.sbuf_tensor(name, shape, dt))

    def sem(name):
        return ctx.enter_context(nc.semaphore(name))

    s_pe, s_act_e, s_dve, s_pool = sem("s_pe"), sem("s_act_e"), sem("s_dve"), sem("s_pool")
    s_free = sem("s_free")
    s_slot = [sem(f"s_slot{k}") for k in range(SLOTS)]
    s_gu = sem("s_gu")
    s_sg = sem("s_sg")
    s_hid = sem("s_hid")
    s_cv = sem("s_cv")
    s_hi = sem("s_hi")
    s_lo = sem("s_lo")
    s_ch = sem("s_ch")
    s_in = sem("s_in")
    s_out = sem("s_out")
    every_sem = [s_pe, s_act_e, s_dve, s_pool, s_free, *s_slot, s_gu, s_sg, s_hid, s_cv, s_hi, s_lo, s_ch, s_in]

    PE, A, V, G = Tensor(nc.tensor, s_pe), Engine(nc.scalar, s_act_e), Engine(nc.vector, s_dve), Engine(nc.gpsimd, s_pool)
    PE.free = s_free
    ring = [sb(f"ring{k}", [P, UNIT]) for k in range(SLOTS)]
    ps = [ctx.enter_context(nc.psum_tensor(f"ps{k}", [P, 512], F32)) for k in range(8)]
    xT = sb("xT", [P, KT, T])
    hT = sb("hT", [P, KT, 2 * T])
    c0 = sb("c0", [P, C0_N])
    rstd = sb("rstd", [P, T])
    zeros = sb("zeros", [P, 512], BF16)
    eps = sb("eps", [P, 5])
    EPS6, EPS12, EPSG, EPSC, ONE = (eps[:, k:k + 1] for k in range(5))
    ident, heads, ones = (c0[:, slice(*C0[k])] for k in ("ident", "heads", "ones"))

    tt, ts, stt = nc.vector.tensor_tensor, nc.vector.tensor_scalar, nc.vector.scalar_tensor_tensor
    act = nc.scalar.activation
    load_n = [0]

    def load(dst, src):
        nc.scalar.dma_start(dst, src).then_inc(s_in, 16)
        load_n[0] += 16
        return (s_in, load_n[0])

    def phase():
        PE.fence()
        for e in (PE, A, V, G):
            e.wait(PE.last, A.last, V.last, G.last)

    def three(ap, n):
        return ap.rearrange("p (a b) -> p a b", a=n)

    def wide(ap, shape):
        return ap.unsqueeze(1).to_broadcast(shape)

    def stream(units, source):
        trips = units // SLOTS
        with nc.sync.Fori(0, trips) as i:
            for k in range(SLOTS):
                nc.sync.wait_ge(s_free, i * SLOTS + (k + 1))
                nc.sync.dma_start(ring[k][:, :], source(i * SLOTS + k)).then_inc(s_slot[k], 16)
        for u in range(trips * SLOTS, units):
            nc.sync.wait_ge(s_free, u + 1)
            nc.sync.dma_start(ring[u % SLOTS][:, :], source(u)).then_inc(s_slot[u % SLOTS], 16)

    unit_at = [0]

    def take_unit():
        u = unit_at[0]
        unit_at[0] += 1
        nc.tensor.wait_ge(s_slot[u % SLOTS], 16 * (u // SLOTS + 1))
        return ring[u % SLOTS]

    def give_unit():
        PE.pending += 1

    def rms(src, dst, g, square, shift=None, after=(), each=None, meanwhile=None):
        for k in range(KT):
            if k % 2 == 0:
                t = A(act, square[:, k:k + 2, :], src[:, k:k + 2, :], ACT.Square, after=after)
            m = PE.mm(ps[7][:, 0:T], ones, square[:, k, :], start=k == 0, stop=k == KT - 1, mark=k in (0, KT - 1), after=[t, V.last])
            if k == 0:
                begun = m
        if meanwhile is not None:
            meanwhile(begun)
        t = A(act, rstd[:, :], ps[7][:, 0:T], ACT.Sqrt, bias=EPS6, scale=1.0 / DM, after=[m, V.last])
        V(nc.vector.reciprocal, rstd[:, :], rstd[:, :], after=[t])
        for k in range(KT):
            t = V(stt, dst[:, k, :], src[:, k, :], g[:, k:k + 1], rstd[:, :], ALU.mult, ALU.mult)
            if shift is not None:
                t = V(ts, dst[:, k, :], dst[:, k, :], shift[:, k:k + 1], None, ALU.add)
            if each is not None:
                each(k, t)
        return t

    ffn_at = [0]
    SPLITS = 3 * FT

    def ffn(tag, norm, conv=None):
        scope = ExitStack()
        hh, hl = (sb(f"{n}_{tag}", [P, KT, T], F32R, scope) for n in ("h_hi", "h_lo"))
        wh, wl = (sb(f"{n}_{tag}", [P, 2, 2, KT, P], F32R, scope) for n in ("gu_hi", "gu_lo"))
        dh, dl = (sb(f"{n}_{tag}", [P, 4, DM], F32R, scope) for n in ("down_hi", "down_lo"))
        sg, hid = (sb(f"{n}_{tag}", [P, 2, T], F32, scope) for n in ("silu", "hid"))
        xh, xl = (sb(f"{n}_{tag}", [P, 2, T], F32R, scope) for n in ("hid_hi", "hid_lo"))
        u0, base = unit_at[0], ffn_at[0] * FT
        sbase, cbase = ffn_at[0] * SPLITS, ffn_at[0] * 2 * FT
        unit_at[0] += 3 * FT // 2
        ffn_at[0] += 1
        nc_t = nc.tensor
        PE.flush()

        def number(kind, c):
            if kind == 2:
                return 3 * c + 5 if c < FT - 1 else SPLITS
            return 3 * c + kind if c else 1 + kind

        def parts(kind, c):
            raw = ring[(u0 + 3 * (c // 2) + kind) % SLOTS]
            if kind == 2:
                return three(raw[:, :], 2)[:, c % 2, :], dh[:, c % 4, :], dl[:, c % 4, :]
            return three(raw[:, :], KT)[:, :, (c % 2) * P:(c % 2 + 1) * P], wh[:, c % 2, kind, :, :], wl[:, c % 2, kind, :, :]

        def round_part(kind, c, i):
            src, hi, _ = parts(kind, c)
            if c % 2 == 0:
                u = u0 + 3 * (c // 2) + kind
                nc.scalar.wait_ge(s_slot[u % SLOTS], i * 16 + 16 * (u // SLOTS + 1))
            act(hi, src, ACT.Copy).then_inc(s_hi, 1)

        def rest_part(kind, c, i):
            src, hi, lo = parts(kind, c)
            nc.vector.wait_ge(s_hi, i * 12 + (sbase + number(kind, c)))
            tt(lo, src, hi.bitcast(F32), ALU.subtract).then_inc(s_lo, 1)
            if c % 2 and kind:
                nc.vector.drain().then_inc(s_free, 2 if kind == 1 else 1)

        def passes(hi, lo, xhi, xlo):
            return (hi, xhi), (hi, xlo), (lo, xhi)

        def gate_up(c, i, ready=(None,) * KT):
            nc_t.wait_ge(s_hid, i * 4 + (base + c + 1))
            nc_t.wait_ge(s_lo, i * 12 + (sbase + number(1, c)))
            for kind in range(2):
                for k in range(KT):
                    PE.wait(ready[k])
                    for n, (w, x) in enumerate(passes(wh[:, c % 2, kind, k, :], wl[:, c % 2, kind, k, :], hh[:, k, :], hl[:, k, :])):
                        last = k == KT - 1 and n == 2
                        PE.mm(ps[c % 2][:, kind * T:(kind + 1) * T], w, x, start=k == 0 and n == 0, stop=last,
                              sem=s_gu if last and kind == 1 else None)

        def down(c, i, last_tile=False):
            nc_t.wait_ge(s_lo, i * 12 + (sbase + number(2, c)))
            nc_t.wait_ge(s_hid, i * 4 + (base + c + 3))
            for m in range(KT):
                o = slice(m * P, (m + 1) * P)
                for n, (w, x) in enumerate(passes(dh[:, c % 4, o], dl[:, c % 4, o], xh[:, c % 2, :], xl[:, c % 2, :])):
                    PE.mm(ps[2 + m // 2][:, (m % 2) * T:(m % 2 + 1) * T], w, x,
                          start=False, stop=last_tile, group=True, mark=last_tile and m == KT - 1 and n == 2)

        behind, split_done = [], [None] * KT

        def rest_h():
            k, t = behind.pop()
            split_done[k] = V(tt, hl[:, k, :], hT[:, k, 0:T], hh[:, k, :].bitcast(F32), ALU.subtract, after=[t])

        def split_h(k, t):
            t = A(act, hh[:, k, :], hT[:, k, 0:T], ACT.Copy, after=[t])
            if behind:
                rest_h()
            behind.append((k, t))

        def first_splits(begun):
            V.wait(begun)
            for kind in range(2):
                round_part(kind, 0, 0)
                rest_part(kind, 0, 0)
            for b in range(4):
                PE.mm(ps[2 + b][:, :], zeros[:, 0:P], zeros[:, :], start=True, stop=False, group=True)

        norm(each=split_h, meanwhile=first_splits)
        rest_h()
        for kind, c in ((0, 1), (1, 1), (2, 0)):
            round_part(kind, c, 0)
            rest_part(kind, c, 0)
        gate_up(0, 0, split_done)
        trips = (FT - 1) // 4
        with nc_t.Fori(0, trips) as i:
            for c in range(4):
                gate_up(c + 1, i)
                down(c, i)
        for c in range(4 * trips, FT):
            if c + 1 < FT:
                gate_up(c + 1, 0)
            down(c, 0, c == FT - 1)

        def silu_tile(c, i):
            nc.scalar.wait_ge(s_gu, i * 4 + (base + c + 1))
            if conv is None:
                act(sg[:, c % 2, :], ps[c % 2][:, 0:T], ACT.Silu).then_inc(s_sg, 1)
                return
            act(conv["pad"][:, c % 2, 1:T + 1], ps[c % 2][:, 0:T], ACT.Copy).then_inc(s_sg, 1)
            nc.scalar.wait_ge(s_cv, i * 12 + (3 * c + 3))
            act(sg[:, c % 2, :], conv["sum"][:, c % 2, :], ACT.Silu).then_inc(s_sg, 1)

        def conv_tile(c, i):
            n = i * 4 + c
            pad, total = conv["pad"][:, c % 2, :], conv["sum"][:, c % 2, :]
            w = [conv["w"][:, bass.ds(n * 3 + k, 1)] for k in range(3)]
            nc.vector.wait_ge(s_sg, i * 8 + (2 * c + 1))
            ts(total, pad[:, 1:T + 1], w[1], conv["b"][:, bass.ds(n, 1)], ALU.mult, ALU.add).then_inc(s_cv, 1)
            for k in (0, 2):
                nc.vector.wait_ge(s_cv, i * 12 + (3 * c + 1 + k // 2))
                stt(total, pad[:, k:k + T], w[k], total, ALU.mult, ALU.add).then_inc(s_cv, 1)

        def hidden_tile(c, i):
            if conv is None:
                nc.vector.wait_ge(s_sg, i * 4 + (base + c + 1))
            else:
                conv_tile(c, i)
                nc.vector.wait_ge(s_sg, i * 8 + (2 * c + 2))
            tt(hid[:, c % 2, :], sg[:, c % 2, :], ps[c % 2][:, T:2 * T], ALU.mult).then_inc(s_ch, 1)
            nc.vector.wait_ge(s_ch, i * 8 + (cbase + 2 * c + 1))
            nc.vector.tensor_copy(xh[:, c % 2, :], hid[:, c % 2, :]).then_inc(s_ch, 1)
            nc.vector.wait_ge(s_ch, i * 8 + (cbase + 2 * c + 2))
            tt(xl[:, c % 2, :], hid[:, c % 2, :], xh[:, c % 2, :].bitcast(F32), ALU.subtract).then_inc(s_hid, 1)

        for eng, step, split in ((nc.scalar, silu_tile, round_part), (nc.vector, hidden_tile, rest_part)):
            with eng.Fori(0, trips) as i:
                for c in range(4):
                    step(c, i)
                    for kind, ahead in ((0, 2), (1, 2), (2, 1)):
                        split(kind, c + ahead, i)
            step(FT - 2, 0)
            split(2, FT - 1, 0)
            step(FT - 1, 0)
        return PE.last, scope

    def start_engines():
        for e in (PE, A, V, G):
            e.restart()
        unit_at[0] = ffn_at[0] = load_n[0] = 0
        nc.tensor.sem_inc(s_free, SLOTS)
        nc.vector.sem_inc(s_hid, 2)

    def end_stretch():
        nc.all_engine_barrier()
        for s in every_sem:
            nc.gpsimd.sem_clear(s)
        nc.all_engine_barrier()

    def first_steps(stream, n):
        for _ in range(n):
            if next(stream, "end") == "end":
                return
            yield

    def interleave(*streams):
        live = [[stream, rate, 0.0] for stream, rate in streams]
        while live:
            for x in list(live):
                x[2] += x[1]
                while x[2] >= 1:
                    x[2] -= 1
                    if next(x[0], "end") == "end":
                        live.remove(x)
                        break

    def attention(tag, nheads, kt_n, q, k, v, store, scope, scale, score_banks, flip_banks, out_bank, bias=None,
                  sink=None, ready=()):
        width = kt_n * P
        nb = width // T
        pr = sb(f"prob_{tag}", [P, 2, 2, width], scope=scope)
        pT = sb(f"probT_{tag}", [P, 1, kt_n, T], scope=scope)
        st = sb(f"stat_{tag}", [P, 2, 8], scope=scope)
        sets = len(score_banks) // nb
        score_read, flip_read, out_read = [None] * sets, None, None
        prob_read, pT_read, sm = [None] * 2, None, [None] * 2

        def scores(h):
            d, d2 = h % 2, h % sets

            def bank(ti):
                b = score_banks[nb * d2 + (ti if nb == 2 else 0)]
                return b[:, 0:width] if nb == 2 else b[:, ti * width:(ti + 1) * width]

            for ti in range(2):
                m = PE.mm(bank(ti), q(h)[:, ti * P:(ti + 1) * P], k(h), mark=True, after=[score_read[d2], *ready])
            sunk = sink is not None and h < sink.shape[-1]
            biased = bias is not None and bias(h, 0) is not None
            for ti in range(2):
                s = pr[:, d, ti, :]
                b = bias(h, ti) if biased else None
                if b is not None:
                    n = b.shape[-1]
                    V(stt, s[:, 0:n], bank(ti)[:, 0:n], scale, b, ALU.mult, ALU.add, after=[m, prob_read[d]])
                    if n < width:
                        V(ts, s[:, n:width], bank(ti)[:, n:width], scale, None, ALU.mult)
            mx, neg, total, e_sink = (st[:, d, 2 * k2:2 * k2 + 2] for k2 in range(4))
            if biased:
                score_read[d2] = V.last
                yield
                V(nc.vector.tensor_reduce, mx, pr[:, d, :, :], AX.X, ALU.max)
                if sunk:
                    V(ts, mx, mx, sink[:, h:h + 1], None, ALU.max)
            else:
                for ti in range(2):
                    V(nc.vector.tensor_reduce, mx[:, ti:ti + 1], bank(ti), AX.X, ALU.max, after=[m])
            t = V(ts, neg, mx, -1.0 if biased else -scale, None, ALU.mult)
            for ti in range(2):
                e = A(act, pr[:, d, ti, :], pr[:, d, ti, :] if biased else bank(ti), ACT.Exp, bias=neg[:, ti:ti + 1],
                      scale=1.0 if biased else scale, accum_out=total[:, ti:ti + 1], after=[t, prob_read[d]])
            if not biased:
                score_read[d2] = e
            if sunk:
                e = A(act, e_sink, neg, ACT.Exp, bias=sink[:, h:h + 1])
            yield
            if sunk:
                V(tt, total, total, e_sink, ALU.add, after=[e])
            V(nc.vector.reciprocal, total, total, after=[e])
            for ti in range(2):
                sm[d] = V(ts, pr[:, d, ti, :], pr[:, d, ti, :], total[:, ti:ti + 1], None, ALU.mult)

        def finish(h):
            nonlocal flip_read, pT_read, out_read
            d = h % 2
            for kt in range(kt_n):
                bank = flip_banks[kt // 2]
                for ti in range(2):
                    m = PE.flip(bank[:, (kt % 2) * T + ti * P:(kt % 2) * T + (ti + 1) * P], pr[:, d, ti, kt * P:(kt + 1) * P],
                                ident, mark=True, after=[sm[d], flip_read])
            prob_read[d] = m
            yield
            for b in range(kt_n // 2):
                c = A(act, pT[:, 0, 2 * b:2 * b + 2, :], three(flip_banks[b][:, :], 2), ACT.Copy, after=[m, pT_read])
            flip_read = c
            yield
            o = out_bank[0:HD, 0:T]
            for kt in range(kt_n):
                m = PE.mm(o, v(h, kt), pT[:, 0, kt, :], start=kt == 0, stop=kt == kt_n - 1, mark=kt == kt_n - 1,
                          after=[c, out_read])
            pT_read = m
            out_read = A(act, store(h), o, ACT.Copy, after=[m])

        for h in range(nheads + 1):
            if h < nheads:
                yield from scores(h)
                yield
            if h > 0:
                yield from finish(h - 1)
                yield

    for c, v in enumerate((1e-6, 1e-12, 64e-5, 1e-5, 1.0)):
        V(nc.vector.memset, eps[:, c:c + 1], v)
    V(nc.vector.memset, zeros[:, :], 0.0)
    load(c0[:, :], c0_in)
    load(xT[:, :, :], xT_in)
    nc.scalar.wait_ge(s_in, 32)
    end_stretch()

    with nc.Fori(0, DEPTH) as layer:
        start_engines()
        lay = ExitStack()
        pl = sb("pl", [P, LP_N], scope=lay)
        mixT = sb("mixT", [P, KT, T], scope=lay)
        t_pl = load(pl[:, :], p_layers[layer, :, :])
        stream(LAYER_UNITS, lambda u: w_layers[layer, u, :, :])
        for e in (V, PE, A):
            e.wait(t_pl)

        def col(name):
            return pl[:, slice(*LP[name])]

        def half_residual(ran):
            done, scope = ran
            for b in range(4):
                t = V(stt, xT[:, 2 * b:2 * b + 2, :], three(ps[2 + b][:, :], 2), 0.5, xT[:, 2 * b:2 * b + 2, :], ALU.mult, ALU.add, after=[done])
            phase()
            scope.close()
            return t

        half_residual(ffn('ffn1', lambda **kw: rms(xT[:, :, :], hT[:, :, 0:T], col("norm_ffn1"), hT[:, :, T:2 * T], **kw)))

        h_done = []
        rms(xT[:, :, :], hT[:, :, 0:T], col("norm_mix"), hT[:, :, T:2 * T], each=lambda k, t: h_done.append(t))
        mix = ExitStack()
        rkv = sb("rkv", [P, 10, T], scope=mix)
        cr = sb("cr", [P, CL["bias"][0]], scope=mix)
        arh = sb("arh", [HD, NH, 2, 2, P], scope=mix)
        bh = sb("bh", [HD, NH, T], scope=mix)
        kh2 = sb("kh2", [HD, NH, T], scope=mix)
        dch = sb("dch", [HD, NH, NC], scope=mix)
        bonus = sb("bonus", [P, JT, T], scope=mix)
        gate = sb("gate", [P, JT, T], scope=mix)
        m1 = ExitStack()
        bias_sb = sb("bias_sb", [P, NH * 2 * T], scope=m1)
        load(cr[:, :], cl_in[:, 0:CL["bias"][0]])
        t_bias = t_cr = load(bias_sb[:, :], cl_in[:, slice(*CL["bias"])])
        raw = sb("raw", [P, 3, T + 1], scope=m1)
        qk = sb("qk", [P, 2 * JT, T], scope=m1)
        vtok = sb("vtok", [P, 2, NH * HD], scope=m1)
        cz = sb("cz", [P, 2, TAPS - 1 + T], scope=m1)
        cu = sb("cu", [P, 2, T], scope=m1)
        cc = sb("cc", [P, 2, T], scope=m1)
        csq = sb("csq", [P, 2, T], scope=m1)
        qh = hT[0:HD, 0:NH, T:2 * T]
        kh = sb("kh", [HD, NH, T], scope=m1)
        rq = sb("rq", [P, JT, T], scope=m1)
        lo = sb("lo", [P, T], scope=m1)
        sgw = sb("sgw", [P, 2, NH * HD], scope=m1)
        d_in = sb("d_in", [P, JT, T], scope=m1)
        d_ex = sb("d_ex", [P, JT, T], scope=m1)
        d_inv = sb("d_inv", [P, JT, T], scope=m1)
        aT = sb("aT", [P, JT, T], scope=m1)
        kk = sb("kk", [P, JT, T], scope=m1)
        knew = sb("knew", [P, JT, T], scope=m1)
        tmp = rq
        V(nc.vector.memset, raw[:, :, 0:1], 0.0)
        V(nc.vector.memset, cz[:, :, 0:TAPS - 1], 0.0)
        w_at = {}

        def columns(tile):
            if tile // 2 not in w_at:
                w_at[tile // 2] = take_unit()
            return three(w_at[tile // 2][:, :], KT)[:, :, (tile % 2) * P:(tile % 2 + 1) * P]

        proj = {}
        mu = col("mu")

        def project_tiles():
            banks = Banks(ps[0:2])
            raw_read = [None] * 3
            for tile in range(23):
                w = columns(tile)
                at, bank, read = banks.next()
                if 16 <= tile < 19:
                    for ti in range(2):
                        for k in range(KT):
                            m = PE.mm(bank[:, ti * T:ti * T + P], hT[:, k, ti * P:(ti + 1) * P], w[:, k, :],
                                      start=k == 0, stop=k == KT - 1, mark=ti == 1 and k == KT - 1, after=[read])
                    t = A(act, vtok[:, :, (tile - 16) * P:(tile - 15) * P], three(bank[:, :], 2)[:, :, 0:P], ACT.Copy, after=[m])
                else:
                    for k in range(KT):
                        m = PE.mm(bank[:, 0:T], w[:, k, :], hT[:, k, 0:T], start=k == 0, stop=k == KT - 1, mark=k == KT - 1,
                                  after=[read, h_done[k]])
                    if tile < 10:
                        b = tile % 3
                        t = A(act, raw[:, b, 1:T + 1], bank[:, 0:T], ACT.Copy, after=[m, raw_read[b]])
                        V(tt, rkv[:, tile, :], raw[:, b, 0:T], raw[:, b, 1:T + 1], ALU.subtract, after=[t])
                        raw_read[b] = V(stt, rkv[:, tile, :], rkv[:, tile, :], mu[:, tile:tile + 1], raw[:, b, 1:T + 1], ALU.mult, ALU.add)
                    elif tile < 16:
                        t = A(act, qk[:, tile - 10, :], bank[:, 0:T], ACT.Copy, after=[m])
                    elif tile < 21:
                        t = A(act, cu[:, tile - 19, :], bank[:, 0:T], ACT.Copy, after=[m])
                    else:
                        t = A(act, cz[:, tile - 21, TAPS - 1:TAPS - 1 + T], bank[:, 0:T], ACT.Sigmoid, after=[m])
                banks.done(at, t)
                proj[tile] = raw_read[tile % 3] if tile < 10 else t
                if tile % 2 or tile == 22:
                    give_unit()
                yield

        small = Banks(ps[6:8])

        def attend():
            for which, dst, g in ((0, qh, "qn"), (1, kh, "kn")):
                src = qk[:, which * JT:(which + 1) * JT, :]
                sq = A(act, prn, src, ACT.Square, after=[proj[15], t_norm[0]])
                for j in range(JT):
                    at, bank, read = small.next()
                    m = PE.mm(bank[:, 0:T], heads, prn[:, j, :], mark=True, after=[sq, read])
                    t = A(act, prn[:, j, :], bank[:, 0:T], ACT.Ln, bias=EPS6, scale=1.0 / HD, after=[m])
                    small.done(at, t)
                    yield
                V.wait(A(act, prn, prn, ACT.Exp, scale=-0.5))
                for p in range(2):
                    r = slice(p * HD, (p + 1) * HD)
                    t_norm[0] = V(stt, dst[:, p::2, :], src[r, :, :], col(g)[r, :], prn[r, :, :], ALU.mult, ALU.mult)
                yield
            V.wait(t_bias)
            yield from attention("l", NH, 2, lambda h: qh[:, h, :], lambda h: kh[:, h, :], lambda h, kt: vtok[:, kt, h * HD:(h + 1) * HD],
                                 lambda h: mixT[(h % 2) * HD:(h % 2 + 1) * HD, JT + h // 2, :], m1, HD ** -0.5,
                                 [ps[2], ps[3]], [ps[4]], ps[5], bias=lambda h, ti: bias_sb[:, (2 * h + ti) * T:(2 * h + ti + 1) * T],
                                 ready=[t_norm[0], proj[18]])

        prn = sb("prn", [P, JT, T], scope=m1)[:, :, :]
        t_norm = [None]

        def convolve():
            V(tt, cz[:, :, TAPS - 1:], cz[:, :, TAPS - 1:], cu[:, :, :], ALU.mult, after=[proj[22]])
            for j in range(2):
                w = col("conv_w")[:, j * TAPS:(j + 1) * TAPS]
                t = V(ts, cc[:, j, :], cz[:, j, 0:T], w[:, 0:1], col("conv_b")[:, j:j + 1], ALU.mult, ALU.add)
                for k in range(1, TAPS):
                    t = V(stt, cc[:, j, :], cz[:, j, k:k + T], w[:, k:k + 1], cc[:, j, :], ALU.mult, ALU.add)
                    if k % 3 == 0:
                        yield
            for step in range(2):
                if step:
                    t = A(act, csq[:, :, :], cc[:, :, :], ACT.Square, after=[t])
                src = csq if step else cc
                at, bank, read = small.next()
                for j in range(2):
                    m = PE.mm(bank[:, 0:T], ones, src[:, j, :], start=j == 0, stop=j == 1, mark=j == 1, after=[t, read])
                if step == 0:
                    for j in range(2):
                        t = V(stt, cc[:, j, :], bank[:, 0:T], -1.0 / (2 * P), cc[:, j, :], ALU.mult, ALU.add, after=[m])
                    small.done(at, t)
                yield
            t = A(act, rstd[:, :], bank[:, 0:T], ACT.Sqrt, bias=EPSC, scale=1.0 / (2 * P), after=[m])
            small.done(at, t)
            V(nc.vector.reciprocal, rstd[:, :], rstd[:, :], after=[t])
            for j in range(2):
                t = V(stt, cc[:, j, :], cc[:, j, :], col("cln_w")[:, j:j + 1], rstd[:, :], ALU.mult, ALU.mult)
                A(act, mixT[:, 2 * JT + j, :], cc[:, j, :], ACT.Silu, bias=col("cln_b")[:, j:j + 1], after=[t])

        def prepare():
            lora = col("lora")
            r_, k_, v_ = (rkv[:, j * JT:(j + 1) * JT, :] for j in range(3))
            V.wait(t_cr)
            PE.wait(t_cr)
            A(act, lo[0:32, :], rkv[0:32, 9, :], ACT.Tanh, after=[proj[9]])
            A(act, lo[32:64, :], rkv[32:64, 9, :], ACT.Copy)
            t_lo = A(act, lo[64:128, :], rkv[64:128, 9, :], ACT.Sigmoid)
            for ti in range(2):
                at, bank, read = small.next()
                m = PE.mm(bank[:, 0:NH * HD], lo[0:32, ti * P:(ti + 1) * P], lora[0:32, :], mark=True, after=[t_lo, read])
                t = V(tt, sgw[:, ti, :], bank[:, 0:NH * HD], col("w0"), ALU.add, after=[m])
                small.done(at, t)
            yield
            for j in range(JT):
                t_kk = V(ts, kk[:, j, :], k_[:, j, :], col("k_k")[:, j:j + 1], None, ALU.mult)
            t_sg = A(act, sgw[:, :, :], sgw[:, :, :], ACT.Sigmoid, after=[t])
            for j in range(JT):
                at, bank, read = small.next()
                m = PE.mm(bank[:, 0:T], lora[32:64, j * P:(j + 1) * P], lo[32:64, :], mark=True, after=[read])
                t_a = A(act, aT[:, j, :], bank[:, 0:T], ACT.Sigmoid, bias=col("a0")[:, j:j + 1], after=[m])
                small.done(at, t_a)
                yield
            for j in range(JT):
                at, bank, read = small.next()
                m = PE.mm(bank[:, 0:T], lora[64:128, j * P:(j + 1) * P], lo[64:128, :], mark=True, after=[read])
                small.done(at, A(act, gate[:, j, :], bank[:, 0:T], ACT.Copy, after=[m]))
                yield
            for j in range(JT):
                at, bank, read = small.next()
                for ti in range(2):
                    m = PE.mm(bank[:, ti * T:(ti + 1) * T], sgw[:, ti, j * P:(j + 1) * P], cr[:, 0:T], mark=True, after=[t_sg, read])
                cum = bank[:, :].rearrange("p (t e s) -> p e t s", t=2, e=2)
                for dst, e, sign in ((d_in, 0, 1.0), (d_ex, 1, 1.0), (d_inv, 0, -1.0)):
                    t_d = A(act, three(dst[:, j, :], 2), cum[:, e, :, :], ACT.Exp, scale=sign, after=[m])
                small.done(at, t_d)
                yield
            t = A(act, tmp[:, :, :], kk[:, :, :], ACT.Square, after=[t_kk])
            for j in range(JT):
                at, bank, read = small.next()
                m = PE.mm(bank[:, 0:T], heads, tmp[:, j, :], mark=True, after=[t, read])
                t2 = A(act, tmp[:, j, :], bank[:, 0:T], ACT.Ln, bias=EPS12, after=[m])
                small.done(at, t2)
                yield
            t = A(act, tmp[:, :, :], tmp[:, :, :], ACT.Exp, scale=-0.5)
            V(tt, kk[:, :, :], kk[:, :, :], tmp[:, :, :], ALU.mult, after=[t])
            yield
            for j in range(JT):
                V(ts, knew[:, j, :], aT[:, j, :], 1.0, col("k_a")[:, j:j + 1], ALU.subtract, ALU.mult, after=[t_a])
            V(stt, knew[:, :, :], knew[:, :, :], 1.0, k_, ALU.add, ALU.mult)
            yield
            for j in range(JT):
                t = V(stt, tmp[:, j, :], r_[:, j, :], col("r_k")[:, j:j + 1], knew[:, j, :], ALU.mult, ALU.mult)
            yield
            for j in range(JT):
                at, bank, read = small.next()
                m = PE.mm(bank[:, 0:T], heads, tmp[:, j, :], mark=True, after=[t, read])
                small.done(at, V(tt, bonus[:, j, :], v_[:, j, :], bank[:, 0:T], ALU.mult, after=[m]))
                yield
            V(tt, d_ex[:, :, :], kk[:, :, :], d_ex[:, :, :], ALU.mult, after=[t_d])
            V(stt, kk[:, :, :], kk[:, :, :], -1.0, aT[:, :, :], ALU.mult, ALU.mult)
            for p in range(2):
                yield
                r = slice(p * HD, (p + 1) * HD)
                tiles = [ap[r, :, :].rearrange("p j (t s) -> p j t s", t=2) for ap in (d_ex, r_, d_in)]
                V(nc.vector.tensor_copy, arh[:, p::2, :, 0, :], tiles[0])
                V(tt, arh[:, p::2, :, 1, :], tiles[1], tiles[2], ALU.mult)
                V(nc.vector.tensor_copy, dch[:, p::2, :], d_in[r, :, :].rearrange("p j (c s) -> p j c s", c=NC)[:, :, :, CH - 1])
                yield
                V(tt, bh[:, p::2, :], kk[r, :, :], d_inv[r, :, :], ALU.mult)
                V(tt, kh2[:, p::2, :], knew[r, :, :], d_inv[r, :, :], ALU.mult)

        tiles = project_tiles()
        for _ in range(10):
            next(tiles)
        prep = prepare()
        interleave((tiles, 1), (first_steps(prep, 26), 2))
        interleave((attend(), 2), (convolve(), 1), (prep, 1))
        phase()
        m1.close()

        m4 = ExitStack()
        mb = sb("mb", [P, NPROB, 2 * P], scope=m4)
        mk = sb("mk", [P, NPROB, 2 * P], scope=m4)
        lw = sb("lw", [P, NPROB, P], scope=m4)
        yi = sb("yi", [P, NPROB, P], scope=m4)
        xi = sb("xi", [P, NPROB, P], scope=m4)
        yT = sb("yT", [HD, NH, T], scope=m4)
        state = sb("state", [HD, NH, HD], scope=m4)
        gs = sb("gs", [P, NH * HD], scope=m4)
        us = sb("us", [P, NH * HD], scope=m4)
        flat = hT[:, :, :].rearrange("p a b -> p (a b)")
        lev = three(flat[:, 0:NPROB * P], NPROB)
        pr1 = three(flat[:, NPROB * P:2 * NPROB * P], NPROB)
        both = cr[:, CL["strict"][0]:CL["incl"][1]]
        level = [cr[:, CL["level"][0] + k * P:CL["level"][0] + (k + 1) * P] for k in range(6)]
        V(nc.vector.memset, gs[:, :], 0.0)
        V(nc.vector.memset, us[:, :], 0.0)
        btok = sb("btok", [P, 2, NH * HD], scope=m4)
        ktok = sb("ktok", [P, 2, NH * HD], scope=m4)
        vtk = sb("vtk", [P, 2, NH * HD], scope=m4)
        banks = Banks(ps[0:8])

        def token_major():
            for ti in range(2):
                t_s = slice(ti * P, (ti + 1) * P)
                for src, dst in ((None, vtk), (bh, btok), (kh2, ktok)):
                    at, bank, read = banks.next()
                    if src is not None:
                        for h_i in range(NH):
                            m = PE.flip(bank[:, h_i * HD:(h_i + 1) * HD], src[:, h_i, t_s], ident[0:HD, 0:HD], mark=h_i == NH - 1, after=[read])
                    else:
                        for j in range(JT):
                            m = PE.flip(bank[:, j * P:(j + 1) * P], rkv[:, 2 * JT + j, t_s], ident, mark=j == JT - 1, after=[read])
                    banks.done(at, A(act, dst[:, ti, :], bank[:, 0:NH * HD], ACT.Copy, after=[m]))
                    yield

        w_out = [three(take_unit()[:, :], KT) for _ in range(4)]

        def out_projection(tiles, give=False):
            for m_i in range(KT):
                at, bank, read = banks.next()
                for k in tiles:
                    m = PE.mm(bank[:, 0:T], w_out[m_i // 2][:, k, (m_i % 2) * P:(m_i % 2 + 1) * P], mixT[:, k, :],
                              start=k == tiles[0], stop=k == tiles[-1], mark=k == tiles[-1], after=[read])
                banks.done(at, V(tt, xT[:, m_i, :], bank[:, 0:T], xT[:, m_i, :], ALU.add, after=[m]))
                if give and m_i % 2:
                    give_unit()
                yield

        early = out_projection(range(JT, KT))
        copies = token_major()
        for b in range(NPROB // 2):
            for src, dst in ((bh, mb), (kh2, mk)):
                at, bank, read = banks.next()
                for q in range(2):
                    h_i, ti = divmod(2 * b + q, 2)
                    m = PE.mm(bank[:, q * T:(q + 1) * T], src[:, h_i, ti * P:(ti + 1) * P], arh[:, h_i, ti, :, :], mark=q == 1, after=[read])
                banks.done(at, V(tt, dst[:, 2 * b:2 * b + 2, :], three(bank[:, :], 2), wide(both, [P, 2, T]), ALU.mult, after=[m]))
            if b % 2:
                next(early)
        for b in range(NPROB // 4):
            at, bank, read = banks.next()
            for q in range(4):
                h_i, ti = divmod(4 * b + q, 2)
                m = PE.mm(bank[:, q * P:(q + 1) * P], arh[:, h_i, ti, 0, :], bh[:, h_i, ti * P:(ti + 1) * P], mark=q == 3, after=[read])
            banks.done(at, A(act, lw[:, 4 * b:4 * b + 4, :], three(bank[:, :], 4), ACT.Copy, after=[m]))

        quad = [P, 4, P]
        built, added = [None] * 3, [None] * 3
        for b in range(3):
            s = slice(4 * b, 4 * b + 4)
            V(tt, xi[:, s, :], lw[:, s, :], wide(level[0], quad), ALU.mult, after=[A.last])
            V(tt, xi[:, s, :], xi[:, s, :], wide(ident, quad), ALU.add)
            V(tt, yi[:, s, :], mb[:, s, 0:P], wide(cr[:, slice(*CL["first"])], quad), ALU.mult)
            added[b] = V(tt, yi[:, s, :], yi[:, s, :], wide(ident, quad), ALU.add)
        for k in range(1, 6):
            for b in range(3):
                s = slice(4 * b, 4 * b + 4)
                t_lev = V(tt, lev[:, s, :], lw[:, s, :], wide(level[k], quad), ALU.mult, after=[built[b]])
                at, bank, read = banks.next()
                for q in range(4):
                    n = 4 * b + q
                    m = PE.mm(bank[:, q * P:(q + 1) * P], lev[:, n, :], yi[:, n, :], mark=q == 3, after=[read, t_lev, added[b]])
                built[b] = A(act, pr1[:, s, :], three(bank[:, :], 4), ACT.Copy, after=[m])
                banks.done(at, built[b])
            next(copies, None)
            next(early, None)
            w = 1 << k

            def blocks(ap, dst):
                return ap.rearrange("p (b e s) -> p b e s", e=2, s=w)[:, :, 1 if dst is yi else 0, :]

            for b in range(3):
                s = slice(4 * b, 4 * b + 4)
                got = []
                for dst in (yi, xi) if k < 5 else (yi,):
                    at, bank, read = banks.next()
                    for q in range(4):
                        n = 4 * b + q
                        l, r = (xi[:, n, :], pr1[:, n, :]) if dst is yi else (pr1[:, n, :], xi[:, n, :])
                        m = PE.mm(bank[:, q * CH:(q + 1) * CH], l, blocks(r, dst), mark=q == 3, after=[read, built[b]])
                    got.append((at, bank, dst))
                built[b] = m
                for at, bank, dst in got:
                    part = blocks(dst[:, s, :].rearrange("p q c -> p (q c)"), dst)
                    added[b] = V(tt, part, bank[:, 0:4 * CH].rearrange("p (b s) -> p b s", s=w), part, ALU.add, after=[m])
                    banks.done(at, added[b])

        for rest in (copies, early):
            for _ in rest:
                pass

        PE.wait(A.last)
        y_read = [None] * 2
        for c in range(NC):
            ti, r = c // 2, slice((c % 2) * CH, (c % 2 + 1) * CH)
            rr = slice(P + r.start, P + r.stop)
            g_ps, u_ps, y_ps, s_ps = ps[0:4] if c % 2 == 0 else ps[4:8]
            for h_i in range(NH):
                n, o = 2 * h_i + ti, slice(h_i * HD, (h_i + 1) * HD)
                if c:
                    PE.mm(g_ps[r, o], arh[:, h_i, ti, 0, r], state[:, h_i, :], start=True, stop=False, after=[V.last])
                m = PE.mm(g_ps[r, o], mk[:, n, r], vtk[:, ti, o], start=c == 0, stop=True, mark=h_i == NH - 1, after=[V.last])
            t = V(nc.vector.tensor_copy, gs[r, :], g_ps[r, 0:NH * HD], after=[m])
            for h_i in range(NH):
                n, o = 2 * h_i + ti, slice(h_i * HD, (h_i + 1) * HD)
                m = PE.mm(u_ps[r, o], yi[:, n, r], gs[:, o], mark=h_i == NH - 1, after=[t])
            t = V(nc.vector.tensor_copy, us[r, :], u_ps[r, 0:NH * HD], after=[m])
            PE.wait(y_read[c % 2])
            if c < NC - 1:
                for h_i in range(NH):
                    o = slice(h_i * HD, (h_i + 1) * HD)
                    PE.mm(s_ps[0:HD, o], btok[r, ti, o], us[r, o], start=True, stop=False, after=[t])
                    m = PE.mm(s_ps[0:HD, o], ktok[r, ti, o], vtk[r, ti, o], start=False, stop=True, mark=h_i == NH - 1)
            for h_i in range(NH):
                n, o = 2 * h_i + ti, slice(h_i * HD, (h_i + 1) * HD)
                y_o = y_ps[0:HD, h_i * CH:(h_i + 1) * CH]
                if c:
                    PE.mm(y_o, state[:, h_i, :], arh[:, h_i, ti, 1, r], start=True, stop=False)
                PE.mm(y_o, us[:, o], mb[:, n, rr], start=c == 0, stop=False, after=[t])
                my = PE.mm(y_o, vtk[:, ti, o], mk[:, n, rr], start=False, stop=True, mark=h_i == NH - 1)
            y_read[c % 2] = A(act, yT[:, :, c * CH:(c + 1) * CH], three(y_ps[0:HD, 0:NH * CH], NH), ACT.Copy, after=[my])
            if c < NC - 1:
                s3 = three(s_ps[0:HD, 0:NH * HD], NH)
                decay = dch[:, :, c:c + 1].to_broadcast([HD, NH, HD])
                if c:
                    V(tt, state[:, :, :], s3, state[:, :, :], ALU.add, after=[m, my])
                    V(tt, state[:, :, :], state[:, :, :], decay, ALU.mult)
                else:
                    V(tt, state[:, :, :], s3, decay, ALU.mult, after=[m])

        yf = yT[:, :, :].rearrange("p a b -> p (a b)")
        sqf = flat[0:HD, 0:NH * T]
        for b in range(3):
            s = slice(b * 512, (b + 1) * 512)
            m = PE.mm(ps[b][0:HD, :], heads[0:HD, 0:HD], yf[:, s], mark=True, after=[A.last, V.last])
            V(stt, yf[:, s], ps[b][0:HD, :], -1.0 / HD, yf[:, s], ALU.mult, ALU.add, after=[m])
        A(act, sqf, yf, ACT.Square, after=[V.last])
        for b in range(3):
            s = slice(b * 512, (b + 1) * 512)
            m = PE.mm(ps[3 + b][0:HD, :], heads[0:HD, 0:HD], sqf[:, s], mark=True, after=[A.last])
            A(act, sqf[:, s], ps[3 + b][0:HD, :], ACT.Ln, bias=EPSG[0:HD, :], scale=1.0 / HD, after=[m])
        t = A(act, sqf, sqf, ACT.Exp, scale=-0.5)
        V(tt, yf, yf, sqf, ALU.mult, after=[t])
        for h_i in range(NH):
            r = slice((h_i % 2) * HD, (h_i % 2 + 1) * HD)
            V(ts, mixT[r, h_i // 2, :], yT[:, h_i, :], col("ln_w")[0:HD, h_i:h_i + 1], col("ln_b")[0:HD, h_i:h_i + 1], ALU.mult, ALU.add)
        V(tt, mixT[:, 0:JT, :], mixT[:, 0:JT, :], bonus[:, :, :], ALU.add)
        h = V(tt, mixT[:, 0:JT, :], mixT[:, 0:JT, :], gate[:, :, :], ALU.mult)
        phase()
        m4.close()
        mix.close()

        for _ in out_projection(range(JT), give=True):
            pass

        residual = V.last
        half_residual(ffn('ffn2', lambda **kw: rms(xT[:, :, :], hT[:, :, 0:T], col("norm_ffn2"), hT[:, :, T:2 * T], after=[residual], **kw)))
        phase()
        lay.close()
        end_stretch()

    start_engines()
    pp = sb("pp", [P, SP2_N])
    cs = sb("cs", [P, CS_N])
    sc = sb("sc", [P, 16])
    mod = sb("mod", [P, 48])
    cmod = sb("cmod", [P, 16])
    scale_x = sb("scale_x", [P, KT])
    scale_c = sb("scale_c", [P, KT])
    scale_2 = sb("scale_2", [P, KT])
    cx = ExitStack()
    ctxT = sb("ctxT", [P, KT, T], scope=cx)
    sq8 = sb("sq8", [P, KT, T], scope=cx)
    load(pp[:, :], p_last)
    load(cs[:, :], cs_in)
    t_in = load(ctxT[:, :, :], ctxT_in)
    stream(LAST_UNITS, lambda u: w_last[u, :, :])
    for e in (V, PE, A):
        e.wait(t_in)

    def col2(name):
        return pp[:, slice(*SP2[name])]

    def const(name):
        return cs[:, slice(*CS[name])]

    t = A(act, sc[:, :], col2("c"), ACT.Silu)
    rows = sb("rows", [2, 2, T], scope=cx)
    banks, row_read, before = Banks(ps[1:5]), [None] * 2, None

    def flip_rows(u, row, t_copy):
        for j in range(2):
            o = 2 * (2 * u + j)
            row_read[row] = PE.flip(ps[0][:, o:o + 2], rows[:, row, j * P:(j + 1) * P], ident[0:2, 0:2], mark=True, after=[t_copy])

    summed, summed_read = sb("summed", [P, 2, T], scope=cx), [None] * 2
    V.wait(t)
    for u in range(24):
        w = three(take_unit()[:, :], KT)
        at, bank, read = banks.next()
        if u >= 8 and u % 2:
            b = u // 2 % 2
            landed = (s_slot[(unit_at[0] - 1) % SLOTS], 16 * ((unit_at[0] - 1) // SLOTS + 1))
            V(ts, summed[:, b, :], w[:, 0, :], sc[:, 0:1], None, ALU.mult, after=[landed, summed_read[b]])
            for k in range(1, KT):
                t_sum = V(stt, summed[:, b, :], w[:, k, :], sc[:, 2 * k:2 * k + 1], summed[:, b, :], ALU.mult, ALU.add)
            m = summed_read[b] = PE.mm(bank[0:2, 0:T], ones[:, 0:2], summed[:, b, :], mark=True, after=[read, t_sum])
        else:
            for k in range(KT):
                m = PE.mm(bank[0:2, 0:T], sc[:, 2 * k:2 * k + 2], w[:, k, :], start=k == 0, stop=k == KT - 1, mark=k == KT - 1,
                          after=[read, t])
        give_unit()
        t_copy = A(act, rows[:, u % 2, :], bank[0:2, 0:T], ACT.Copy, after=[m, row_read[u % 2]])
        banks.done(at, t_copy)
        if before:
            flip_rows(*before)
        before = (u, u % 2, t_copy)
    flip_rows(*before)
    m = PE.last
    mod_ps = ps[0][:, 0:96].rearrange("p (a b) -> p a b", b=2)
    V(tt, mod[:, :], mod_ps[:, :, 0], col2("b_mod"), ALU.add, after=[m])
    V(tt, cmod[:, :], mod_ps[:, 0:16, 1], col2("b_mod")[:, 0:16], ALU.add)
    shift1, gate1, shift2, gate2 = mod[:, 0:8], mod[:, 16:24], mod[:, 24:32], mod[:, 40:48]
    V(stt, scale_x[:, :], mod[:, 8:16], 1.0, col2("norm1"), ALU.add, ALU.mult)
    V(stt, scale_c[:, :], cmod[:, 8:16], 1.0, col2("norm1"), ALU.add, ALU.mult)
    V(stt, scale_2[:, :], mod[:, 32:40], 1.0, col2("norm2"), ALU.add, ALU.mult)
    rms(xT[:, :, :], hT[:, :, 0:T], scale_x, sq8[:, :, :], shift=shift1)
    h = rms(ctxT[:, :, :], hT[:, :, T:2 * T], scale_c, sq8[:, :, :], shift=cmod[:, 0:8], after=[PE.last])
    phase()
    cx.close()

    branches, ssd, atn, s2 = ExitStack(), ExitStack(), ExitStack(), ExitStack()
    yaT = sb("yaT", [P, 4, T], scope=branches)
    ygT = sb("ygT", [P, 4, T], scope=branches)
    bT = sb("bT", [P, 2, T], scope=ssd)
    cT = sb("cT", [P, 2, T], scope=ssd)
    xs = sb("xs", [P, 2, DM], scope=ssd)
    dt = sb("dt", [P, 4, 32], scope=ssd)
    da = sb("da", [P, 4, 32], scope=ssd)
    acs = sb("acs", [P, 4, 32], scope=ssd)
    eac = sb("eac", [P, 4, 32], scope=ssd)
    h0 = sb("h0", [P, 2, DM], scope=ssd)
    def project(dst_bank, w, width, after, mark=True):
        for k in range(KT):
            m = PE.mm(dst_bank[:, 0:width], w[:, k, :], hT[:, k, 0:width], start=k == 0, stop=k == KT - 1, mark=k == KT - 1, after=after)
        return m

    def half(w, j):
        return w[:, :, j * P:(j + 1) * P]

    kr = sb("kr", [P, 2, 2 * T], scope=atn)
    vt2 = sb("vt2", [P, 4, 2 * P], scope=atn)
    q8 = sb("q8", [P, 8, T], scope=atn)
    ready_q, ready_k = [None] * 8, [None] * 2
    banks = Banks(ps[0:6])
    w = three(take_unit()[:, :], KT)
    for j in range(2):
        at, bank, read = banks.next()
        m = project(bank, half(w, j), 2 * T, [read, h])
        ready_k[j] = A(act, kr[:, j, :], bank[:, :], ACT.Copy, after=[m])
        banks.done(at, ready_k[j])
    give_unit()
    w = three(take_unit()[:, :], KT)
    for ti in range(4):
        at, bank, read = banks.next()
        for k in range(KT):
            m = PE.mm(bank[:, 0:2 * P], hT[:, k, ti * P:(ti + 1) * P], w[:, k, :], start=k == 0, stop=k == KT - 1, mark=k == KT - 1, after=[read])
        banks.done(at, A(act, vt2[:, ti, :], bank[:, 0:2 * P], ACT.Copy, after=[m]))
    give_unit()
    for j in range(8):
        if j % 2 == 0:
            w = three(take_unit()[:, :], KT)
        at, bank, read = banks.next()
        m = project(bank, half(w, j % 2), T, [read])
        ready_q[j] = A(act, q8[:, j, :], bank[:, 0:T], ACT.Copy, after=[m])
        banks.done(at, ready_q[j])
        if j % 2:
            give_unit()

    qs = sb("qs", [HD, 16, T], scope=atn)
    ks = sb("ks", [HD, 4, 2 * T], scope=atn)
    nrm = sb("nrm", [P, 2, 512], scope=atn)
    rtmp = sb("rtmp", [P, 2, T], scope=atn)

    def attend_both():
        pair, nrm_read = Banks(ps[0:2]), [None] * 2
        for j in (4, 0, 1, 2, 3):
            grid_q = j < 4
            src, width = (q8[:, 4 + j, :], T) if grid_q else (kr[:, 1, :], 2 * T)
            buf = nrm[:, j % 2, 0:width]
            t = A(act, buf, src, ACT.Square, after=[nrm_read[j % 2], ready_q[4 + j] if grid_q else ready_k[1]])
            at, bank, read = pair.next()
            m = PE.mm(bank[:, 0:width], heads, buf, mark=True, after=[t, read])
            t = A(act, buf, bank[:, 0:width], ACT.Sqrt, bias=EPS6, scale=1.0 / HD, after=[m])
            pair.done(at, t)
            V(nc.vector.reciprocal, buf, buf, after=[t])
            nrm_read[j % 2] = V(stt, src, src, col2("qn" if grid_q else "kn"), buf, ALU.mult, ALU.mult)
            if grid_q:
                ready_q[4 + j] = V.last
            else:
                ready_k[1] = V.last
            yield
        for j in range(10):
            src, ready = (q8[:, j, :], ready_q[j]) if j < 8 else (kr[:, j - 8, 0:T], ready_k[j - 8])
            turned = rtmp[:, j % 2, :]
            at, bank, read = pair.next()
            m = PE.mm(bank[:, 0:T], const("rot"), src, mark=True, after=[ready, read])
            pair.done(at, V(tt, turned, bank[:, 0:T], const("sin"), ALU.mult, after=[m]))
            V(tt, src, src, const("cos"), ALU.mult)
            for p in range(2):
                r = slice(p * HD, (p + 1) * HD)
                dst = qs[:, 2 * j + p, :] if j < 8 else ks[:, 2 * (j - 8) + p, 0:T]
                t = V(tt, dst, src[r, :], turned[r, :], ALU.add)
                if j >= 8:
                    t = V(nc.vector.tensor_copy, ks[:, 2 * (j - 8) + p, T:2 * T], kr[r, j - 8, T:2 * T])
            yield
        yield from attention("both", 16, 4, lambda h_i: qs[:, h_i, :], lambda h_i: ks[:, h_i // 4, :],
                             lambda h_i, kt: vt2[:, kt, (h_i // 4) * HD:(h_i // 4 + 1) * HD],
                             lambda h_i: (yaT if h_i < 8 else ygT)[(h_i % 2) * HD:(h_i % 2 + 1) * HD, h_i % 8 // 2, :],
                             s2, HD ** -0.5, ps[0:2], ps[2:4], ps[4],
                             bias=lambda h_i, ti: const("window")[:, ti * T:(ti + 1) * T] if h_i < 8 else None,
                             sink=col2("sink"), ready=[t])

    xc = sb("xc", [P, 2, DM], scope=s2)
    bc = sb("bc", [P, 2, 2 * P], scope=s2)
    cpad = sb("cpad", [P, 2, 2, T + 2], scope=s2)
    cout = sb("cout", [P, 2, 2, T], scope=s2)
    dtmp = sb("dtmp", [P, 3, 128], scope=s2)
    xw = sb("xw", [P, DM], scope=s2)
    acoef = sb("acoef", [P, 32], scope=s2)
    dec = sb("dec", [P, 2, 32], scope=s2)
    order = [three(const("fwd"), 2), three(const("bwd"), 2)]
    t_zero = V(nc.vector.memset, cpad[:, :, :, :], 0.0)

    def state_space():
        read_pad, read_out = [t_zero] * 2, [None] * 2
        banks, flip_read = Banks(ps[5:7]), None
        for j in range(12):
            d = j % 2
            if j % 2 == 0:
                w = three(take_unit()[:, :], KT)
            at, bank, read = banks.next()
            for k in range(KT):
                m = PE.mm(bank[:, :], half(w, d)[:, k, :], hT[:, k, :], start=k == 0, stop=k == KT - 1, mark=k == KT - 1, after=[read])
                if k % 2:
                    yield
            if d:
                give_unit()
            t = A(act, cpad[:, d, :, 1:T + 1], three(bank[:, :], 2), ACT.Copy, after=[m, read_pad[d]])
            banks.done(at, t)
            cw = [col2("conv_w")[:, 3 * j + k:3 * j + k + 1] for k in range(3)]
            V(ts, cout[:, d, :, :], cpad[:, d, :, 1:T + 1], cw[1], col2("conv_b")[:, j:j + 1], ALU.mult, ALU.add, after=[t, read_out[d]])
            V(stt, cout[:, d, :, :], cpad[:, d, :, 0:T], cw[0], cout[:, d, :, :], ALU.mult, ALU.add)
            t = read_pad[d] = V(stt, cout[:, d, :, :], cpad[:, d, :, 2:T + 2], cw[2], cout[:, d, :, :], ALU.mult, ALU.add)
            yield
            if j < 8:
                for ti in range(4):
                    m = PE.flip(ps[7][:, ti * P:(ti + 1) * P], cout[:, d, ti // 2, (ti % 2) * P:(ti % 2 + 1) * P], ident, mark=ti == 3,
                                after=[t, flip_read])
                read_out[d] = m
                A(act, xs[:, :, j * P:(j + 1) * P], three(ps[7][:, :], 4)[:, 0:2, :], ACT.Copy, after=[m])
                flip_read = A(act, xc[:, :, j * P:(j + 1) * P], three(ps[7][:, :], 4)[:, 2:4, :], ACT.Copy)
            elif j < 10:
                A(act, bT[:, j - 8, :], cout[:, d, 0, :], ACT.Copy, after=[t])
                for ti in range(2):
                    m = PE.flip(ps[7][:, ti * P:(ti + 1) * P], cout[:, d, 1, ti * P:(ti + 1) * P], ident, mark=ti == 1, after=[t, flip_read])
                flip_read = read_out[d] = A(act, bc[:, :, (j - 8) * P:(j - 7) * P], three(ps[7][:, 0:T], 2), ACT.Copy, after=[m])
            else:
                read_out[d] = A(act, cT[:, j - 10, :], cout[:, d, 0, :], ACT.Copy, after=[t])
            yield
        w_dt = three(col2("w_dt"), KT)
        at, bank, read = banks.next()
        for ti in range(4):
            for k in range(KT):
                m = PE.mm(bank[:, ti * 32:(ti + 1) * 32], hT[:, k, ti * P:(ti + 1) * P], w_dt[:, k, :], start=k == 0, stop=k == KT - 1,
                          mark=ti == 3 and k == KT - 1, after=[read])
        dt_f = dt[:, :, :].rearrange("p a b -> p (a b)")
        e_, u_, l_ = dtmp[:, 0, :], dtmp[:, 1, :], dtmp[:, 2, :]
        banks.done(at, V(tt, dt[:, :, :], three(bank[:, 0:128], 4), wide(col2("dt_bias"), [P, 4, 32]), ALU.add, after=[m]))
        t = V(stt, e_, dt_f, -1.0, dt_f, ALU.mult, ALU.max)
        t = A(act, e_, e_, ACT.Exp, scale=-1.0, after=[t])
        t_coef = A(act, acoef[:, :], col2("a_log"), ACT.Exp)
        yield
        V(ts, u_, e_, 2.0, None, ALU.add, after=[t])
        V(nc.vector.reciprocal, u_, u_)
        V(tt, u_, u_, e_, ALU.mult)
        V(tt, e_, u_, u_, ALU.mult)
        V(ts, l_, e_, 1.0 / 15, None, ALU.mult)
        yield
        for n in (13, 11, 9, 7, 5, 3):
            V(stt, l_, l_, 1.0 / n, e_, ALU.add, ALU.mult)
        yield
        V(stt, l_, l_, 1.0, u_, ALU.add, ALU.mult)
        V(ts, l_, l_, 2.0, None, ALU.mult)
        V(stt, dt_f, dt_f, 0.0, l_, ALU.max, ALU.add)
        t = V(stt, da[:, :, :], dt[:, :, :], -1.0, wide(acoef[:, :], [P, 4, 32]), ALU.mult, ALU.mult, after=[t_coef])
        yield
        at, bank, read = banks.next()
        for g in range(2):
            for ti in range(2):
                for d in range(2):
                    o = (2 * g + ti) * 32 + d * 16
                    for st in range(2):
                        m = PE.mm(bank[:, o:o + 16], order[d][:, st, ti * P:(ti + 1) * P], da[:, 2 * g + st, d * 16:(d + 1) * 16],
                                  start=st == 0, stop=st == 1, mark=True, after=[t, read])
        for st in range(2):
            m = PE.mm(bank[:, 128:160], ones, da[:, 2 + st, :], start=st == 0, stop=st == 1, mark=st == 1)
        t_acs = V(nc.vector.tensor_copy, acs[:, :, :], three(bank[:, 0:128], 4), after=[m])
        for ti in range(2):
            t = V(tt, dec[:, ti, :], bank[:, 128:160], acs[:, 2 + ti, :], ALU.subtract)
        banks.done(at, t)
        t = A(act, dec[:, :, :], dec[:, :, :], ACT.Exp, after=[t])
        A(act, eac[:, :, :], acs[:, :, :], ACT.Exp, after=[t_acs])
        V(tt, dec[:, :, :], dec[:, :, :], dt[:, 2:4, :], ALU.mult, after=[t])
        yield
        for part in (xc, bc, bT, cT, xs):
            t = A(act, part[:, :, :], part[:, :, :], ACT.Silu)
            if part is bc:
                t_xc = t
        yield
        xw_read = None
        for d in range(2):
            got = [banks.next() for _ in range(2)]
            for ti in range(2):
                t = V(tt, three(xw[:, :], 16), three(xc[:, ti, :], 16), dec[:, ti, d * 16:(d + 1) * 16].unsqueeze(2).to_broadcast([P, 16, HD]),
                      ALU.mult, after=[xw_read, t_xc])
                for g, (at, bank, read) in enumerate(got):
                    xw_read = PE.mm(bank[:, :], bc[:, ti, g * P:(g + 1) * P], xw[:, g * 512:(g + 1) * 512], start=ti == 0, stop=ti == 1,
                                    mark=True, after=[read, t])
                yield
            for g, (at, bank, read) in enumerate(got):
                banks.done(at, A(act, h0[:, d, g * 512:(g + 1) * 512], bank[:, :], ACT.Copy, after=[xw_read]))
            yield

    interleave((attend_both(), 1), (state_space(), 1))
    phase()
    s2.close()
    atn.close()

    ysT = sb("ysT", [P, KT, T], scope=ssd)
    gates = sb("gates", [P, 24, T], scope=ssd)
    s3_ = ExitStack()
    zs = sb("zs", [P, 2, DM], scope=s3_)
    st4 = sb("st4", [P, 4], scope=s3_)
    y = sb("y", [P, 2, DM], scope=s3_)
    cbm = sb("cbm", [P, 2, 2, 2 * T], scope=s3_)
    xdt = sb("xdt", [P, 2, 2, DM], scope=s3_)
    arow2 = sb("arow2", [32, 2, T], scope=s3_)
    lm = sb("lm", [P, 2, 2, T], scope=s3_)
    off = sb("off", [P, 512], scope=s3_)
    t_z, t_gates = [], []

    def gate_projections():
        banks = Banks([ps[4], ps[7]])
        for u in range(4):
            w = three(take_unit()[:, :], KT)
            for ti in range(2):
                at, bank, read = banks.next()
                for k in range(KT):
                    m = PE.mm(bank[:, 0:T], hT[:, k, ti * P:(ti + 1) * P], w[:, k, :], start=k == 0, stop=k == KT - 1, mark=k == KT - 1,
                              after=[read])
                    if k % 4 == 3:
                        yield
                t_z.append(A(act, zs[:, ti, u * T:(u + 1) * T], bank[:, 0:T], ACT.Copy, after=[m]))
                banks.done(at, t_z[-1])
            give_unit()
        for j in range(24):
            if j % 2 == 0:
                w = three(take_unit()[:, :], KT)
            at, bank, read = banks.next()
            for k in range(KT):
                m = PE.mm(bank[:, 0:T], half(w, j % 2)[:, k, :], hT[:, k, 0:T], start=k == 0, stop=k == KT - 1, mark=k == KT - 1, after=[read])
                if k % 4 == 3:
                    yield
            t_gates.append(A(act, gates[:, j, :], bank[:, 0:T], ACT.Copy, after=[m]))
            banks.done(at, t_gates[-1])
            if j % 2:
                give_unit()

    def scan():
        for g in range(2):
            for st in range(2):
                m = PE.mm(ps[g][:, st * T:(st + 1) * T], bT[:, g, st * P:(st + 1) * P], cT[:, g, :], mark=True)
            for d in range(2):
                V(tt, cbm[:, d, g, :], ps[g][:, :], const("fwd" if d == 0 else "bwd"), ALU.mult, after=[m])
        for d in range(2):
            for ti in range(2):
                V(tt, three(xdt[:, d, ti, :], 16), three(xs[:, ti, :], 16), dt[:, ti, d * 16:(d + 1) * 16].unsqueeze(2).to_broadcast([P, 16, HD]), ALU.mult)
        for ti in range(2):
            V(tt, three(y[:, ti, :], 16), three(xs[:, ti, :], 16), col2("d_skip").unsqueeze(2).to_broadcast([P, 16, HD]), ALU.mult)
        yield
        banks = Banks(ps[2:4])
        for d in range(2):
            for g in range(2):
                for ti in range(2):
                    at, bank, read = banks.next()
                    yield
                    m = PE.mm(bank[:, :], cT[:, g, ti * P:(ti + 1) * P], h0[:, d, g * 512:(g + 1) * 512], mark=True, after=[read])
                    t = V(tt, three(off[:, :], 8), three(bank[:, :], 8),
                          eac[:, ti, d * 16 + g * 8:d * 16 + (g + 1) * 8].unsqueeze(2).to_broadcast([P, 8, HD]), ALU.mult, after=[m])
                    banks.done(at, t)
                    V(tt, y[:, ti, g * 512:(g + 1) * 512], y[:, ti, g * 512:(g + 1) * 512], off[:, :], ALU.add)
        for d in range(2):
            for st in range(2):
                m = PE.mm(ps[5][0:32, d * T:(d + 1) * T], da[:, st, :], order[d][:, st, :], start=st == 0, stop=st == 1, mark=True)
        t_row = V(nc.vector.tensor_copy, arow2[:, :, :], three(ps[5][0:32, :], 2), after=[m])
        banks = Banks(ps[5:7])
        lm_read = [None] * 2
        acc = [ps[0], ps[1], ps[2], ps[3]]
        PE.wait(V.last)
        for b in range(4):
            PE.mm(acc[b][:, :], zeros[:, 0:P], zeros[:, :], start=True, stop=False, group=True)

        def diag(hd):
            d, h_i = divmod(hd, 16)
            b = hd % 2
            at, bank, read = banks.next()
            m = PE.mm(bank[:, 0:T], ident[0:32, hd:hd + 1].to_broadcast([32, P]), arow2[:, d, :], mark=True, after=[read, t_row])
            for st in range(2):
                t = V(ts, lm[:, b, st, :], bank[:, 0:T], acs[:, st, hd:hd + 1], 0.0, ALU.subtract, ALU.min, after=[m, lm_read[b]])
            banks.done(at, t)
            t = A(act, lm[:, b, :, :], lm[:, b, :, :], ACT.Exp, after=[t])
            return V(tt, lm[:, b, :, :], lm[:, b, :, :], three(cbm[:, d, h_i // 8, :], 2), ALU.mult, after=[t])

        def diag_sum(hd, t):
            d, h_i = divmod(hd, 16)
            b = hd % 2
            for ti in range(2):
                tiles = [0] if (d, ti) == (0, 0) else [1] if (d, ti) == (1, 1) else [0, 1]
                for st in tiles:
                    m = PE.mm(acc[2 * ti + h_i // 8][:, (h_i % 8) * HD:(h_i % 8 + 1) * HD], lm[:, b, st, ti * P:(ti + 1) * P],
                              xdt[:, d, st, h_i * HD:(h_i + 1) * HD], start=False, stop=hd == 31, group=True,
                              mark=ti == 1 and st == tiles[-1], after=[t])
            lm_read[b] = m

        before = None
        for hd in range(32):
            t = diag(hd)
            yield
            if before:
                diag_sum(*before)
                yield
            before = (hd, t)
        diag_sum(*before)
        t = A(act, zs[:, :, :], zs[:, :, :], ACT.Silu, after=t_z)
        for ti in range(2):
            for g in range(2):
                V(tt, y[:, ti, g * 512:(g + 1) * 512], acc[2 * ti + g][:, :], y[:, ti, g * 512:(g + 1) * 512], ALU.add, after=[lm_read[1]])
        yield
        V(tt, y[:, :, :], y[:, :, :], zs[:, :, :], ALU.mult, after=[t])
        yield
        for ti in range(2):
            A(act, zs[:, ti, :], y[:, ti, :], ACT.Square, accum_out=st4[:, ti:ti + 1], after=[V.last])
        t = A(act, st4[:, 2:4], st4[:, 0:2], ACT.Sqrt, bias=EPS6, scale=1.0 / DM)
        V(nc.vector.reciprocal, st4[:, 2:4], st4[:, 2:4], after=[t])
        for ti in range(2):
            t = V(ts, y[:, ti, :], y[:, ti, :], st4[:, 2 + ti:3 + ti], None, ALU.mult)
        banks = Banks(ps[0:4])
        for j in range(KT):
            yield
            at, bank, read = banks.next()
            for ti in range(2):
                m = PE.flip(bank[:, ti * P:(ti + 1) * P], y[:, ti, j * P:(j + 1) * P], ident, mark=ti == 1, after=[read, t])
            banks.done(at, V(ts, ysT[:, j, :], bank[:, 0:T], col2("ssm_norm")[:, j:j + 1], None, ALU.mult, after=[m]))

    interleave((scan(), 1), (gate_projections(), 0.85))
    for b in range(3):
        t_sig = A(act, gates[:, b * KT:(b + 1) * KT, :], gates[:, b * KT:(b + 1) * KT, :], ACT.Sigmoid, after=t_gates)
    phase()
    s3_.close()

    mg = ExitStack()
    mT = sb("mT", [P, KT, T], scope=mg)
    prod = sb("prod", [P, 2, T], scope=mg)
    banks = Banks(ps[2:8])
    for hf in range(2):
        w_a, w_c = three(take_unit()[:, :], 4), three(take_unit()[:, :], 4)
        w_b = [three(take_unit()[:, :], KT) for _ in range(2)]
        for mi in range(4):
            m_i = 4 * hf + mi
            o = slice(mi * P, (mi + 1) * P)
            parts = [(w_a[:, :, o], yaT, 4), (w_b[mi // 2][:, :, (mi % 2) * P:(mi % 2 + 1) * P], ysT, KT), (w_c[:, :, o], ygT, 4)]
            for b, (wv, src, nk) in enumerate(parts):
                at, bank, read = banks.next()
                for k in range(nk):
                    m = PE.mm(bank[:, 0:T], wv[:, k, :], src[:, k, :], start=k == 0, stop=k == nk - 1, mark=k == nk - 1, after=[read])
                dst = mT[:, m_i, :] if b == 0 else prod[:, b - 1, :]
                banks.done(at, V(tt, dst, gates[:, b * KT + m_i, :], bank[:, 0:T], ALU.mult, after=[m, A.last]))
                if b:
                    t = V(tt, mT[:, m_i, :], mT[:, m_i, :], dst, ALU.add)
        PE.pending += 4
        PE.flush()
    banks = Banks(ps[0:4])
    PE.wait(A.last)
    for m_i in range(KT):
        if m_i % 2 == 0:
            w = three(take_unit()[:, :], KT)
        at, bank, read = banks.next()
        for k in range(KT):
            m = PE.mm(bank[:, 0:T], w[:, k, (m_i % 2) * P:(m_i % 2 + 1) * P], mT[:, k, :], start=k == 0, stop=k == KT - 1, mark=k == KT - 1,
                      after=[read, t])
        if m_i % 2:
            give_unit()
        banks.done(at, V(stt, xT[:, m_i, :], bank[:, 0:T], gate1[:, m_i:m_i + 1], xT[:, m_i, :], ALU.mult, ALU.add, after=[m]))
    phase()
    mg.close()
    ssd.close()
    branches.close()

    sq9 = sb("sq9", [P, KT, T])
    pad = sb("pad", [P, 2, T + 2])
    csum = sb("csum", [P, 2, T])
    V(nc.vector.memset, pad[:, :, :], 0.0)
    residual = V.last
    A.wait(residual)
    done, ffn_scope = ffn('ffn3', lambda **kw: rms(xT[:, :, :], hT[:, :, 0:T], scale_2, sq9[:, :, :], shift=shift2, after=[residual], **kw), conv={"pad": pad, "sum": csum, "w": col2("fconv_w"), "b": col2("fconv_b")})
    for m_i in range(KT):
        V(stt, xT[:, m_i, :], ps[2 + m_i // 2][:, (m_i % 2) * T:(m_i % 2 + 1) * T], gate2[:, m_i:m_i + 1], xT[:, m_i, :],
          ALU.mult, ALU.add, after=[done])
    t = rms(xT[:, :, :], hT[:, :, 0:T], col2("final"), sq9[:, :, :], after=[V.last])
    A.wait(t)
    nc.scalar.dma_start(out, hT[:, :, 0:T]).then_inc(s_out, 16)
    nc.scalar.wait_ge(s_out, 16)
    nc.all_engine_barrier()
    ffn_scope.close()
    ctx.close()


def _cols(v, n=None):
    v = np.asarray(v)
    return np.moveaxis(v.reshape(*v.shape[:-1], -1, P), -1, -2)


def _in_units(w, cols):
    k = w.shape[0] // P
    return w.reshape(k, P, -1, cols).transpose(2, 1, 0, 3).reshape(-1, P, k * cols)


def _ffn_units(g, u, d):
    gu = [_in_units(w, 2 * P) for w in (g, u)]
    dn = d.reshape(FT // 2, 2, P, DM).transpose(0, 2, 1, 3).reshape(FT // 2, P, UNIT)
    return np.stack([*gu, dn], axis=1).reshape(-1, P, UNIT)


def kernel(**inputs):
    import concourse.bacc as _bacc
    from concourse.bass_utils import run_bass_kernel_spmd as _run

    a = {k: np.asarray(v) for k, v in inputs.items()}
    f = np.float32
    w_layers, p_layers = [], []
    for l in range(DEPTH):
        w_in = np.concatenate([a["w_in"][l], np.zeros((DM, P), f)], axis=1)
        w_layers.append(np.concatenate([
            _ffn_units(a["ffn1_w_gate"][l], a["ffn1_w_up"][l], a["ffn1_w_down"][l]),
            _in_units(w_in, 2 * P), _in_units(a["w_out"][l], 2 * P),
            _ffn_units(a["ffn2_w_gate"][l], a["ffn2_w_up"][l], a["ffn2_w_down"][l])]))
        p = np.zeros((P, LP_N), f)

        def put(name, v):
            p[:v.shape[0], slice(*LP[name])] = v

        for n in ("norm_ffn1", "norm_mix", "norm_ffn2"):
            put(n, _cols(a[n][l]))
        put("mu", _cols(a["shift_mu"][l]))
        put("a0", _cols(a["rwkv_a0"][l]))
        put("k_k", _cols(a["rwkv_k_k"][l]))
        put("k_a", _cols(a["rwkv_k_a"][l]))
        put("r_k", _cols(a["rwkv_r_k"][l].reshape(-1)))
        put("ln_w", a["rwkv_ln_w"][l].reshape(NH, HD).T)
        put("ln_b", a["rwkv_ln_b"][l].reshape(NH, HD).T)
        put("qn", np.tile(a["attn_q_norm"][l], 2)[:, None])
        put("kn", np.tile(a["attn_k_norm"][l], 2)[:, None])
        put("conv_w", a["conv_dw_w"][l].reshape(TAPS, 2, P).transpose(2, 1, 0).reshape(P, 2 * TAPS))
        put("conv_b", _cols(a["conv_dw_b"][l]))
        put("cln_w", _cols(a["conv_ln_w"][l]))
        put("cln_b", _cols(a["conv_ln_b"][l]))
        put("lora", np.concatenate([a["rwkv_w2"][l], a["rwkv_a2"][l], a["rwkv_g2"][l]], axis=0))
        put("w0", np.broadcast_to(a["rwkv_w0"][l], (P, NH * HD)))
        p_layers.append(p)
    w_layers, p_layers = np.stack(w_layers), np.stack(p_layers)

    b = {k[:-2]: (v[0] if v.ndim > 1 and k not in ("c_2", "ctx_2") else v) for k, v in a.items() if k.endswith("_2")}
    w2 = b["w_in"]
    at, span = 0, {}
    for n, width in (("a_q", 512), ("a_k", 128), ("a_v", 128), ("z", 1024), ("xbc", 1536), ("dt", 32), ("c_q", 512),
                     ("c_k", 128), ("c_v", 128), ("gates", 3072)):
        span[n] = w2[:, at:at + width]
        at += width
    pair = lambda x, y: _in_units(np.concatenate([span[x], span[y]], axis=1), 2 * P)
    oa, oc, ob = _in_units(b["w_oa"], 512), _in_units(b["w_oc"], 512), _in_units(b["w_ob"], 2 * P)
    w_last = np.concatenate([
        _in_units(b["w_mod"], 2 * P), pair("a_k", "c_k"), pair("a_v", "c_v"), _in_units(span["a_q"], 2 * P),
        _in_units(span["c_q"], 2 * P), _in_units(span["xbc"], 2 * P), _in_units(span["z"], 2 * P),
        _in_units(span["gates"], 2 * P), oa[0:1], oc[0:1], ob[0:2], oa[1:2], oc[1:2], ob[2:4],
        _in_units(b["w_out"], 2 * P), _ffn_units(b["ffn_w_gate"], b["ffn_w_up"], b["ffn_w_down"])])
    p = np.zeros((P, SP2_N), f)

    def put2(name, v):
        p[:, slice(*SP2[name])] = v

    put2("c", np.stack([_cols(b["c"].reshape(-1)), _cols(b["c_ctx"])], axis=2).reshape(P, 16))
    put2("b_mod", _cols(b["b_mod"]))
    put2("norm1", _cols(b["norm1"]))
    put2("norm2", _cols(b["norm2"]))
    put2("final", _cols(b["final_norm"]))
    put2("conv_w", b["ssm_conv_w"].reshape(3, 12, P).transpose(2, 1, 0).reshape(P, 36))
    put2("conv_b", _cols(b["ssm_conv_b"]))
    put2("a_log", np.broadcast_to(b["ssm_A_log"].reshape(1, 32), (P, 32)))
    put2("dt_bias", np.broadcast_to(b["ssm_dt_bias"].reshape(1, 32), (P, 32)))
    put2("d_skip", np.broadcast_to(b["ssm_D"].reshape(1, 16), (P, 16)))
    put2("ssm_norm", _cols(b["ssm_norm"]))
    put2("qn", np.tile(b["c_q_norm"], 2)[:, None])
    put2("kn", np.tile(b["c_k_norm"], 2)[:, None])
    put2("sink", np.broadcast_to(b["a_sink"].reshape(1, 8), (P, 8)))
    put2("fconv_w", b["ffn_conv_w"].reshape(3, FT, P).transpose(2, 1, 0).reshape(P, 3 * FT))
    put2("fconv_b", _cols(b["ffn_conv_b"]))
    put2("w_dt", span["dt"].reshape(KT, P, 32).transpose(1, 0, 2).reshape(P, KT * 32))
    c0, cl, cs = constants()

    def chan(x):
        return x.reshape(T, KT, P).transpose(2, 1, 0)

    arrays = {"xT": chan(a["x"]), "ctxT": chan(b["ctx"]), "w_layers": w_layers, "w_last": w_last, "p_layers": p_layers,
              "p_last": p, "c0": c0, "cl": cl, "cs": cs}
    arrays = {k: np.ascontiguousarray(v) for k, v in arrays.items()}
    nc = _bacc.Bacc("TRN2", target_bir_lowering=False, num_devices=1)
    args = [nc.dram_tensor("in_" + k, v.shape, F32, kind="ExternalInput").ap() for k, v in arrays.items()]
    out = nc.dram_tensor("out_x", (P, KT, T), F32, kind="ExternalOutput").ap()
    build(nc, *args, out)
    r = _run(nc, [{"in_" + k: v for k, v in arrays.items()}], core_ids=[0])
    return np.ascontiguousarray(r.results[0]["out_x"].transpose(2, 1, 0)).reshape(1, T, DM)
```
